# Optimizing a Trainium2 kernel written in Bass

```python
import math
import jax, jax.numpy as jnp
from jax import lax
import numpy as np

D_MODEL = 1024
BATCH = 1
SEQ = 512
DEPTH = 1

CHUNK = 64
N_MEM = 256
N_MIXERS = 3
MIXER_W = D_MODEL
GDN_DK = 128
GDN_DV = 128
GDN_HEADS = MIXER_W // GDN_DV
GDN_KW = GDN_HEADS * GDN_DK
GDN_VW = GDN_HEADS * GDN_DV
GDN_QKV = 2 * GDN_KW + GDN_VW
CONV_K = 4
ML_DQK = 64
ML_DV = 128
ML_HEADS = MIXER_W // ML_DV
ML_KW = ML_HEADS * ML_DQK
ML_VW = ML_HEADS * ML_DV
SB_DH = 64
SB_HEADS = MIXER_W // SB_DH
SB_W = SB_HEADS * SB_DH
SB_BLOCK = 128
MEM_HEADS = 4
MEM_DH = 128
MEM_W = MEM_HEADS * MEM_DH
MIX_W = MIXER_W + MEM_W
GDN_IN = GDN_QKV + GDN_VW + 2 * GDN_HEADS + MEM_W
ML_IN = 2 * ML_KW + 2 * ML_VW + 2 * ML_HEADS + MEM_W
SB_IN = 3 * SB_W + MEM_W
D_FF = -(-8 * D_MODEL // (3 * 256)) * 256
N_GDN = (DEPTH + 2) // N_MIXERS
N_ML = (DEPTH + 1) // N_MIXERS
N_SB = DEPTH // N_MIXERS
EPS = 1e-6


def rms_norm(x, g):
    xf = x.astype(jnp.float32)
    y = xf * lax.rsqrt(jnp.mean(xf * xf, axis=-1, keepdims=True) + EPS)
    return (y * g.astype(jnp.float32)).astype(x.dtype)

def l2norm(x):
    return x * lax.rsqrt(jnp.sum(x * x, axis=-1, keepdims=True) + EPS)

def split_heads(t, n):
    b, s, _ = t.shape
    return t.reshape(b, s, n, -1).transpose(0, 2, 1, 3)

def merge_heads(t):
    b, h, s, d = t.shape
    return t.transpose(0, 2, 1, 3).reshape(b, s, h * d)

def to_chunks(t):
    b, h, s = t.shape[:3]
    return t.reshape(b, h, s // CHUNK, CHUNK, *t.shape[3:])

def causal_dwconv(x, w):
    k, c = w.shape
    return lax.conv_general_dilated(x, w[:, None, :].astype(x.dtype), window_strides=(1,),
                                    padding=[(k - 1, 0)], dimension_numbers=("NWC", "WIO", "NWC"),
                                    feature_group_count=c)

def gated_delta_rule(q, k, v, a, b, a_log, dt_bias):
    f32 = jnp.float32
    q, k, v, a, b = (t.astype(f32) for t in (q, k, v, a, b))
    q = l2norm(q) * GDN_DK ** -0.5
    k = l2norm(k)
    beta = jax.nn.sigmoid(b)
    g = -jnp.exp(a_log.astype(f32))[None, :, None] * jax.nn.softplus(a + dt_bias.astype(f32)[None, :, None])
    qc, kc, vc, bc, gc = (to_chunks(t) for t in (q, k, v, beta, g))
    G = jnp.cumsum(gc, axis=-1)
    incl = jnp.tril(jnp.ones((CHUNK, CHUNK), dtype=bool))
    strict = jnp.tril(jnp.ones((CHUNK, CHUNK), dtype=bool), -1)
    diff = G[..., :, None] - G[..., None, :]
    decay = jnp.where(incl, jnp.exp(jnp.where(incl, diff, 0.0)), 0.0)
    kk = jnp.einsum("bhnid,bhnjd->bhnij", kc, kc)
    lower = jnp.where(strict, bc[..., :, None] * kk * decay, 0.0)
    rhs = jnp.concatenate([vc * bc[..., None], kc * (bc * jnp.exp(G))[..., None]], axis=-1)
    sol = lax.linalg.triangular_solve(lower + jnp.eye(CHUNK, dtype=f32), rhs, left_side=True,
                                      lower=True, unit_diagonal=True)
    u, w = sol[..., :GDN_DV], sol[..., GDN_DV:]
    p = jnp.einsum("bhnid,bhnjd->bhnij", qc, kc) * decay
    qg = qc * jnp.exp(G)[..., None]
    kg = kc * jnp.exp(G[..., -1:] - G)[..., None]
    gl = jnp.exp(G[..., -1])

    def step(state, xs):
        u_n, w_n, qg_n, kg_n, p_n, gl_n = xs
        v_new = u_n - jnp.einsum("bhcd,bhde->bhce", w_n, state)
        o_n = jnp.einsum("bhcd,bhde->bhce", qg_n, state) + jnp.einsum("bhij,bhje->bhie", p_n, v_new)
        state = state * gl_n[..., None, None] + jnp.einsum("bhcd,bhce->bhde", kg_n, v_new)
        return state, o_n

    bn, hn = q.shape[:2]
    s0 = jnp.zeros((bn, hn, GDN_DK, GDN_DV), f32)
    xs = tuple(jnp.moveaxis(t, 2, 0) for t in (u, w, qg, kg, p, gl))
    _, o = lax.scan(step, s0, xs)
    return jnp.moveaxis(o, 0, 2).reshape(bn, hn, -1, GDN_DV)

def mlstm_cell(q, k, v, i_pre, f_pre):
    f32 = jnp.float32
    q, k, v, i_pre, f_pre = (t.astype(f32) for t in (q, k, v, i_pre, f_pre))
    k = k * ML_DQK ** -0.5
    lf = jax.nn.log_sigmoid(f_pre)
    qc, kc, vc, lic, lfc = (to_chunks(t) for t in (q, k, v, i_pre, lf))
    bcum = jnp.cumsum(lfc, axis=-1)
    incl = jnp.tril(jnp.ones((CHUNK, CHUNK), dtype=bool))
    dmat = jnp.where(incl, bcum[..., :, None] - bcum[..., None, :] + lic[..., None, :], -jnp.inf)
    m_intra = jnp.max(dmat, axis=-1)
    sqk = jnp.einsum("bhnid,bhnjd->bhnij", qc, kc) * jnp.exp(dmat - m_intra[..., None])
    num_intra = jnp.einsum("bhnij,bhnje->bhnie", sqk, vc)
    den_intra = jnp.sum(sqk, axis=-1)
    bl = bcum[..., -1]
    wk = bl[..., None] - bcum + lic
    m_chunk = jnp.max(wk, axis=-1)
    e = jnp.exp(wk - m_chunk[..., None])
    kv_c = jnp.einsum("bhnc,bhncd,bhnce->bhnde", e, kc, vc)
    ks_c = jnp.einsum("bhnc,bhncd->bhnd", e, kc)

    def step(carry, xs):
        c_s, n_s, m_s = carry
        kv_n, ks_n, bl_n, mc_n = xs
        m_new = jnp.maximum(bl_n + m_s, mc_n)
        a = jnp.exp(bl_n + m_s - m_new)
        c = jnp.exp(mc_n - m_new)
        c_new = a[..., None, None] * c_s + c[..., None, None] * kv_n
        n_new = a[..., None] * n_s + c[..., None] * ks_n
        return (c_new, n_new, m_new), (c_s, n_s, m_s)

    bn, hn = q.shape[:2]
    init = (jnp.zeros((bn, hn, ML_DQK, ML_DV), f32), jnp.zeros((bn, hn, ML_DQK), f32),
            jnp.zeros((bn, hn), f32))
    xs = tuple(jnp.moveaxis(t, 2, 0) for t in (kv_c, ks_c, bl, m_chunk))
    _, (c_prev, n_prev, m_prev) = lax.scan(step, init, xs)
    c_prev = jnp.moveaxis(c_prev, 0, 2)
    n_prev = jnp.moveaxis(n_prev, 0, 2)
    m_prev = jnp.moveaxis(m_prev, 0, 2)
    a_inter = bcum + m_prev[..., None]
    m_t = jnp.maximum(a_inter, m_intra)
    s_inter = jnp.exp(a_inter - m_t)
    s_intra = jnp.exp(m_intra - m_t)
    num = s_inter[..., None] * jnp.einsum("bhncd,bhnde->bhnce", qc, c_prev) + s_intra[..., None] * num_intra
    den = s_inter * jnp.einsum("bhncd,bhnd->bhnc", qc, n_prev) + s_intra * den_intra
    h = num / jnp.maximum(jnp.abs(den), jnp.exp(-m_t))[..., None]
    return h.reshape(bn, hn, -1, ML_DV)

def stick_breaking(q, k, v):
    seq = q.shape[2]
    scale = SB_DH ** -0.5
    outs = []
    for blk in range(seq // SB_BLOCK):
        q0 = blk * SB_BLOCK
        kend = q0 + SB_BLOCK
        z = jnp.einsum("bhtd,bhsd->bhts", q[:, :, q0:kend], k[:, :, :kend]).astype(jnp.float32) * scale
        t_idx = q0 + jnp.arange(SB_BLOCK)[:, None]
        s_idx = jnp.arange(kend)[None, :]
        causal = s_idx < t_idx
        log_1mb = jnp.where(causal, jax.nn.log_sigmoid(-z), 0.0)
        tail = lax.cumsum(log_1mb, axis=3, reverse=True) - log_1mb
        att = jnp.where(causal, jnp.exp(jax.nn.log_sigmoid(z) + tail), 0.0)
        outs.append(jnp.einsum("bhts,bhsd->bhtd", att.astype(v.dtype), v[:, :, :kend]))
    return jnp.concatenate(outs, axis=2)

def memory_attention(q_mem, mem_k, mem_v):
    q = split_heads(q_mem, MEM_HEADS)
    k = split_heads(mem_k, MEM_HEADS)
    v = split_heads(mem_v, MEM_HEADS)
    s = jnp.einsum("bhtd,bhmd->bhtm", q, k).astype(jnp.float32) * MEM_DH ** -0.5
    p = jax.nn.softmax(s, axis=-1).astype(v.dtype)
    return merge_heads(jnp.einsum("bhtm,bhmd->bhtd", p, v))

def gdn_branch(proj, conv_w, a_log, dt_bias, out_norm):
    qkv, z, a, b, q_mem = jnp.split(proj, [GDN_QKV, GDN_QKV + GDN_VW, GDN_QKV + GDN_VW + GDN_HEADS,
                                           GDN_QKV + GDN_VW + 2 * GDN_HEADS], axis=-1)
    qkv = jax.nn.silu(causal_dwconv(qkv, conv_w))
    q, k, v = jnp.split(qkv, [GDN_KW, 2 * GDN_KW], axis=-1)
    o = gated_delta_rule(split_heads(q, GDN_HEADS), split_heads(k, GDN_HEADS), split_heads(v, GDN_HEADS),
                         a.transpose(0, 2, 1), b.transpose(0, 2, 1), a_log, dt_bias)
    o = rms_norm(o, out_norm) * jax.nn.silu(split_heads(z, GDN_HEADS).astype(jnp.float32))
    return merge_heads(o).astype(proj.dtype), q_mem

def mlstm_branch(proj, i_bias, f_bias, out_norm):
    q, k, v, o, i_pre, f_pre, q_mem = jnp.split(
        proj, [ML_KW, 2 * ML_KW, 2 * ML_KW + ML_VW, 2 * ML_KW + 2 * ML_VW,
               2 * ML_KW + 2 * ML_VW + ML_HEADS, 2 * ML_KW + 2 * ML_VW + 2 * ML_HEADS], axis=-1)
    i_pre = (i_pre + i_bias).transpose(0, 2, 1)
    f_pre = (f_pre + f_bias).transpose(0, 2, 1)
    h = mlstm_cell(split_heads(q, ML_HEADS), split_heads(k, ML_HEADS), split_heads(v, ML_HEADS), i_pre, f_pre)
    h = rms_norm(h, out_norm) * jax.nn.sigmoid(split_heads(o, ML_HEADS).astype(jnp.float32))
    return merge_heads(h).astype(proj.dtype), q_mem

def sb_branch(proj):
    q, k, v, q_mem = jnp.split(proj, [SB_W, 2 * SB_W, 3 * SB_W], axis=-1)
    o = stick_breaking(split_heads(q, SB_HEADS), split_heads(k, SB_HEADS), split_heads(v, SB_HEADS))
    return merge_heads(o), q_mem

def swiglu(x, w_in, w_out):
    g, u = jnp.split(x @ w_in, 2, axis=-1)
    return (jax.nn.silu(g) * u) @ w_out

def _w(key, shape, fan_in):
    return jax.random.normal(key, shape, jnp.float32) * fan_in ** -0.5

def _gain(key, shape):
    return 1.0 + 0.02 * jax.random.normal(key, shape, jnp.float32)

def first_inputs(seed: int = 0) -> dict:
    key = jax.random.key(seed)
    ks = jax.random.split(key, 24)
    dt = jnp.exp(jax.random.uniform(ks[14], (N_GDN, GDN_HEADS), jnp.float32,
                                    minval=math.log(1e-3), maxval=math.log(1e-1)))
    return {
        "x": jax.random.normal(ks[0], (BATCH, SEQ, D_MODEL), jnp.float32),
        "mem": jax.random.normal(ks[1], (BATCH, N_MEM, D_MODEL), jnp.float32),
        "mem_norm": _gain(ks[2], (D_MODEL,)),
        "norm_pre_mix": _gain(ks[3], (DEPTH, D_MODEL)),
        "norm_post_mix": _gain(ks[4], (DEPTH, D_MODEL)),
        "norm_pre_ffn": _gain(ks[5], (DEPTH, D_MODEL)),
        "norm_post_ffn": _gain(ks[6], (DEPTH, D_MODEL)),
        "w_mem_kv": _w(ks[7], (DEPTH, D_MODEL, 2 * MEM_W), D_MODEL),
        "w_out": _w(ks[8], (DEPTH, MIX_W, D_MODEL), MIX_W),
        "w_ffn_in": _w(ks[9], (DEPTH, D_MODEL, 2 * D_FF), D_MODEL),
        "w_ffn_out": _w(ks[10], (DEPTH, D_FF, D_MODEL), D_FF),
        "gdn_w_in": _w(ks[11], (N_GDN, D_MODEL, GDN_IN), D_MODEL),
        "gdn_conv": _w(ks[12], (N_GDN, CONV_K, GDN_QKV), CONV_K),
        "gdn_a_log": jnp.log(jax.random.uniform(ks[13], (N_GDN, GDN_HEADS), jnp.float32, minval=1.0, maxval=16.0)),
        "gdn_dt_bias": dt + jnp.log(-jnp.expm1(-dt)),
        "gdn_out_norm": _gain(ks[15], (N_GDN, GDN_DV)),
        "ml_w_in": _w(ks[16], (N_ML, D_MODEL, ML_IN), D_MODEL),
        "ml_i_bias": 0.1 * jax.random.normal(ks[17], (N_ML, ML_HEADS), jnp.float32),
        "ml_f_bias": jax.random.uniform(ks[18], (N_ML, ML_HEADS), jnp.float32, minval=3.0, maxval=6.0),
        "ml_out_norm": _gain(ks[19], (N_ML, ML_DV)),
        "sb_w_in": _w(ks[20], (N_SB, D_MODEL, SB_IN), D_MODEL),
    }

def first_block(x, mem, mem_norm, norm_pre_mix, norm_post_mix, norm_pre_ffn, norm_post_ffn, w_mem_kv,
              w_out, w_ffn_in, w_ffn_out, gdn_w_in, gdn_conv, gdn_a_log, gdn_dt_bias, gdn_out_norm,
              ml_w_in, ml_i_bias, ml_f_bias, ml_out_norm, sb_w_in):
    h = x
    mem_n = rms_norm(mem, mem_norm)
    for layer in range(DEPTH):
        kind = layer % N_MIXERS
        j = layer // N_MIXERS
        u = rms_norm(h, norm_pre_mix[layer])
        if kind == 0:
            y_mix, q_mem = gdn_branch(u @ gdn_w_in[j], gdn_conv[j], gdn_a_log[j], gdn_dt_bias[j], gdn_out_norm[j])
        elif kind == 1:
            y_mix, q_mem = mlstm_branch(u @ ml_w_in[j], ml_i_bias[j], ml_f_bias[j], ml_out_norm[j])
        else:
            y_mix, q_mem = sb_branch(u @ sb_w_in[j])
        mem_k, mem_v = jnp.split(mem_n @ w_mem_kv[layer], 2, axis=-1)
        y_mem = memory_attention(q_mem, mem_k, mem_v)
        y = jnp.concatenate([y_mix, y_mem], axis=-1) @ w_out[layer]
        h = h + rms_norm(y, norm_post_mix[layer])
        f = swiglu(rms_norm(h, norm_pre_ffn[layer]), w_ffn_in[layer], w_ffn_out[layer])
        h = h + rms_norm(f, norm_post_ffn[layer])
    return h


DEPTH_2 = 2

N_HEADS = 16
N_KV_GROUPS = 2
HEADS_PER_GROUP = N_HEADS // N_KV_GROUPS
HEAD_DIM = 64
N_KV_PARTS = 6
N_BRANCH = 3
L_CMP = 32
STRIDE_CMP = 16
L_SLC = 64
N_SEL = 16
WINDOW = 512
Q_CHUNK = 64
CONV_WIDTH = 31
FFN_HIDDEN = -(-(8 * D_MODEL) // (3 * 256)) * 256
NEG = -1e30
FORCE = 1e9


def rmsnorm(x, g):
    xf = x.astype(jnp.float32)
    y = xf * lax.rsqrt(jnp.mean(xf * xf, axis=-1, keepdims=True) + EPS)
    return (y * g.astype(jnp.float32)).astype(x.dtype)

def layernorm(x, g, b):
    xf = x.astype(jnp.float32)
    mu = jnp.mean(xf, axis=-1, keepdims=True)
    var = jnp.mean(jnp.square(xf - mu), axis=-1, keepdims=True)
    y = (xf - mu) * lax.rsqrt(var + EPS)
    return (y * g.astype(jnp.float32) + b.astype(jnp.float32)).astype(x.dtype)

def swiglu_ffn(x, norm_g, w_in, w_out):
    gate, up = jnp.split(rmsnorm(x, norm_g) @ w_in, 2, axis=-1)
    return (jax.nn.silu(gate) * up) @ w_out

def conformer_conv(x, norm_g, pw1_w, pw1_b, dw_w, dw_b, ln_g, ln_b, pw2_w, pw2_b):
    a, b = jnp.split(rmsnorm(x, norm_g) @ pw1_w + pw1_b, 2, axis=-1)
    h = a * jax.nn.sigmoid(b)
    h = lax.conv_general_dilated(
        h, dw_w[:, None, :], window_strides=(1,),
        padding=[(CONV_WIDTH - 1, 0)],
        dimension_numbers=('NWC', 'WIO', 'NWC'),
        feature_group_count=h.shape[-1]) + dw_b
    h = jax.nn.silu(layernorm(h, ln_g, ln_b))
    return h @ pw2_w + pw2_b

def shared_kv(h, kv_norm, w_kv, cmp_pos_k, cmp_pos_v, phi_k_w1, phi_k_w2, phi_v_w1, phi_v_w2):
    B, S, _ = h.shape
    kv = (rmsnorm(h, kv_norm) @ w_kv).reshape(B, S, N_KV_PARTS, N_KV_GROUPS, HEAD_DIM)
    kv = kv.transpose(2, 0, 3, 1, 4)
    k_cmp_raw, v_cmp_raw, k_slc, v_slc, k_win, v_win = kv
    n_cmp = (S - L_CMP) // STRIDE_CMP + 1
    idx = np.arange(n_cmp)[:, None] * STRIDE_CMP + np.arange(L_CMP)[None, :]

    def compress(raw, pos, w1, w2):
        blk = raw[:, :, idx] + pos
        blk = blk.reshape(B, N_KV_GROUPS, n_cmp, L_CMP * HEAD_DIM)
        return jax.nn.silu(blk @ w1) @ w2

    k_cmp = compress(k_cmp_raw, cmp_pos_k, phi_k_w1, phi_k_w2)
    v_cmp = compress(v_cmp_raw, cmp_pos_v, phi_v_w1, phi_v_w2)
    n_slc = S // L_SLC
    k_slc_blk = k_slc.reshape(B, N_KV_GROUPS, n_slc, L_SLC, HEAD_DIM)
    v_slc_blk = v_slc.reshape(B, N_KV_GROUPS, n_slc, L_SLC, HEAD_DIM)
    pad = ((0, 0), (0, 0), (WINDOW, 0), (0, 0))
    k_win_pad = jnp.pad(k_win, pad)
    v_win_pad = jnp.pad(v_win, pad)
    return (k_cmp, v_cmp, k_slc_blk, v_slc_blk, k_win_pad, v_win_pad)

def nsa_attention(x, norm_g, w_in, w_out, kv):
    k_cmp, v_cmp, k_slc_blk, v_slc_blk, k_win_pad, v_win_pad = kv
    B, S, _ = x.shape
    G, Hg, dh = N_KV_GROUPS, HEADS_PER_GROUP, HEAD_DIM
    n_chunk = S // Q_CHUNK
    n_cmp = k_cmp.shape[2]
    n_slc = k_slc_blk.shape[2]
    k_sel = min(N_SEL, n_slc)
    scale = HEAD_DIM ** -0.5

    proj = rmsnorm(x, norm_g) @ w_in
    q = proj[..., :N_HEADS * dh]
    gates = jax.nn.sigmoid(proj[..., N_HEADS * dh:])
    q = q.reshape(B, n_chunk, Q_CHUNK, G, Hg, dh).transpose(1, 0, 3, 4, 2, 5)
    gates = gates.reshape(B, n_chunk, Q_CHUNK, N_BRANCH, G, Hg).transpose(1, 3, 0, 4, 5, 2)
    starts = jnp.arange(n_chunk, dtype=jnp.int32) * Q_CHUNK

    slopes = jnp.asarray(2.0 ** (-8.0 * (np.arange(N_HEADS) + 1) / N_HEADS), jnp.float32)
    slopes = slopes.reshape(G, Hg)[:, :, None, None]
    cmp_end = jnp.arange(n_cmp, dtype=jnp.int32) * STRIDE_CMP + (L_CMP - 1)
    cs = np.arange(n_cmp)[:, None] * STRIDE_CMP
    ss = np.arange(n_slc)[None, :] * L_SLC
    overlap = jnp.asarray((cs <= ss + L_SLC - 1) & (cs + L_CMP - 1 >= ss), jnp.float32)
    blk = jnp.arange(n_slc, dtype=jnp.int32)
    bidx = jnp.arange(B)[:, None, None, None]
    gidx = jnp.arange(G)[None, :, None, None]

    def chunk_fn(args):
        q_c, g_c, c0 = args
        t = c0 + jnp.arange(Q_CHUNK, dtype=jnp.int32)

        dist = (t[:, None] - cmp_end[None, :]).astype(jnp.float32)
        valid = dist >= 0
        s = jnp.einsum('bghqd,bgnd->bghqn', q_c, k_cmp).astype(jnp.float32) * scale
        s = jnp.where(valid, s - slopes * dist, NEG)
        p_cmp = jax.nn.softmax(s, axis=-1) * valid.any(-1, keepdims=True)
        o_cmp = jnp.einsum('bghqn,bgnd->bghqd', p_cmp.astype(v_cmp.dtype), v_cmp)

        imp = jnp.einsum('bghqn,nj->bgqj', p_cmp, overlap)
        t_blk = t // L_SLC
        forced = (blk[None] == 0) | (blk[None] == t_blk[:, None]) | (blk[None] == t_blk[:, None] - 1)
        causal = blk[None] * L_SLC <= t[:, None]
        imp = jnp.where(forced, FORCE, jnp.where(causal, imp, -FORCE))
        _, sel = lax.top_k(imp, k_sel)
        ks = k_slc_blk[bidx, gidx, sel]
        vs = v_slc_blk[bidx, gidx, sel]
        pos = sel[..., None] * L_SLC + jnp.arange(L_SLC, dtype=jnp.int32)
        dist = (t[None, None, :, None, None] - pos).astype(jnp.float32)[:, :, None]
        s = jnp.einsum('bghqd,bgqkld->bghqkl', q_c, ks).astype(jnp.float32) * scale
        s = jnp.where(dist >= 0, s - slopes[..., None] * dist, NEG)
        p = jax.nn.softmax(s.reshape(B, G, Hg, Q_CHUNK, k_sel * L_SLC), axis=-1)
        o_slc = jnp.einsum('bghqm,bgqmd->bghqd', p.astype(vs.dtype),
                           vs.reshape(B, G, Q_CHUNK, k_sel * L_SLC, dh))

        kw = lax.dynamic_slice_in_dim(k_win_pad, c0, WINDOW + Q_CHUNK, axis=2)
        vw = lax.dynamic_slice_in_dim(v_win_pad, c0, WINDOW + Q_CHUNK, axis=2)
        s_pos = c0 - WINDOW + jnp.arange(WINDOW + Q_CHUNK, dtype=jnp.int32)
        dist = (t[:, None] - s_pos[None, :]).astype(jnp.float32)
        ok = (dist >= 0) & (dist < WINDOW) & (s_pos[None, :] >= 0)
        s = jnp.einsum('bghqd,bgmd->bghqm', q_c, kw).astype(jnp.float32) * scale
        s = jnp.where(ok, s - slopes * dist, NEG)
        p = jax.nn.softmax(s, axis=-1)
        o_win = jnp.einsum('bghqm,bgmd->bghqd', p.astype(vw.dtype), vw)

        o = (g_c[0][..., None] * o_cmp + g_c[1][..., None] * o_slc
             + g_c[2][..., None] * o_win)
        return o.transpose(0, 3, 1, 2, 4).reshape(B, Q_CHUNK, N_HEADS * dh).astype(x.dtype)

    out = lax.map(chunk_fn, (q, gates, starts))
    out = out.transpose(1, 0, 2, 3).reshape(B, S, N_HEADS * dh)
    return out @ w_out

def second_inputs(seed: int = 0) -> dict:
    key = jax.random.key(seed)
    ks = jax.random.split(key, 32)
    n_a = DEPTH_2 // 2
    n_b = DEPTH_2 - n_a
    D, F = D_MODEL, FFN_HIDDEN
    f32 = jnp.float32

    def w(k, shape, fan_in):
        return jax.random.normal(k, shape, f32) * fan_in ** -0.5

    def gain(k, shape):
        return 1.0 + 0.05 * jax.random.normal(k, shape, f32)

    def bias(k, shape):
        return 0.02 * jax.random.normal(k, shape, f32)

    return {
        "x": jax.random.normal(ks[0], (BATCH, SEQ, D), f32),
        "a_norm": gain(ks[1], (n_a, D)),
        "a_pw1_w": w(ks[2], (n_a, D, 2 * D), D),
        "a_pw1_b": bias(ks[3], (n_a, 2 * D)),
        "a_dw_w": w(ks[4], (n_a, CONV_WIDTH, D), CONV_WIDTH),
        "a_dw_b": bias(ks[5], (n_a, D)),
        "a_ln_g": gain(ks[6], (n_a, D)),
        "a_ln_b": bias(ks[7], (n_a, D)),
        "a_pw2_w": w(ks[8], (n_a, D, D), D),
        "a_pw2_b": bias(ks[9], (n_a, D)),
        "kv_norm": gain(ks[10], (D,)),
        "w_kv": w(ks[11], (D, N_KV_PARTS * N_KV_GROUPS * HEAD_DIM), D),
        "cmp_pos_k": 0.1 * jax.random.normal(ks[12], (L_CMP, HEAD_DIM), f32),
        "cmp_pos_v": 0.1 * jax.random.normal(ks[13], (L_CMP, HEAD_DIM), f32),
        "phi_k_w1": w(ks[14], (L_CMP * HEAD_DIM, HEAD_DIM), L_CMP * HEAD_DIM),
        "phi_k_w2": w(ks[15], (HEAD_DIM, HEAD_DIM), HEAD_DIM),
        "phi_v_w1": w(ks[16], (L_CMP * HEAD_DIM, HEAD_DIM), L_CMP * HEAD_DIM),
        "phi_v_w2": w(ks[17], (HEAD_DIM, HEAD_DIM), HEAD_DIM),
        "b_norm": gain(ks[18], (n_b, D)),
        "b_w_in": w(ks[19], (n_b, D, N_HEADS * HEAD_DIM + N_BRANCH * N_HEADS), D),
        "b_w_out": w(ks[20], (n_b, N_HEADS * HEAD_DIM, D), N_HEADS * HEAD_DIM),
        "ffn_norm": gain(ks[21], (DEPTH_2, D)),
        "ffn_w_in": w(ks[22], (DEPTH_2, D, 2 * F), D),
        "ffn_w_out": w(ks[23], (DEPTH_2, F, D), F),
        "final_norm": gain(ks[24], (D,)),
    }

def second_block(x, a_norm, a_pw1_w, a_pw1_b, a_dw_w, a_dw_b, a_ln_g, a_ln_b, a_pw2_w, a_pw2_b,
              kv_norm, w_kv, cmp_pos_k, cmp_pos_v, phi_k_w1, phi_k_w2, phi_v_w1, phi_v_w2,
              b_norm, b_w_in, b_w_out, ffn_norm, ffn_w_in, ffn_w_out, final_norm):
    n_a = DEPTH_2 // 2
    h = x
    kv = None
    for layer in range(DEPTH_2):
        if layer < n_a:
            i = layer
            h = h + conformer_conv(h, a_norm[i], a_pw1_w[i], a_pw1_b[i], a_dw_w[i], a_dw_b[i],
                                   a_ln_g[i], a_ln_b[i], a_pw2_w[i], a_pw2_b[i])
        else:
            j = layer - n_a
            h = h + nsa_attention(h, b_norm[j], b_w_in[j], b_w_out[j], kv)
        h = h + swiglu_ffn(h, ffn_norm[layer], ffn_w_in[layer], ffn_w_out[layer])
        if layer == n_a - 1:
            kv = shared_kv(h, kv_norm, w_kv, cmp_pos_k, cmp_pos_v,
                           phi_k_w1, phi_k_w2, phi_v_w1, phi_v_w2)
    return rmsnorm(h, final_norm)


def setup_inputs(seed=0):
    out = dict(first_inputs(seed))
    for name, value in second_inputs(seed + 1).items():
        if name != "x":
            out[name + "_2"] = value
    return out


def reference(
    x, mem, mem_norm, norm_pre_mix, norm_post_mix, norm_pre_ffn, norm_post_ffn, w_mem_kv, w_out,
    w_ffn_in, w_ffn_out, gdn_w_in, gdn_conv, gdn_a_log, gdn_dt_bias, gdn_out_norm, ml_w_in,
    ml_i_bias, ml_f_bias, ml_out_norm, sb_w_in, a_norm_2, a_pw1_w_2, a_pw1_b_2, a_dw_w_2,
    a_dw_b_2, a_ln_g_2, a_ln_b_2, a_pw2_w_2, a_pw2_b_2, kv_norm_2, w_kv_2, cmp_pos_k_2,
    cmp_pos_v_2, phi_k_w1_2, phi_k_w2_2, phi_v_w1_2, phi_v_w2_2, b_norm_2, b_w_in_2, b_w_out_2,
    ffn_norm_2, ffn_w_in_2, ffn_w_out_2, final_norm_2,
):
    x = first_block(
        x, mem, mem_norm, norm_pre_mix, norm_post_mix, norm_pre_ffn, norm_post_ffn, w_mem_kv,
        w_out, w_ffn_in, w_ffn_out, gdn_w_in, gdn_conv, gdn_a_log, gdn_dt_bias, gdn_out_norm,
        ml_w_in, ml_i_bias, ml_f_bias, ml_out_norm, sb_w_in,
    )
    return second_block(
        x, a_norm_2, a_pw1_w_2, a_pw1_b_2, a_dw_w_2, a_dw_b_2, a_ln_g_2, a_ln_b_2, a_pw2_w_2,
        a_pw2_b_2, kv_norm_2, w_kv_2, cmp_pos_k_2, cmp_pos_v_2, phi_k_w1_2, phi_k_w2_2,
        phi_v_w1_2, phi_v_w2_2, b_norm_2, b_w_in_2, b_w_out_2, ffn_norm_2, ffn_w_in_2,
        ffn_w_out_2, final_norm_2,
    )


_drawn_inputs = setup_inputs


def setup_inputs(seed=0):
    import zlib

    import numpy as np

    out = dict(_drawn_inputs(seed))
    spreads = {}
    factors = {'mem_norm': 8.0,
     'norm_post_mix': 3.124,
     'norm_pre_ffn': 2.921,
     'norm_post_ffn': 4.241,
     'gdn_out_norm': 3.266,
     'a_norm_2': 2.773,
     'a_pw1_b_2': 6.736,
     'a_dw_b_2': 3.74,
     'a_ln_b_2': 7.18,
     'a_pw2_b_2': 4.327,
     'kv_norm_2': 4.971,
     'cmp_pos_k_2': 8.0,
     'cmp_pos_v_2': 3.985,
     'b_norm_2': 8.0}
    for name, (base, spread) in spreads.items():
        noise = np.random.default_rng([zlib.crc32(name.encode()), seed]).standard_normal(out[name].shape)
        drawn = base * np.exp(spread * noise) if base else spread * noise
        out[name] = __import__('jax').numpy.asarray(drawn.astype(out[name].dtype))
    for name, factor in factors.items():
        out[name] = (out[name] * factor).astype(out[name].dtype)
    return out
```

```python
from contextlib import ExitStack

import numpy as np

import concourse.bass as bass
from concourse import mybir

F32 = mybir.dt.float32
F32R = mybir.dt.float32r
ALU = mybir.AluOpType
ACT = mybir.ActivationFunctionType
AX = mybir.AxisListType

P = 128
SEQ = 512
D = 1024
DT = D // P
NB = SEQ // P
EPS = 1e-6
HEADS = 8
CONV_K = 4
MEM = 256
MEM_HEADS = 4
DFF = 2816
FT = DFF // P
TAPS = 31
PAD = TAPS - 1
N_CMP = 31
L_CMP = 32
STRIDE = 16
NQ = 8
LEVELS = 7
FAR = 1.0e34

SEGMENTS = [
    ("mem", 8, 9), ("gdn", 8, 36), ("out1", 6, 16), ("in1", 8, 44), ("down1", 11, 16),
    ("pw1", 8, 16), ("pw2", 8, 8), ("in2", 8, 44), ("down2", 11, 16),
    ("kvq", 8, 15), ("out2", 8, 8), ("in3", 8, 44), ("down3", 11, 16),
]
UNITS_PER_TILE = {8: 1, 6: 2, 11: 2}
SLOT = 11 * P


class Segment:

    def __init__(self, unit0, tile0, source0, kt, units):
        self.unit0, self.tile0, self.source0, self.kt, self.units = unit0, tile0, source0, kt, units
        self.per_tile = UNITS_PER_TILE[kt]


def plan_segments():
    table, unit, tile, source = {}, 0, 0, {8: 0, 6: 0, 11: 0}
    for name, kt, units in SEGMENTS:
        table[name] = Segment(unit, tile, source[kt], kt, units)
        unit += units
        source[kt] += units
        tile += units // UNITS_PER_TILE[kt]
    return table


SEG = plan_segments()

PARAMS = {}
_at = 0
for _name, _n in [("mem_norm", DT), ("pre_mix", DT), ("post_mix", DT), ("pre_ffn", DT), ("post_ffn", DT),
                  ("gdn_out", 1), ("conv4", 24 * CONV_K), ("a_norm", DT), ("pw1_a", DT), ("pw1_b", DT),
                  ("dw_b", DT), ("ln_g", DT), ("ln_b", DT), ("pw2_b", DT), ("kv_norm", DT), ("b_norm", DT),
                  ("ffn1", DT), ("ffn2", DT), ("final", DT), ("a_log", 1), ("dt_bias", 1), ("slopes", 16),
                  ("conv31", DT * TAPS), ("pos_k", L_CMP), ("pos_v", L_CMP)]:
    PARAMS[_name] = (_at, _n)
    _at += _n
N_PARAMS = _at

IDENT, ONES, TRI, LEVEL0 = 0, 1, 2, 3
N_CONST = LEVEL0 + LEVELS


def constant_tables():
    p, f = np.arange(P)[:, None], np.arange(P)[None, :]
    square = np.zeros((P, N_CONST, P), np.float32)
    square[:, IDENT] = p == f
    square[:, ONES] = 1.0
    square[:, TRI] = p <= f
    for s in range(LEVELS):
        square[:, LEVEL0 + s] = (p >> (s + 1) == f >> (s + 1)) & (p >> s & 1 == 1) & (f >> s & 1 == 0)
    dist = SEQ - P + p - np.arange(SEQ)[None, :]
    dist = np.where(dist >= 0, dist, FAR).astype(np.float32)
    n = np.arange(32)[None, None, :]
    t = np.arange(NB)[None, :, None] * P + np.arange(P)[:, None, None]
    cmp = t - (n * STRIDE + L_CMP - 1)
    cmp = np.where((cmp >= 0) & (n < N_CMP), cmp, FAR).astype(np.float32)
    seen = np.broadcast_to(t >= L_CMP - 1, (P, NB, 1)).reshape(P, NB).astype(np.float32)
    return np.concatenate([square.reshape(P, -1), dist, cmp.reshape(P, -1), seen], axis=1)


TABLE_COLS = N_CONST * P + SEQ + NB * 32 + NB
TABLE_ROOM = -(-4 * TABLE_COLS // 32) * 32
PARAM_ROOM = -(-4 * N_PARAMS // 32) * 32


def program(nc, t, out, stop=None):
    with ExitStack() as ctx:
        base = nc.sbuf_base
        base = (base + 31) // 32 * 32
        KB = 1024

        def at(name, offset, cols, dt=F32, parts=P):
            return nc.alloc_sbuf_tensor_at(name, [parts, cols], dt, offset=base + offset)

        hT = at("hT", 0, DT * SEQ)
        XR = at("XR", 16 * KB, DT * SEQ, F32R)
        XL = at("XL", 32 * KB, DT * SEQ, F32R)
        raw = at("raw", 48 * KB, 2 * SLOT)
        WR = at("WR", 59 * KB, 2 * SLOT, F32R)
        WL = at("WL", 70 * KB, 2 * SLOT, F32R)
        MR = at("MR", 81 * KB, FT * SEQ, F32R)
        ML = at("ML", 125 * KB, FT * SEQ, F32R)
        Y = at("Y", 169 * KB, DT * SEQ)
        table = at("table", 185 * KB, TABLE_COLS)
        params = at("params", 185 * KB + TABLE_ROOM, N_PARAMS)
        low = 185 * KB + TABLE_ROOM + PARAM_ROOM
        R = at("R", low, SEQ)
        small = at("small", low + 2 * KB, 8)
        ctx.enter_context(nc.sbuf_tensor("fence", [P, (low + 2 * KB + 32 + 64) // 4], F32))

        X_R = XR[:, :].rearrange("p (k n) -> p k n", k=DT)
        X_L = XL[:, :].rearrange("p (k n) -> p k n", k=DT)
        M_R = MR[:, :].rearrange("p (k n) -> p k n", k=FT)
        M_L = ML[:, :].rearrange("p (k n) -> p k n", k=FT)

        def const(i):
            return table[:, i * P:(i + 1) * P]

        ident, ones, tri = const(IDENT), const(ONES), const(TRI)
        dist = table[:, N_CONST * P:N_CONST * P + SEQ]
        dist_cmp = table[:, N_CONST * P + SEQ:N_CONST * P + SEQ + NB * 32]
        seen = table[:, TABLE_COLS - NB:TABLE_COLS]
        eps_col, one_col = small[:, 0:1], small[:, 1:2]

        def param(name, i=0, n=1):
            first = PARAMS[name][0]
            return params[:, first + i:first + i + n] if isinstance(i, int) else params[:, bass.ds(first + i, n)]

        bank = [ctx.enter_context(nc.psum_tensor(f"bank{i}", [P, 512], F32)) for i in range(8)]

        def sem(name):
            return ctx.enter_context(nc.semaphore(name))

        tables_loaded = sem("tables_loaded")
        x_loaded = sem("x_loaded")
        eps_set = sem("eps_set")
        passed = sem("passed")
        weight_loaded = [sem(f"weight_loaded{i}") for i in range(2)]
        high_split = sem("high_split")
        weight_split = sem("weight_split")
        unit_done = sem("unit_done")
        tile_taken = sem("tile_taken")
        input_high = sem("input_high")
        input_ready = sem("input_ready")
        squared = sem("squared")
        summed = sem("summed")
        total_done = sem("total_done")
        log_done = sem("log_done")
        norm_ready = sem("norm_ready")
        vec = sem("vec")
        sca = sem("sca")
        stored = sem("stored")

        def wait_apart(engine, semaphore, value):
            engine.wait_ge(semaphore, value)
            engine.sem_inc(passed, 1)

        source = {8: t["w8"], 6: t["w6"], 11: t["w11"]}

        def load_unit(sp, seg, unit, row, slot):
            if not (isinstance(unit, int) and unit < 2):
                sp.wait_ge(weight_split, unit - 1)
            sp.dma_start(raw[:, slot * SLOT:slot * SLOT + seg.kt * P],
                         source[seg.kt][row]).then_inc(weight_loaded[slot], 16)

        def split_unit(pool, seg, unit, turn, slot):
            here = slice(slot * SLOT, slot * SLOT + seg.kt * P)
            pool.wait_ge(weight_loaded[slot], turn * 16 + 16)
            if not (isinstance(unit, int) and unit < 2):
                wait_apart(pool, unit_done, unit - 1)
            nc.gpsimd.tensor_copy(WR[:, here], raw[:, here]).then_inc(high_split, 1)
            pool.wait_ge(high_split, unit + 1)
            nc.gpsimd.tensor_tensor(WL[:, here], raw[:, here], WR[:, here].bitcast(F32),
                                    ALU.subtract).then_inc(weight_split, 1)

        def stream(engine, seg, step):
            pairs = seg.units // 2
            u0 = seg.unit0
            peel = 1 if u0 == 0 else 0
            for j in range(2 * peel):
                step(j, j, 0, j)
            with engine.Fori(peel, pairs) as i:
                for j in range(2):
                    slot = (u0 + j) % 2
                    step(i * 2 + (u0 + j), i * 2 + j, i + (u0 + j) // 2, slot)
            if seg.units % 2:
                j = seg.units - 1
                step(u0 + j, j, (u0 + j) // 2, (u0 + j) % 2)

        def products(pe, seg, unit, slot, k0, into, xr, xl, first, last, ks=None):
            n = seg.kt if ks is None else ks[1] - ks[0]
            k_from = 0 if ks is None else ks[0]
            if k_from == 0:
                pe.wait_ge(weight_split, unit + 1)
            for k in range(k_from, k_from + n):
                wr = WR[:, slot * SLOT + k * P:slot * SLOT + (k + 1) * P]
                wl = WL[:, slot * SLOT + k * P:slot * SLOT + (k + 1) * P]
                start, stop = first and k == 0, last and k == seg.kt - 1
                nc.tensor.matmul(into, wr, xr(k0 + k), start=start, stop=False)
                nc.tensor.matmul(into, wr, xl(k0 + k), start=False, stop=False)
                mm = nc.tensor.matmul(into, wl, xr(k0 + k), start=False, stop=stop)
            if k_from + n == seg.kt:
                mm.then_inc(unit_done, 1)

        def tiles(pe, seg, xr, xl):
            u0, t0 = seg.unit0, seg.tile0
            if seg.per_tile == 1:
                with pe.Fori(0, seg.units // 2) as i:
                    for j in range(2):
                        pe.wait_ge(tile_taken, i * 2 + (t0 + j - 1))
                        products(pe, seg, i * 2 + (u0 + j), (u0 + j) % 2, 0, bank[(t0 + j) % 2][:, :],
                                 xr, xl, True, True)
            else:
                n = seg.units // 2
                with pe.Fori(0, n // 2) as i:
                    for j in range(2):
                        pe.wait_ge(tile_taken, i * 2 + (t0 + j - 1))
                        for half in range(2):
                            products(pe, seg, i * 4 + (u0 + 2 * j + half), (u0 + half) % 2, half * seg.kt,
                                     bank[(t0 + j) % 2][:, :], xr, xl, half == 0, half == 1)


        class Order:

            def __init__(self, engine, s):
                self.engine, self.s, self.base, self.k, self.i, self.per = engine, s, 0, 0, None, 0

            def value(self):
                return self.base + self.k if self.i is None else self.i * self.per + (self.base + self.k)

            def mark(self, ins):
                ins.then_inc(self.s, 1)
                self.k += 1

            def sync(self):
                self.engine.wait_ge(self.s, self.value())

            def link(self, ins):
                self.mark(ins)
                self.sync()

            def enter(self, i, per):
                self.base, self.k, self.i, self.per = self.base + self.k, 0, i, per

            def leave(self, turns):
                assert self.k == self.per, f"{self.k} marks in a loop of {self.per}"
                self.base, self.k, self.i = self.base + self.per * turns, 0, None

        def cols(tile, i, n=SEQ):
            return tile[:, i * n:(i + 1) * n] if isinstance(i, int) else tile[:, bass.ds(i * n, n)]

        def blocks(tile):
            return tile.rearrange("p (b n) -> p b n", b=NB)

        def over_blocks(square):
            return square.unsqueeze(1).broadcast_to([P, NB, P])

        def over_columns(scalars, n=P):
            return scalars.unsqueeze(2).broadcast_to([P, scalars.shape[1], n])

        NORM = {n: i for i, n in enumerate(["mem", "x", "mix", "h1", "ffn", "h2", "var", "h3", "h4", "h5", "h6"])}
        INPUT = {n: DT * i for i, n in enumerate(["mem", "x", "h1", "h2", "conv", "h3", "kv", "q", "h5"])}
        SQ = at("SQ", low + 2 * KB + 32, 2 * SEQ)
        ACC = at("ACC", low + 6 * KB + 32, SEQ)

        def square_tile(act, norm, n, parity, src, width=SEQ):
            if not (isinstance(n, int) and NORM[norm] == 0 and n < 2):
                wait_apart(act, summed, n + (DT * NORM[norm] - 1))
            nc.scalar.activation(SQ[:, parity * SEQ:parity * SEQ + width], src, ACT.Square).then_inc(squared, 1)

        def clear_sum(dve, order, norm, width=SEQ):
            if NORM[norm]:
                dve.wait_ge(total_done, NORM[norm])
            order.link(nc.vector.memset(ACC[:, 0:width], 0.0))

        def add_squares(dve, norm, n, parity, width=SEQ):
            dve.wait_ge(squared, n + (DT * NORM[norm] + 1))
            if not (isinstance(n, int) and NORM[norm] == 0 and n == 0):
                dve.wait_ge(summed, n + DT * NORM[norm])
            nc.vector.tensor_tensor(ACC[:, 0:width], ACC[:, 0:width], SQ[:, parity * SEQ:parity * SEQ + width],
                                    ALU.add).then_inc(summed, 1)

        def total(pe, norm, width=SEQ):
            pe.wait_ge(summed, DT * (NORM[norm] + 1))
            nc.tensor.matmul(bank[2][:, 0:width], ones, ACC[:, 0:width], start=True, stop=True).then_inc(total_done, 1)

        def root(act, norm, width=SEQ):
            e = NORM[norm]
            act.wait_ge(total_done, e + 1)
            nc.scalar.activation(R[:, 0:width], bank[2][:, 0:width], ACT.Ln, bias=eps_col, scale=1.0 / D).then_inc(log_done, 1)
            act.wait_ge(log_done, e + 1)
            nc.scalar.activation(R[:, 0:width], R[:, 0:width], ACT.Exp, scale=-0.5).then_inc(norm_ready, 1)

        def high_part(act, name, n, dst, src, gain):
            nc.scalar.activation(dst, src, ACT.Identity, scale=gain).then_inc(input_high, 1)

        def low_part(dve, name, n, dst, src, high, gain):
            dve.wait_ge(input_high, n + (INPUT[name] + 1))
            nc.vector.scalar_tensor_tensor(dst, src, gain, high.bitcast(F32), ALU.mult, ALU.subtract).then_inc(input_ready, 1)

        mem_loaded = sem("mem_loaded")
        scratch = {}

        def place(regions):
            for start, size, names in regions:
                spot = start
                for name, n in names:
                    scratch[name] = at(name, spot, n)
                    spot += (4 * n + 31) // 32 * 32
                assert spot <= start + size, (names[-1][0], spot - start - size)

        HP = SEQ + 8
        place([
            ((81 + 24) * KB, 20 * KB, [("pre0", HP), ("pre1", HP), ("pre2", HP), ("act0", SEQ), ("act1", SEQ),
                                       ("act2", SEQ), ("gate_z", SEQ), ("keys", SEQ), ("queries", SEQ)]),
            ((125 + 24) * KB, 20 * KB, [("D_E", SEQ), ("q_decayed", SEQ), ("v_beta", SEQ), ("k_gained", SEQ),
                                        ("lower", SEQ), ("pT", SEQ), ("low_a", SEQ), ("low_b", SEQ), ("T", SEQ),
                                        ("U", SEQ)]),
            (169 * KB, 16 * KB, [("As", SEQ), ("sq_k", SEQ), ("sq_q", SEQ), ("r_k", SEQ), ("r_q", SEQ),
                                 ("o_rows", SEQ), ("S", P), ("X", P), ("v_new", P), ("scalars", 6 * 32)]),
        ])
        g_ = scratch
        memT = at("memT", 169 * KB, DT * MEM)
        mem_t = at("mem_t", (81 + 24) * KB, 2 * MEM)
        x_t = at("x_t", (81 + 28) * KB, 2 * SEQ)
        q_mem = at("q_mem", 0, MEM_HEADS * SEQ)
        mem_keys = at("mem_keys", 8 * KB, MEM_HEADS * MEM)
        mem_values = at("mem_values", 12 * KB, 2 * SEQ)
        gates40 = at("gates40", (125 + 24) * KB, SEQ, parts=64)
        gate_t = at("gate_t", (125 + 26) * KB, SEQ, parts=64)
        gate_u = at("gate_u", (125 + 28) * KB, SEQ, parts=64)
        scal = g_["scalars"]
        beta, cum, k_gain, last_gain, neg_beta_decay, gcol = (scal[:, 32 * i:32 * i + 32] for i in range(6))

        mem_in_R = MR[:, 0:DT * MEM].rearrange("p (k n) -> p k n", k=DT)
        mem_in_L = ML[:, 0:DT * MEM].rearrange("p (k n) -> p k n", k=DT)

        scaled = sem("scaled")
        gate_part = sem("gate_part")
        gate_act = sem("gate_act")
        gates_turned = sem("gates_turned")
        gates_copied = sem("gates_copied")
        sums_done = sem("sums_done")
        decay_exp = sem("decay_exp")
        gates_ready = sem("gates_ready")

        def split_normed(act, dve, name, n, dst_r, dst_l, tmp):
            if act is not None:
                act.wait_ge(scaled, INPUT[name] + n + 1)
                nc.scalar.activation(dst_r, tmp, ACT.Identity).then_inc(input_high, 1)
            else:
                dve.wait_ge(input_high, INPUT[name] + n + 1)
                nc.vector.tensor_tensor(dst_l, tmp, dst_r.bitcast(F32), ALU.subtract).then_inc(input_ready, 1)

        START = [("mem", memT, MEM, "mem_norm", mem_t, mem_in_R, mem_in_L),
                 ("x", hT, SEQ, "pre_mix", x_t, X_R, X_L)]

        def start_scalar(act):
            act.wait_ge(tables_loaded, 32)
            for e, (name, src, w, gain, tmp, dr, dl) in enumerate(START):
                if e == 0:
                    act.wait_ge(mem_loaded, 16)
                    act.wait_ge(eps_set, 1)
                else:
                    act.wait_ge(x_loaded, 16)
                for n in range(DT):
                    square_tile(act, name, n, n % 2, cols(src, n, w), w)
                root(act, name, w)
                for n in range(DT):
                    split_normed(act, None, name, n, dr[:, n], dl[:, n], cols(tmp, n % 2, w))

        def start_vector(dve, order):
            nc.vector.memset(eps_col, EPS)
            nc.vector.memset(one_col, 1.0).then_inc(eps_set, 1)
            dve.wait_ge(tables_loaded, 32)
            for e, (name, src, w, gain, tmp, dr, dl) in enumerate(START):
                clear_sum(dve, order, name, w)
                for n in range(DT):
                    add_squares(dve, name, n, n % 2, w)
                dve.wait_ge(norm_ready, e + 1)
                for n in range(DT + 1):
                    if n < DT:
                        if n >= 2:
                            dve.wait_ge(input_ready, INPUT[name] + n - 1)
                        nc.vector.scalar_tensor_tensor(cols(tmp, n % 2, w), cols(src, n, w), param(gain, n), R[:, 0:w],
                                                       ALU.mult, ALU.mult).then_inc(scaled, 1)
                    if n:
                        split_normed(None, dve, name, n - 1, dr[:, n - 1], dl[:, n - 1], cols(tmp, (n - 1) % 2, w))

        def mem_tensor(pe):
            pe.wait_ge(tables_loaded, 32)
            total(pe, "mem", MEM)
            pe.wait_ge(input_ready, DT)
            seg = SEG["mem"]
            for j in range(MEM_HEADS):
                if j == 2:
                    total(pe, "x")
                if j >= 2:
                    pe.wait_ge(tile_taken, j - 1)
                products(pe, seg, j, j % 2, 0, bank[j % 2][:, 0:MEM], lambda k: mem_in_R[:, k], lambda k: mem_in_L[:, k], True, True)
            pe.wait_ge(tile_taken, 4)
            for u in range(4):
                pe.wait_ge(weight_split, 5 + u)
                for kk in range(2):
                    k = 2 * u + kk
                    here = slice((u % 2) * SLOT + kk * SEQ, (u % 2) * SLOT + (kk + 1) * SEQ)
                    for b in range(2):
                        tok = slice(b * P, (b + 1) * P)
                        nc.tensor.matmul(bank[b][:, :], mem_in_R[:, k, tok], WR[:, here], start=k == 0, stop=False)
                        nc.tensor.matmul(bank[b][:, :], mem_in_L[:, k, tok], WR[:, here], start=False, stop=False)
                        mm = nc.tensor.matmul(bank[b][:, :], mem_in_R[:, k, tok], WL[:, here], start=False, stop=k == DT - 1)
                mm.then_inc(unit_done, 1)
            pe.wait_ge(input_ready, 2 * DT)
            pe.wait_ge(tile_taken, 8)
            products(pe, seg, 8, 0, 0, bank[0][:, :], lambda k: X_R[:, k], lambda k: X_L[:, k], True, True)

        def mem_scalar(act):
            for j in range(MEM_HEADS):
                act.wait_ge(unit_done, j + 1)
                if j == 0:
                    act.wait_ge(scaled, 2 * DT)
                nc.scalar.activation(cols(mem_keys, j, MEM), bank[j % 2][:, 0:MEM], ACT.Identity).then_inc(tile_taken, 1)
            act.wait_ge(unit_done, 8)
            for j in range(4):
                b, half = j // 2, j % 2
                nc.scalar.activation(mem_values[:, b * SEQ + half * MEM:b * SEQ + (half + 1) * MEM],
                                     bank[b][:, half * MEM:(half + 1) * MEM], ACT.Identity).then_inc(tile_taken, 1)

        def gates_scalar(act):
            act.wait_ge(gate_part, 1)
            nc.scalar.activation(gate_u[0:8, :], gate_u[0:8, :], ACT.Exp, scale=-1.0).then_inc(gate_act, 1)
            nc.scalar.activation(small[0:8, 2:3], param("a_log")[0:8], ACT.Exp).then_inc(gate_act, 1)
            act.wait_ge(gate_act, 1)
            nc.scalar.activation(gate_u[0:8, :], gate_u[0:8, :], ACT.Ln, bias=one_col[0:8]).then_inc(gate_act, 1)
            act.wait_ge(gate_part, 2)
            nc.scalar.activation(gates40[32:40, :], gates40[32:40, :], ACT.Sigmoid).then_inc(gate_act, 1)
            act.wait_ge(gate_part, 5)
            for i, (dst, src) in enumerate([(k_gain, k_gain), (last_gain, last_gain), (neg_beta_decay, cum)]):
                nc.scalar.activation(dst, src, ACT.Exp).then_inc(decay_exp, 1)

        def gates_vector(dve, order):
            order.link(nc.vector.memset(gates40[:, :], 0.0))
            dve.wait_ge(unit_done, 9)
            order.link(nc.vector.tensor_scalar(gate_t[0:8, :], bank[0][0:8, :], param("dt_bias")[0:8], None, ALU.add))
            nc.vector.scalar_tensor_tensor(gate_u[0:8, :], gate_t[0:8, :], -1.0, gate_t[0:8, :], ALU.mult, ALU.max).then_inc(gate_part, 1)
            nc.vector.tensor_copy(gates40[32:40, :], bank[0][32:40, :]).then_inc(gate_part, 1)
            dve.wait_ge(gate_part, 2)
            nc.vector.tensor_scalar(gate_t[0:8, :], gate_t[0:8, :], 0.0, None, ALU.max).then_inc(tile_taken, 1)
            dve.wait_ge(tile_taken, 9)
            dve.wait_ge(gate_act, 3)
            order.link(nc.vector.tensor_tensor(gate_t[0:8, :], gate_t[0:8, :], gate_u[0:8, :], ALU.add))
            nc.vector.tensor_scalar(gates40[0:8, :], gate_t[0:8, :], small[0:8, 2:3], -1.0, ALU.mult, ALU.mult).then_inc(gate_part, 1)
            dve.wait_ge(gates_turned, 1)
            turned = bank[3][:, 0:NB * 40].rearrange("p (b c) -> p c b", b=NB)
            nc.vector.tensor_copy(gcol.rearrange("p (h b) -> p h b", b=NB), turned[:, 0:8]).then_inc(gates_copied, 1)
            nc.vector.tensor_copy(beta.rearrange("p (h b) -> p h b", b=NB), turned[:, 32:40]).then_inc(gates_copied, 1)
            dve.wait_ge(sums_done, 1)
            order.link(nc.vector.tensor_copy(cum, bank[4][:, 0:32]))
            nc.vector.tensor_tensor(k_gain, bank[4][:, 32:64], cum, ALU.subtract).then_inc(gate_part, 1)
            nc.vector.tensor_copy(last_gain, bank[4][:, 32:64]).then_inc(gate_part, 1)
            dve.wait_ge(decay_exp, 3)
            nc.vector.scalar_tensor_tensor(neg_beta_decay, neg_beta_decay, -1.0, beta, ALU.mult, ALU.mult).then_inc(gates_ready, 1)
            dve.wait_ge(gates_ready, 1)

        def gates_tensor(pe):
            pe.wait_ge(gate_part, 3)
            pe.wait_ge(gate_act, 4)
            for b in range(NB):
                mm = nc.tensor.transpose(bank[3][:, b * 40:b * 40 + 40], gates40[0:40, b * P:(b + 1) * P], ident[0:40, 0:40])
            mm.then_inc(gates_turned, 1)
            pe.wait_ge(gates_copied, 2)
            nc.tensor.matmul(bank[4][:, 0:32], tri, gcol, start=True, stop=True)
            nc.tensor.matmul(bank[4][:, 32:64], ones, gcol, start=True, stop=True).then_inc(sums_done, 1)

        names = ("conv_done silu_done keys_squared norm_summed norms_rooted keys_ready queries_ready "
                 "gate_rows_ready rows_done gap_ready decay_ready row_decay_ready q_decayed_ready v_turned "
                 "k_turned v_beta_ready k_gained_ready kk_done qk_done pT_ready T_ready T_turned U_ready "
                 "low_ready A_done A_ready UT_done UT_ready kS_done X_ready v_done v_ready o_done S_sum_done "
                 "S_ready o_squared o_copied o_summed o_rooted z_ready head_ready head_high head_stored").split()
        s_ = {n: sem(n) for n in names}
        GROUP_TILES = 4
        seg_g = SEG["gdn"]
        pre = [g_["pre0"], g_["pre1"], g_["pre2"]]
        acts = [g_["act0"], g_["act1"], g_["act2"]]
        QS = float(P) ** -0.5

        def row4(tile, h):
            return tile[:, bass.ds(h * NB, NB)] if not isinstance(h, int) else tile[:, h * NB:(h + 1) * NB]

        def col1(tile, h, b):
            return tile[:, bass.ds(h * NB + b, 1)] if not isinstance(h, int) else tile[:, h * NB + b:h * NB + b + 1]

        def group_chunks(pe, g):
            for j in range(GROUP_TILES):
                unit = g * GROUP_TILES + (seg_g.unit0 + j)
                pe.wait_ge(tile_taken, g * GROUP_TILES + (seg_g.tile0 + j - 1))
                for k in range(DT):
                    products(pe, seg_g, unit, (seg_g.unit0 + j) % 2, 0, bank[(seg_g.tile0 + j) % 2][:, :],
                             lambda k: X_R[:, k], lambda k: X_L[:, k], True, True, ks=(k, k + 1))
                    yield

        def head_tensor(pe, h, g):
            chunks = group_chunks(pe, g)

            def gap(n):
                for _ in range(n):
                    next(chunks, None)

            pe.wait_ge(s_["keys_squared"], h * 2 + 1)
            nc.tensor.matmul(bank[2][:, :], ones, g_["sq_k"][:, :], start=True, stop=True).then_inc(s_["norm_summed"], 1)
            pe.wait_ge(s_["keys_squared"], h * 2 + 2)
            nc.tensor.matmul(bank[3][:, :], ones, g_["sq_q"][:, :], start=True, stop=True).then_inc(s_["norm_summed"], 1)
            pe.wait_ge(s_["gate_rows_ready"], h + 1)
            nc.tensor.matmul(bank[4][:, :], ones, g_["D_E"][:, :], start=True, stop=True).then_inc(s_["rows_done"], 1)
            pe.wait_ge(s_["silu_done"], h * 3 + 2)
            for b in range(NB):
                mm = nc.tensor.transpose(bank[5][:, b * P:(b + 1) * P], acts[1][:, b * P:(b + 1) * P], ident)
            mm.then_inc(s_["v_turned"], 1)
            gap(3)
            pe.wait_ge(s_["keys_ready"], h + 1)
            for b in range(NB):
                kb = g_["keys"][:, b * P:(b + 1) * P]
                mm = nc.tensor.matmul(bank[7][:, b * P:(b + 1) * P], kb, kb, start=True, stop=True)
            mm.then_inc(s_["kk_done"], 1)
            for b in range(NB):
                mm = nc.tensor.transpose(bank[6][:, b * P:(b + 1) * P], g_["keys"][:, b * P:(b + 1) * P], ident)
            mm.then_inc(s_["k_turned"], 1)
            pe.wait_ge(s_["queries_ready"], h + 1)
            for b in range(NB):
                here = slice(b * P, (b + 1) * P)
                mm = nc.tensor.matmul(bank[2][:, here], g_["keys"][:, here], g_["queries"][:, here], start=True, stop=True)
            mm.then_inc(s_["qk_done"], 1)
            gap(4)
            pe.wait_ge(s_["T_ready"], h + 1)
            for b in range(NB):
                mm = nc.tensor.transpose(bank[3][:, b * P:(b + 1) * P], g_["T"][:, b * P:(b + 1) * P], ident)
            mm.then_inc(s_["T_turned"], 1)
            gap(1)
            pe.wait_ge(s_["row_decay_ready"], h + 1)
            pe.wait_ge(s_["v_beta_ready"], h + 1)
            pe.wait_ge(s_["k_gained_ready"], h + 1)
            for lv in range(LEVELS - 1):
                joins = g_["low_a"] if lv % 2 == 0 else g_["low_b"]
                pe.wait_ge(s_["low_ready"], h * 6 + (lv + 1))
                if lv == 0:
                    pe.wait_ge(s_["U_ready"], h + 1)
                else:
                    pe.wait_ge(s_["UT_ready"], h * 6 + lv)
                for b in range(NB):
                    here = slice(b * P, (b + 1) * P)
                    mm = nc.tensor.matmul(bank[4][:, here], joins[:, here], g_["U"][:, here], start=True, stop=True)
                mm.then_inc(s_["A_done"], 1)
                gap(1)
                pe.wait_ge(s_["A_ready"], h * 6 + (lv + 1))
                for b in range(NB):
                    here = slice(b * P, (b + 1) * P)
                    mm = nc.tensor.matmul(bank[5][:, here], g_["T"][:, here], g_["As"][:, here], start=True, stop=True)
                if lv < LEVELS - 2:
                    for b in range(NB):
                        here = slice(b * P, (b + 1) * P)
                        mm = nc.tensor.matmul(bank[6][:, here], g_["As"][:, here], g_["T"][:, here], start=True, stop=True)
                mm.then_inc(s_["UT_done"], 1)
                gap(2)
            pe.wait_ge(s_["pT_ready"], h + 1)
            pe.wait_ge(s_["q_decayed_ready"], h + 1)
            pe.wait_ge(s_["UT_ready"], h * 6 + 6)
            for b in range(NB):
                here = slice(b * P, (b + 1) * P)
                if b:
                    pe.wait_ge(s_["S_ready"], h * 3 + b)
                    nc.tensor.matmul(bank[7][:, 0:P], g_["keys"][:, here], g_["S"][:, :], start=True, stop=True).then_inc(s_["kS_done"], 1)
                    gap(1)
                    pe.wait_ge(s_["X_ready"], h * 3 + b)
                rhs = g_["X"][:, :] if b else g_["v_beta"][:, here]
                nc.tensor.matmul(bank[2][:, 0:P], g_["U"][:, here], rhs, start=True, stop=True).then_inc(s_["v_done"], 1)
                if b:
                    nc.tensor.matmul(bank[3][:, here], g_["S"][:, :], g_["q_decayed"][:, here], start=True, stop=False)
                gap(1)
                pe.wait_ge(s_["v_ready"], h * 4 + (b + 1))
                if b < NB - 1:
                    nc.tensor.matmul(bank[4][:, 0:P], g_["k_gained"][:, here], g_["v_new"][:, :], start=True, stop=True).then_inc(s_["S_sum_done"], 1)
                mm = nc.tensor.matmul(bank[3][:, here], g_["v_new"][:, :], g_["pT"][:, here], start=b == 0, stop=True)
                if b == NB - 1:
                    mm.then_inc(s_["o_done"], 1)
            gap(40)
            pe.wait_ge(s_["o_squared"], h + 1)
            nc.tensor.matmul(bank[5][:, :], ones, g_["sq_k"][:, :], start=True, stop=True).then_inc(s_["o_summed"], 1)

        def take_row(act, g, j):
            act.wait_ge(unit_done, g * GROUP_TILES + (seg_g.unit0 + j + 1))
            if not (isinstance(g, int) and g == 0):
                act.wait_ge(s_["conv_done"], g * 3 + (j - 2))
            nc.scalar.activation(pre[j][:, 8:HP], bank[(seg_g.tile0 + j) % 2][:, :], ACT.Identity).then_inc(tile_taken, 1)

        def take_z(act, g):
            act.wait_ge(unit_done, g * GROUP_TILES + (seg_g.unit0 + 4))
            nc.scalar.activation(g_["gate_z"][:, :], bank[(seg_g.tile0 + 3) % 2][:, :], ACT.Identity).then_inc(tile_taken, 1)

        def take_q_mem(act, j):
            act.wait_ge(unit_done, seg_g.unit0 + 8 * GROUP_TILES + j + 1)
            nc.scalar.activation(cols(q_mem, j), bank[(seg_g.tile0 + j) % 2][:, :], ACT.Identity).then_inc(tile_taken, 1)

        def silu_row(act, g, j):
            act.wait_ge(s_["conv_done"], g * 3 + (j + 1))
            nc.scalar.activation(acts[j][:, :], acts[j][:, :], ACT.Silu).then_inc(s_["silu_done"], 1)

        def conv_steps(dve, g, j):
            kind = [8, 16, 0][j]
            dve.wait_ge(tile_taken, g * GROUP_TILES + (seg_g.tile0 + j + 1))
            if j == 1 and not (isinstance(g, int) and g == 0):
                dve.wait_ge(s_["v_turned"], g)

            def tap(k):
                if isinstance(g, int):
                    return param("conv4", (g + kind) * CONV_K + k)
                return param("conv4", g * CONV_K + (kind * CONV_K + k))

            for k in reversed(range(CONV_K)):
                src = pre[j][:, 8 - (CONV_K - 1 - k):HP - (CONV_K - 1 - k)]
                if k == CONV_K - 1:
                    ins = nc.vector.tensor_scalar(acts[j][:, :], src, tap(k), None, ALU.mult)
                else:
                    ins = nc.vector.scalar_tensor_tensor(acts[j][:, :], src, tap(k), acts[j][:, :], ALU.mult, ALU.add)
                if k:
                    ins.then_inc(s_["tap_done"], 1)
                    dve.wait_ge(s_["tap_done"], g * 9 + (3 * j + CONV_K - k))
                else:
                    ins.then_inc(s_["conv_done"], 1)
                yield

        s_["tap_done"] = sem("tap_done")

        def head_scalar(act, order, h, g, last):
            def exp_root(dst, src, scale, done):
                order.link(nc.scalar.activation(dst, src, ACT.Ln, bias=eps_col, scale=scale))
                nc.scalar.activation(dst, dst, ACT.Exp, scale=-0.5).then_inc(done, 1)

            act.wait_ge(s_["silu_done"], h * 3 + 3)
            nc.scalar.activation(g_["sq_k"][:, :], acts[0][:, :], ACT.Square).then_inc(s_["keys_squared"], 1)
            nc.scalar.activation(g_["sq_q"][:, :], acts[2][:, :], ACT.Square).then_inc(s_["keys_squared"], 1)
            act.wait_ge(s_["norm_summed"], h * 2 + 1)
            exp_root(g_["r_k"][:, :], bank[2][:, :], 1.0, s_["norms_rooted"])
            act.wait_ge(s_["norm_summed"], h * 2 + 2)
            exp_root(g_["r_q"][:, :], bank[3][:, :], 1.0, s_["norms_rooted"])
            act.wait_ge(s_["gap_ready"], h + 1)
            nc.scalar.activation(g_["D_E"][:, :], g_["D_E"][:, :], ACT.Exp, scale=-1.0).then_inc(s_["decay_ready"], 1)
            nc.scalar.activation(g_["q_decayed"][:, :], bank[4][:, :], ACT.Exp).then_inc(s_["row_decay_ready"], 1)
            act.wait_ge(s_["T_turned"], h + 1)
            nc.scalar.activation(g_["U"][:, :], bank[3][:, :], ACT.Identity).then_inc(s_["U_ready"], 1)
            for lv in range(LEVELS - 1):
                act.wait_ge(s_["A_done"], h * 6 + (lv + 1))
                nc.scalar.activation(g_["As"][:, :], bank[4][:, :], ACT.Identity).then_inc(s_["A_ready"], 1)
                if lv in (0, 3):
                    take_q_mem(act, lv // 3) if last else take_row(act, g, lv // 3)
            for b in range(NB):
                act.wait_ge(s_["v_done"], h * 4 + (b + 1))
                nc.scalar.activation(g_["v_new"][:, :], bank[2][:, 0:P], ACT.Identity).then_inc(s_["v_ready"], 1)
                if b == 0:
                    take_q_mem(act, 2) if last else take_row(act, g, 2)
            act.wait_ge(s_["o_done"], h + 1)
            nc.scalar.activation(g_["sq_k"][:, :], bank[3][:, :], ACT.Square).then_inc(s_["o_squared"], 1)
            nc.scalar.activation(g_["o_rows"][:, :], bank[3][:, :], ACT.Identity).then_inc(s_["o_copied"], 1)
            act.wait_ge(tile_taken, h * GROUP_TILES + (seg_g.tile0 + 4))
            nc.scalar.activation(g_["gate_z"][:, :], g_["gate_z"][:, :], ACT.Silu).then_inc(s_["z_ready"], 1)
            if not last:
                for j in range(3):
                    silu_row(act, g, j)
            act.wait_ge(s_["o_summed"], h + 1)
            exp_root(g_["r_k"][:, :], bank[5][:, :], 1.0 / P, s_["o_rooted"])
            wait_apart(act, s_["head_ready"], h + 1)
            nc.scalar.activation(M_R[:, h] if isinstance(h, int) else cols(MR, h), g_["o_rows"][:, :], ACT.Identity).then_inc(s_["head_high"], 1)
            if last:
                take_q_mem(act, 3)
            else:
                take_z(act, g)

        def head_vector(dve, order, h, g, last):
            V = nc.vector
            convs = [] if last else [conv_steps(dve, g, j) for j in range(3)]

            def conv(j, n):
                if not last:
                    for _ in range(n):
                        next(convs[j], None)

            D_E, m = g_["D_E"][:, :], g_["lower"][:, :]
            V.tensor_tensor(blocks(D_E), over_blocks(tri), over_columns(row4(gcol, h)), ALU.mult).then_inc(s_["gate_rows_ready"], 1)
            dve.wait_ge(s_["norms_rooted"], h * 2 + 1)
            V.tensor_tensor(g_["keys"][:, :], acts[0][:, :], g_["r_k"][:, :], ALU.mult).then_inc(s_["keys_ready"], 1)
            dve.wait_ge(s_["rows_done"], h + 1)
            order.link(V.tensor_tensor(blocks(D_E), blocks(bank[4][:, :]), over_columns(row4(cum, h)), ALU.subtract))
            V.scalar_tensor_tensor(D_E, D_E, -1.0, D_E, ALU.mult, ALU.max).then_inc(s_["gap_ready"], 1)
            dve.wait_ge(s_["norms_rooted"], h * 2 + 2)
            V.scalar_tensor_tensor(g_["queries"][:, :], acts[2][:, :], QS, g_["r_q"][:, :], ALU.mult, ALU.mult).then_inc(s_["queries_ready"], 1)
            dve.wait_ge(s_["v_turned"], h + 1)
            V.tensor_tensor(blocks(g_["v_beta"][:, :]), blocks(bank[5][:, :]), over_columns(row4(beta, h)), ALU.mult).then_inc(s_["v_beta_ready"], 1)
            dve.wait_ge(s_["kk_done"], h + 1)
            dve.wait_ge(s_["decay_ready"], h + 1)
            order.link(V.tensor_tensor(m, bank[7][:, :], D_E, ALU.mult))
            order.link(V.tensor_tensor(blocks(m), blocks(m), over_columns(row4(beta, h)), ALU.mult))
            order.link(V.tensor_tensor(blocks(g_["low_b"][:, :]), blocks(m), over_blocks(const(LEVEL0)), ALU.mult))
            V.tensor_tensor(blocks(g_["T"][:, :]), over_blocks(ident), blocks(g_["low_b"][:, :]), ALU.subtract).then_inc(s_["T_ready"], 1)
            V.tensor_tensor(blocks(g_["low_a"][:, :]), blocks(m), over_blocks(const(LEVEL0 + 1)), ALU.mult).then_inc(s_["low_ready"], 1)
            dve.wait_ge(s_["k_turned"], h + 1)
            V.tensor_tensor(blocks(g_["k_gained"][:, :]), blocks(bank[6][:, :]), over_columns(row4(k_gain, h)), ALU.mult).then_inc(s_["k_gained_ready"], 1)
            dve.wait_ge(s_["T_ready"], h + 1)
            V.tensor_tensor(blocks(g_["low_b"][:, :]), blocks(m), over_blocks(const(LEVEL0 + 2)), ALU.mult).then_inc(s_["low_ready"], 1)
            dve.wait_ge(s_["qk_done"], h + 1)
            order.link(V.tensor_tensor(g_["pT"][:, :], bank[2][:, :], D_E, ALU.mult))
            V.tensor_tensor(blocks(g_["pT"][:, :]), blocks(g_["pT"][:, :]), over_blocks(tri), ALU.mult).then_inc(s_["pT_ready"], 1)
            dve.wait_ge(s_["row_decay_ready"], h + 1)
            dve.wait_ge(s_["queries_ready"], h + 1)
            V.tensor_tensor(g_["q_decayed"][:, :], g_["q_decayed"][:, :], g_["queries"][:, :], ALU.mult).then_inc(s_["q_decayed_ready"], 1)
            dve.wait_ge(s_["U_ready"], h + 1)
            for lv in range(LEVELS - 1):
                dve.wait_ge(s_["UT_done"], h * 6 + (lv + 1))
                if lv < LEVELS - 2:
                    order.mark(V.tensor_tensor(g_["T"][:, :], g_["T"][:, :], bank[6][:, :], ALU.subtract))
                V.tensor_tensor(g_["U"][:, :], g_["U"][:, :], bank[5][:, :], ALU.subtract).then_inc(s_["UT_ready"], 1)
                if lv < LEVELS - 3:
                    low = g_["low_a"] if lv % 2 == 0 else g_["low_b"]
                    V.tensor_tensor(blocks(low[:, :]), blocks(m), over_blocks(const(LEVEL0 + lv + 3)), ALU.mult).then_inc(s_["low_ready"], 1)
                dve.wait_ge(s_["UT_ready"], h * 6 + (lv + 1))
                if lv < LEVELS - 2:
                    order.sync()
                if lv < 4:
                    conv(0, 1)
                else:
                    conv(1, 2)
            for b in range(NB):
                here = slice(b * P, (b + 1) * P)
                if b:
                    dve.wait_ge(s_["kS_done"], h * 3 + b)
                    V.scalar_tensor_tensor(g_["X"][:, :], bank[7][:, 0:P], col1(neg_beta_decay, h, b), g_["v_beta"][:, here],
                                           ALU.mult, ALU.add).then_inc(s_["X_ready"], 1)
                if b < NB - 1:
                    dve.wait_ge(s_["S_sum_done"], h * 3 + (b + 1))
                    if b == 0:
                        V.tensor_copy(g_["S"][:, :], bank[4][:, 0:P]).then_inc(s_["S_ready"], 1)
                    else:
                        V.scalar_tensor_tensor(g_["S"][:, :], g_["S"][:, :], col1(last_gain, h, b), bank[4][:, 0:P],
                                               ALU.mult, ALU.add).then_inc(s_["S_ready"], 1)
                    dve.wait_ge(s_["S_ready"], h * 3 + (b + 1))
                    if b:
                        conv(2, 2)
            o = g_["o_rows"][:, :]
            dve.wait_ge(s_["o_copied"], h + 1)
            dve.wait_ge(s_["o_rooted"], h + 1)
            order.link(V.scalar_tensor_tensor(o, o, param("gdn_out"), g_["r_k"][:, :], ALU.mult, ALU.mult))
            dve.wait_ge(s_["z_ready"], h + 1)
            V.tensor_tensor(o, o, g_["gate_z"][:, :], ALU.mult).then_inc(s_["head_ready"], 1)
            dve.wait_ge(s_["head_high"], h + 1)
            V.tensor_tensor(M_L[:, h] if isinstance(h, int) else cols(ML, h), o,
                            (M_R[:, h] if isinstance(h, int) else cols(MR, h)).bitcast(F32), ALU.subtract).then_inc(s_["head_stored"], 1)
            if last:
                dve.wait_ge(s_["head_stored"], h + 1)

        def gdn_tensor(pe):
            for _ in group_chunks(pe, 0):
                pass
            with pe.Fori(0, HEADS - 1) as h:
                head_tensor(pe, h, h + 1)
            head_tensor(pe, HEADS - 1, HEADS)

        def gdn_scalar(act, order):
            for j in range(3):
                take_row(act, 0, j)
            take_z(act, 0)
            for j in range(3):
                silu_row(act, 0, j)
            with act.Fori(0, HEADS - 1) as h:
                order.enter(h, 3)
                head_scalar(act, order, h, h + 1, False)
                order.leave(HEADS - 1)
            head_scalar(act, order, HEADS - 1, HEADS, True)

        def gdn_vector(dve, order):
            for j in range(3):
                order.link(nc.vector.memset(pre[j][:, 0:8], 0.0))
            for j in range(3):
                for _ in conv_steps(dve, 0, j):
                    pass
            with dve.Fori(0, HEADS - 1) as h:
                order.enter(h, DVE_PER_HEAD)
                head_vector(dve, order, h, h + 1, False)
                order.leave(HEADS - 1)
            head_vector(dve, order, HEADS - 1, HEADS, True)

        DVE_PER_HEAD = 11

        M_SCALE = float(P) ** -0.5
        mq = at("mq", (125 + 24) * KB, SEQ)
        mv = at("mv", (125 + 26) * KB, 2 * P)
        mp = at("mp", (125 + 27) * KB, NB * MEM)
        mpT = [at(f"mpT{i}", (125 + 31 + 2 * i) * KB, SEQ) for i in range(2)]
        mst = at("mst", (125 + 35) * KB, 16)
        mq_ready, mv_ready, m_scored, m_max, m_neg, m_exp, m_inv, m_normed, m_turned, mT_act, mT_dve, m_out, m_high, m_stored = (
            sem(n) for n in ("mq_ready mv_ready m_scored m_max m_neg m_exp m_inv m_normed m_turned mT_act mT_dve "
                             "m_out m_high m_stored").split())

        def mem_head_tensor(pe, h):
            pe.wait_ge(mq_ready, h + 1)
            keys = mem_keys[:, bass.ds(h * MEM, MEM)]
            for b in range(NB):
                mm = nc.tensor.matmul(bank[3 + b // 2][:, b % 2 * MEM:(b % 2 + 1) * MEM], mq[:, b * P:(b + 1) * P],
                                      keys, start=True, stop=True)
                if b % 2:
                    mm.then_inc(m_scored, 1)
            for b in range(NB):
                pe.wait_ge(m_normed, h * NB + (b + 1))
                for c in range(2):
                    mm = nc.tensor.transpose(bank[5 + c][:, b * P:(b + 1) * P], mp[:, b * MEM + c * P:b * MEM + (c + 1) * P], ident)
            mm.then_inc(m_turned, 1)
            pe.wait_ge(mv_ready, h + 1)
            pe.wait_ge(mT_act, h + 1)
            nc.tensor.matmul(bank[7][:, :], mv[:, 0:P], mpT[0][:, :], start=True, stop=False)
            pe.wait_ge(mT_dve, h + 1)
            nc.tensor.matmul(bank[7][:, :], mv[:, P:2 * P], mpT[1][:, :], start=False, stop=True).then_inc(m_out, 1)

        def mem_head_scalar(act, h):
            nc.scalar.activation(mq[:, :], cols(q_mem, h), ACT.Identity).then_inc(mq_ready, 1)
            for b in range(NB):
                act.wait_ge(m_neg, h * 2 + (b // 2 + 1))
                nc.scalar.activation(mp[:, b * MEM:(b + 1) * MEM], bank[3 + b // 2][:, b % 2 * MEM:(b % 2 + 1) * MEM],
                                     ACT.Exp, bias=mst[:, 4 + b:5 + b], scale=M_SCALE,
                                     accum_out=mst[:, 8 + b:9 + b]).then_inc(m_exp, 1)
            act.wait_ge(m_turned, h + 1)
            nc.scalar.activation(mpT[0][:, :], bank[5][:, :], ACT.Identity).then_inc(mT_act, 1)
            wait_apart(act, m_out, h + 1)
            nc.scalar.activation(cols(MR, h + 8), bank[7][:, :], ACT.Identity).then_inc(m_high, 1)

        def mem_head_vector(dve, h):
            V = nc.vector
            V.tensor_copy(mv[:, :].rearrange("p (c d) -> p c d", c=2),
                          mem_values[:, :].rearrange("p (c n) -> p c n", c=2)[:, :, bass.ds(h * P, P)]).then_inc(mv_ready, 1)
            for j in range(2):
                dve.wait_ge(m_scored, h * 2 + (j + 1))
                V.tensor_reduce(mst[:, 2 * j:2 * j + 2], bank[3 + j][:, :].rearrange("p (b m) -> p b m", b=2), AX.X, ALU.max).then_inc(m_max, 1)
                dve.wait_ge(m_max, h * 2 + (j + 1))
                V.tensor_scalar(mst[:, 4 + 2 * j:6 + 2 * j], mst[:, 2 * j:2 * j + 2], -M_SCALE, None, ALU.mult).then_inc(m_neg, 1)
            dve.wait_ge(m_exp, h * NB + NB)
            V.reciprocal(mst[:, 12:16], mst[:, 8:12]).then_inc(m_inv, 1)
            dve.wait_ge(m_inv, h + 1)
            for b in range(NB):
                V.tensor_scalar(mp[:, b * MEM:(b + 1) * MEM], mp[:, b * MEM:(b + 1) * MEM], mst[:, 12 + b:13 + b], None,
                                ALU.mult).then_inc(m_normed, 1)
            dve.wait_ge(m_turned, h + 1)
            V.tensor_copy(mpT[1][:, :], bank[6][:, :]).then_inc(mT_dve, 1)
            dve.wait_ge(m_high, h + 1)
            V.tensor_tensor(cols(ML, h + 8), bank[7][:, :], cols(MR, h + 8).bitcast(F32), ALU.subtract).then_inc(m_stored, 1)

        residual_ready = sem("residual_ready")
        y_normed = sem("y_normed")
        JOIN = {"mix": 0, "ffn": 1}

        def unit_after(seg, n):
            return n * seg.per_tile + (seg.unit0 + seg.per_tile)

        def keep_scalar(act, seg, norm):
            with act.Fori(0, DT // 2) as i:
                for j in range(2):
                    n = i * 2 + j
                    act.wait_ge(unit_done, unit_after(seg, n))
                    src = bank[(seg.tile0 + j) % 2][:, :]
                    square_tile(act, norm, n, j, src)
                    nc.scalar.activation(cols(Y, n), src, ACT.Identity).then_inc(tile_taken, 1)
            root(act, norm)

        def keep_vector(dve, order, norm):
            clear_sum(dve, order, norm)
            with dve.Fori(0, DT // 2) as i:
                for j in range(2):
                    add_squares(dve, norm, i * 2 + j, j)

        def join_scalar(act, norm, nxt, gain):
            base_n = DT * JOIN[norm]
            with act.Fori(0, DT // 2) as i:
                for j in range(2):
                    n = i * 2 + j
                    wait_apart(act, residual_ready, n + (base_n + 1))
                    high_part(act, nxt, n, cols(XR, n), cols(hT, n), param(gain, n))
                    square_tile(act, nxt, n, j, cols(hT, n))
            root(act, nxt)

        def join_vector(dve, order, norm, post_gain, nxt, gain):
            base_n = DT * JOIN[norm]
            dve.wait_ge(norm_ready, NORM[norm] + 1)
            clear_sum(dve, order, nxt)
            with dve.Fori(0, DT // 2) as i:
                for j in range(2):
                    n = i * 2 + j
                    nc.vector.scalar_tensor_tensor(cols(Y, n), cols(Y, n), param(post_gain, n), R[:, :], ALU.mult, ALU.mult).then_inc(y_normed, 1)
                for j in range(2):
                    n = i * 2 + j
                    dve.wait_ge(y_normed, n + (base_n + 1))
                    nc.vector.tensor_tensor(cols(hT, n), cols(hT, n), cols(Y, n), ALU.add).then_inc(residual_ready, 1)
                for j in range(2):
                    n = i * 2 + j
                    low_part(dve, nxt, n, cols(XL, n), cols(hT, n), cols(XR, n), param(gain, n))
                    add_squares(dve, nxt, n, j)

        def join_tensor(pe, nxt):
            total(pe, nxt)

        def stream_scalar(act, seg, nxt, inp, gain):
            with act.Fori(0, DT // 2) as i:
                for j in range(2):
                    n = i * 2 + j
                    wait_apart(act, tile_taken, n + (seg.tile0 + 1))
                    if inp:
                        high_part(act, inp, n, cols(XR, n), cols(hT, n), param(gain, n))
                    square_tile(act, nxt, n, j, cols(hT, n))
            root(act, nxt)

        def stream_vector(dve, order, seg, nxt, inp, gain, bias=None):
            clear_sum(dve, order, nxt)
            with dve.Fori(0, DT // 2) as i:
                for j in range(2):
                    n = i * 2 + j
                    dve.wait_ge(unit_done, unit_after(seg, n))
                    src = bank[(seg.tile0 + j) % 2][:, :]
                    if bias:
                        ins = nc.vector.scalar_tensor_tensor(cols(hT, n), src, param(bias, n), cols(hT, n), ALU.add, ALU.add)
                    else:
                        ins = nc.vector.tensor_tensor(cols(hT, n), src, cols(hT, n), ALU.add)
                    ins.then_inc(tile_taken, 1)
                    if inp:
                        dve.wait_ge(tile_taken, n + (seg.tile0 + 1))
                        low_part(dve, inp, n, cols(XL, n), cols(hT, n), cols(XR, n), param(gain, n))
                    add_squares(dve, nxt, n, j)

        gate_silu, mid_ready, mid_high, mid_low = (sem(n) for n in ("gate_silu", "mid_ready", "mid_high", "mid_low"))
        f_gate = at("f_gate", 169 * KB, SEQ)
        f_up = at("f_up", 171 * KB, SEQ)
        f_mid = at("f_mid", 173 * KB, SEQ)

        def ffn_tensor(pe, which, inp):
            seg, down = SEG[f"in{which}"], SEG[f"down{which}"]
            pe.wait_ge(input_ready, INPUT[inp] + DT)
            tiles(pe, seg, lambda k: X_R[:, k], lambda k: X_L[:, k])
            pe.wait_ge(mid_low, FT * which)
            tiles(pe, down, lambda k: M_R[:, k], lambda k: M_L[:, k])

        def ffn_scalar(act, which):
            seg, done = SEG[f"in{which}"], FT * (which - 1)
            with act.Fori(0, FT) as i:
                act.wait_ge(tile_taken, i * 2 + (seg.tile0 + 1))
                nc.scalar.activation(f_gate[:, :], f_gate[:, :], ACT.Silu).then_inc(gate_silu, 1)
                wait_apart(act, mid_ready, i + (done + 1))
                nc.scalar.activation(cols(MR, i), f_mid[:, :], ACT.Identity).then_inc(mid_high, 1)

        def ffn_vector(dve, which, norm):
            seg, done = SEG[f"in{which}"], FT * (which - 1)
            dve.wait_ge(norm_ready, NORM[norm] + 1)
            with dve.Fori(0, FT) as i:
                dve.wait_ge(unit_done, i * 2 + (seg.unit0 + 1))
                nc.vector.tensor_tensor(f_gate[:, :], bank[seg.tile0 % 2][:, :], R[:, :], ALU.mult).then_inc(tile_taken, 1)
                dve.wait_ge(unit_done, i * 2 + (seg.unit0 + 2))
                nc.vector.tensor_tensor(f_up[:, :], bank[(seg.tile0 + 1) % 2][:, :], R[:, :], ALU.mult).then_inc(tile_taken, 1)
                dve.wait_ge(tile_taken, i * 2 + (seg.tile0 + 2))
                dve.wait_ge(gate_silu, i + (done + 1))
                nc.vector.tensor_tensor(f_mid[:, :], f_gate[:, :], f_up[:, :], ALU.mult).then_inc(mid_ready, 1)
                dve.wait_ge(mid_high, i + (done + 1))
                nc.vector.tensor_tensor(cols(ML, i), f_mid[:, :], cols(MR, i).bitcast(F32), ALU.subtract).then_inc(mid_low, 1)

        c_row = [at(f"c_row{i}", (81 + 0) * KB + i * 2304, SEQ + 64) for i in range(1)]
        c_a = at("c_a", (81 + 6) * KB, SEQ)
        c_b = at("c_b", (81 + 8) * KB, SEQ)
        c_t = at("c_t", (125 + 20) * KB, 2 * SEQ)
        glu_gate, glu_ready, tap_added, mean_added, mean_done, mean_ready, centred, ln_scaled, ln_silu = (
            sem(n) for n in "glu_gate glu_ready tap_added mean_added mean_done mean_ready centred ln_scaled ln_silu".split())

        def conv_tensor(pe):
            seg = SEG["pw1"]
            pe.wait_ge(input_ready, INPUT["h2"] + DT)
            tiles(pe, seg, lambda k: X_R[:, k], lambda k: X_L[:, k])
            pe.wait_ge(mean_added, DT)
            nc.tensor.matmul(bank[3][:, :], ones, ACC[:, :], start=True, stop=True).then_inc(mean_done, 1)
            total(pe, "var")
            pe.wait_ge(input_ready, INPUT["conv"] + DT)
            tiles(pe, SEG["pw2"], lambda k: M_R[:, k], lambda k: M_L[:, k])
            total(pe, "h3")

        def conv_scalar(act):
            seg = SEG["pw1"]
            with act.Fori(0, DT) as i:
                wait_apart(act, tile_taken, i * 2 + (seg.tile0 + 2))
                nc.scalar.activation(c_b[:, :], c_b[:, :], ACT.Sigmoid, bias=param("pw1_b", i)).then_inc(glu_gate, 1)
            with act.Fori(0, DT // 2) as i:
                for j in range(2):
                    act.wait_ge(centred, i * 2 + (j + 1))
                    square_tile(act, "var", i * 2 + j, j, cols(Y, i * 2 + j))
            root(act, "var")
            with act.Fori(0, DT // 2) as i:
                for j in range(2):
                    n = i * 2 + j
                    tmp = c_t[:, j * SEQ:(j + 1) * SEQ]
                    wait_apart(act, ln_scaled, n + 1)
                    nc.scalar.activation(tmp, tmp, ACT.Silu, bias=param("ln_b", n), scale=param("ln_g", n)).then_inc(ln_silu, 1)
                    wait_apart(act, ln_silu, n + 1)
                    nc.scalar.activation(cols(MR, n), tmp, ACT.Identity).then_inc(input_high, 1)
            stream_scalar(act, SEG["pw2"], "h3", "h3", "ffn1")

        def conv_vector(dve, order):
            seg = SEG["pw1"]
            V = nc.vector
            row = c_row[0]
            order.link(V.memset(row[:, 0:PAD + 2], 0.0))
            dve.wait_ge(norm_ready, NORM["h2"] + 1)
            clear_sum_now(dve, order, "h2")
            with dve.Fori(0, DT) as i:
                dve.wait_ge(unit_done, i * 2 + (seg.unit0 + 1))
                V.tensor_tensor(c_a[:, :], bank[seg.tile0 % 2][:, :], R[:, :], ALU.mult).then_inc(tile_taken, 1)
                dve.wait_ge(unit_done, i * 2 + (seg.unit0 + 2))
                V.tensor_tensor(c_b[:, :], bank[(seg.tile0 + 1) % 2][:, :], R[:, :], ALU.mult).then_inc(tile_taken, 1)
                dve.wait_ge(tile_taken, i * 2 + (seg.tile0 + 1))
                dve.wait_ge(glu_gate, i + 1)
                V.scalar_tensor_tensor(row[:, PAD + 2:PAD + 2 + SEQ], c_a[:, :], param("pw1_a", i), c_b[:, :], ALU.add, ALU.mult).then_inc(glu_ready, 1)
                dve.wait_ge(glu_ready, i + 1)
                y = cols(Y, i)
                for k in range(TAPS):
                    src, w = row[:, 2 + k:2 + k + SEQ], param("conv31", i * TAPS + k)
                    if k == 0:
                        V.tensor_scalar(y, src, w, param("dw_b", i), ALU.mult, ALU.add).then_inc(tap_added, 1)
                    else:
                        dve.wait_ge(tap_added, i * TAPS + k)
                        V.scalar_tensor_tensor(y, src, w, y, ALU.mult, ALU.add).then_inc(tap_added, 1)
                dve.wait_ge(tap_added, i * TAPS + TAPS)
                V.tensor_tensor(ACC[:, :], ACC[:, :], y, ALU.add).then_inc(mean_added, 1)
            dve.wait_ge(mean_done, 1)
            V.tensor_scalar(R[:, :], bank[3][:, :], 1.0 / D, None, ALU.mult).then_inc(mean_ready, 1)
            dve.wait_ge(mean_ready, 1)
            order.link(V.memset(ACC[:, :], 0.0))
            with dve.Fori(0, DT // 2) as i:
                for j in range(2):
                    V.tensor_tensor(cols(Y, i * 2 + j), cols(Y, i * 2 + j), R[:, :], ALU.subtract).then_inc(centred, 1)
                for j in range(2):
                    add_squares(dve, "var", i * 2 + j, j)
            dve.wait_ge(norm_ready, NORM["var"] + 1)
            with dve.Fori(0, DT // 2) as i:
                for j in range(2):
                    n = i * 2 + j
                    dve.wait_ge(input_ready, n + (INPUT["conv"] - 1))
                    V.tensor_tensor(c_t[:, j * SEQ:(j + 1) * SEQ], cols(Y, n), R[:, :], ALU.mult).then_inc(ln_scaled, 1)
                for j in range(2):
                    n = i * 2 + j
                    dve.wait_ge(input_high, n + (INPUT["conv"] + 1))
                    V.tensor_tensor(cols(ML, n), c_t[:, j * SEQ:(j + 1) * SEQ], cols(MR, n).bitcast(F32), ALU.subtract).then_inc(input_ready, 1)
            stream_vector(dve, order, SEG["pw2"], "h3", "h3", "ffn1", bias="pw2_b")

        def clear_sum_now(dve, order, norm):
            dve.wait_ge(total_done, NORM[norm] + 1)
            order.link(nc.vector.memset(ACC[:, :], 0.0))

        seg_a = SEG["kvq"]
        q_in_R = [MR[:, k * SEQ:(k + 1) * SEQ] for k in range(DT)]
        q_in_L = [ML[:, k * SEQ:(k + 1) * SEQ] for k in range(DT)]
        phi1 = at("phi1", 169 * KB, 2 * L_CMP * 64)
        behind_r, behind_l = (81 + 32) * KB, (125 + 32) * KB
        k_rows = [at(f"k_rows{i}", behind_r + 2 * i * KB, SEQ) for i in range(2)]
        v_rows = [at(f"v_rows{i}", behind_r + (4 + 2 * i) * KB, SEQ) for i in range(2)]
        v_tok = [at(f"v_tok{i}", behind_r + (8 + 2 * i) * KB, SEQ) for i in range(2)]
        k_cmp = at("k_cmp", behind_l, 32)
        v_cmp = at("v_cmp", behind_l + 128, P, parts=32)
        gates = at("gates", behind_l + 640, NB * 48)
        g_rows = at("g_rows", behind_l + 2 * KB, SEQ)
        c_rows = [at(f"c_rows{i}", behind_l + (4 + 2 * i) * KB, SEQ) for i in range(2)]
        windows = [at(f"windows{i}", (32 + 4 * i) * KB, L_CMP * 32) for i in range(2)]
        hidden = at("hidden", 40 * KB, 64)
        KV_TILES = [c_rows[0], c_rows[1], k_rows[0], k_rows[1], v_rows[0], v_rows[1]]
        phi_loaded, phi2_loaded, windows_ready, hid_done, hid_ready, cmp_done, cmp_ready, vt_turned, vt_ready, gate_sig, gate_turned, gate_ready = (
            sem(n) for n in ("phi_loaded phi2_loaded windows_ready hid_done hid_ready cmp_done cmp_ready "
                             "vt_turned vt_ready gate_sig gate_turned gate_ready").split())
        phi2 = at("phi2", low + 8 * KB + 32, 2 * P)

        def kv_tensor(pe):
            pe.wait_ge(input_ready, INPUT["kv"] + DT)
            xr, xl = (lambda k: X_R[:, k]), (lambda k: X_L[:, k])
            for j in range(6):
                pe.wait_ge(tile_taken, seg_a.tile0 + j - 1)
                products(pe, seg_a, seg_a.unit0 + j, (seg_a.unit0 + j) % 2, 0, bank[(seg_a.tile0 + j) % 2][:, :], xr, xl, True, True)
            pe.wait_ge(input_ready, INPUT["q"] + DT)
            pe.wait_ge(tile_taken, seg_a.tile0 + 5)
            products(pe, seg_a, seg_a.unit0 + 6, (seg_a.unit0 + 6) % 2, 0, bank[(seg_a.tile0 + 6) % 2][:, :],
                     lambda k: q_in_R[k], lambda k: q_in_L[k], True, True)
            for i in range(2):
                pe.wait_ge(tile_taken, seg_a.tile0 + 6)
                for b in range(NB):
                    mm = nc.tensor.transpose(bank[3 + i][:, b * P:(b + 1) * P], v_rows[i][:, b * P:(b + 1) * P], ident)
                mm.then_inc(vt_turned, 1)
            pe.wait_ge(phi_loaded, 16)
            pe.wait_ge(phi2_loaded, 16)
            for i in range(2):
                pe.wait_ge(windows_ready, 2 * i + 2)
                for g in range(2):
                    rows = slice(64 * g, 64 * g + 64)
                    for l in range(L_CMP):
                        w = phi1[rows, (i * L_CMP + l) * 64:(i * L_CMP + l + 1) * 64]
                        mm = nc.tensor.matmul(bank[5 + i][rows, 0:32], w, windows[i][rows, l * 32:(l + 1) * 32],
                                              start=l == 0, stop=l == L_CMP - 1)
                mm.then_inc(hid_done, 1)
            pe.wait_ge(hid_ready, 2)
            nc.tensor.matmul(bank[7][:, 0:32], phi2[:, 0:P], hidden[:, 0:32], start=True, stop=True)
            nc.tensor.matmul(bank[7][0:32, 128:256], hidden[:, 32:64], phi2[:, P:2 * P], start=True, stop=True).then_inc(cmp_done, 1)
            pe.wait_ge(gate_sig, 1)
            for b in range(NB):
                mm = nc.tensor.transpose(bank[2][:, b * 48:(b + 1) * 48], g_rows[0:48, b * P:(b + 1) * P], ident[0:48, 0:48])
            mm.then_inc(gate_turned, 1)

        def kv_scalar(act):
            act.wait_ge(unit_done, seg_a.unit0)
            for n in range(DT):
                high_part(act, "q", n, q_in_R[n], cols(hT, n), param("b_norm", n))
            for i in range(2):
                act.wait_ge(hid_done, i + 1)
                nc.scalar.activation(hidden[:, i * 32:(i + 1) * 32], bank[5 + i][:, 0:32], ACT.Silu).then_inc(hid_ready, 1)
            act.wait_ge(tile_taken, seg_a.tile0 + 7)
            nc.scalar.activation(g_rows[0:48, :], g_rows[0:48, :], ACT.Sigmoid).then_inc(gate_sig, 1)

        def kv_vector(dve, order):
            V = nc.vector
            dve.wait_ge(norm_ready, NORM["h4"] + 1)
            low_parts = iter(range(DT))
            for j in range(6):
                dve.wait_ge(unit_done, seg_a.unit0 + j + 1)
                V.tensor_tensor(KV_TILES[j][:, :], bank[(seg_a.tile0 + j) % 2][:, :], R[:, :], ALU.mult).then_inc(tile_taken, 1)
                for n in (next(low_parts, None), next(low_parts, None)):
                    if n is not None:
                        low_part(dve, "q", n, q_in_L[n], cols(hT, n), q_in_R[n], param("b_norm", n))
            dve.wait_ge(tile_taken, seg_a.tile0 + 6)
            dve.wait_ge(unit_done, seg_a.unit0 + 7)
            V.tensor_tensor(g_rows[0:48, :], bank[(seg_a.tile0 + 6) % 2][0:48, :], R[0:48, :], ALU.mult).then_inc(tile_taken, 1)
            for i in range(2):
                order.link(V.memset(windows[i][:, :], 0.0))
                out_w = windows[i][:, :].rearrange("p (l n) -> p l n", l=L_CMP)
                rows = c_rows[i][:, :].rearrange("p (n s) -> p s n", s=STRIDE)
                for half in range(2):
                    pos = params[:, PARAMS["pos_k" if i == 0 else "pos_v"][0] + half * STRIDE:][:, 0:STRIDE]
                    V.tensor_tensor(out_w[:, half * STRIDE:(half + 1) * STRIDE, 0:N_CMP], rows[:, :, half:half + N_CMP],
                                    over_columns(pos, N_CMP), ALU.add).then_inc(windows_ready, 1)
            for i in range(2):
                dve.wait_ge(vt_turned, i + 1)
                V.tensor_copy(v_tok[i][:, :], bank[3 + i][:, :]).then_inc(vt_ready, 1)
            dve.wait_ge(cmp_done, 1)
            V.tensor_copy(k_cmp[:, :], bank[7][:, 0:32]).then_inc(cmp_ready, 1)
            V.tensor_copy(v_cmp[:, :], bank[7][0:32, 128:256]).then_inc(cmp_ready, 1)
            dve.wait_ge(gate_turned, 1)
            V.tensor_copy(gates[:, :], bank[2][:, 0:NB * 48]).then_inc(gate_ready, 1)
            dve.wait_ge(gate_ready, 1)

        PIECES = [[(3, 0)], [(2, 512), (0, 896)], [(1, 1024)]]
        GROUPS = [(0, 512), (512, 1024), (1024, 1280)]
        WHERE = {b: col for piece in PIECES for b, col in piece}
        PCOLS = 1280
        KEY_SCALE = 0.125
        ITEMS = [(j, g, r) for j in range(2) for g in range(2) for r in range(3)]
        N_ITEMS = len(ITEMS)
        xr0 = 16 * KB
        qT = [at(f"qT{j}", xr0 + 2 * j * KB, SEQ) for j in range(2)]
        alibi = [at(f"alibi{g}", xr0 + (4 + 2 * g) * KB, SEQ) for g in range(2)]
        alibi_c = [at(f"alibi_c{g}", xr0 + 8 * KB + 512 * g, P) for g in range(2)]
        Pc = at("Pc", xr0 + 9 * KB, P)
        PcT = at("PcT", xr0 + 29 * KB, SEQ, parts=32)
        y_tok = at("y_tok", xr0 + 10 * KB, SEQ)
        o_tmp = at("o_tmp", xr0 + 12 * KB, 2 * P)
        stats = at("stats", xr0 + 13 * KB, 32)
        c_max = at("c_max", xr0 + 13 * KB + 128, 8)
        Pr = [at(f"Pr{m}", xr0 + (14 + 5 * m) * KB, PCOLS) for m in range(2)]
        PT = at("PT", xr0 + 24 * KB, PCOLS)
        (alibi_ready, c_scored, scores_read, c_maxed, c_shifted, probs_done, c_summed, c_turned, cT_ready, scored,
         turned, pT_act, pT_dve, pv_done, inverse, weight_ready, weighed, added, y_turned, y_high, y_low) = (
            sem(n) for n in ("alibi_ready c_scored scores_read c_maxed c_shifted probs_done c_summed c_turned cT_ready "
                             "scored turned pT_act pT_dve pv_done inverse weight_ready weighed added y_turned y_high y_low").split())
        q_units, q_tiles = seg_a.unit0 + 7, seg_a.tile0 + 7

        def nth(i, idx):
            return i * N_ITEMS + idx

        def s_nth(i, idx):
            return i * 8 + sum(1 for it in ITEMS[:idx] if it[2])

        def c_nth(i, idx):
            return i * 4 + sum(1 for it in ITEMS[:idx] if not it[2])

        def s_parity(idx):
            return sum(1 for it in ITEMS[:idx] if it[2]) % 2

        def stat(idx, what):
            at0 = 16 * (idx % 2) + 4 * what
            return stats[:, at0:at0 + 4]

        def pair_tensor(pe, i, j):
            pe.wait_ge(tile_taken, i * 2 + (q_tiles + j - 1))
            products(pe, seg_a, i * 2 + (q_units + j), (q_units + j) % 2, 0, bank[(q_tiles + j) % 2][:, :],
                     lambda k: q_in_R[k], lambda k: q_in_L[k], True, True)

        def scores_tensor(pe, i, idx):
            j, g, r = ITEMS[idx]
            rows = slice(64 * g, 64 * g + 64)
            pe.wait_ge(tile_taken, i * 2 + (q_tiles + j + 1))
            pe.wait_ge(scores_read, nth(i, idx) + 1)
            if r == 0:
                for b in range(NB):
                    mm = nc.tensor.matmul(bank[2][:, b * 32:(b + 1) * 32], qT[j][rows, b * P:(b + 1) * P], k_cmp[rows, :],
                                          start=True, stop=True)
                mm.then_inc(c_scored, 1)
                return
            for n, pieces in enumerate(PIECES):
                for b, col in pieces:
                    at0 = col - GROUPS[n][0]
                    mm = nc.tensor.matmul(bank[2 + n][:, at0:at0 + (b + 1) * P], qT[j][rows, b * P:(b + 1) * P],
                                          k_rows[r - 1][rows, 0:(b + 1) * P], start=True, stop=True)
            mm.then_inc(scored, 1)

        def finish_tensor(pe, i, idx):
            j, g, r = ITEMS[idx]
            d = slice(64 * g, 64 * g + 64)
            pe.wait_ge(probs_done, nth(i, idx) + 1)
            if r == 0:
                for b in range(NB):
                    mm = nc.tensor.transpose(bank[5][0:32, b * P:(b + 1) * P], Pc[:, b * 32:(b + 1) * 32], ident)
                mm.then_inc(c_turned, 1)
                pe.wait_ge(cT_ready, c_nth(i, idx) + 1)
                pe.wait_ge(weighed, nth(i, idx) + 1)
                for b in range(NB):
                    mm = nc.tensor.matmul(bank[7][:, b * 64:(b + 1) * 64], PcT[:, b * P:(b + 1) * P], v_cmp[:, d], start=True, stop=True)
                mm.then_inc(pv_done, 1)
                return
            P_ = Pr[s_parity(idx)]
            m = s_nth(i, idx)
            for n, (first, end) in enumerate(GROUPS):
                into = bank[6] if n == 1 else bank[5]
                if n == 2:
                    pe.wait_ge(pT_act, m * 2 + 1)
                for c in range(first, end, P):
                    mm = nc.tensor.transpose(into[:, c - first:c - first + P], P_[:, c:c + P], ident)
                mm.then_inc(turned, 1)
            pe.wait_ge(weighed, nth(i, idx) + 1)
            pe.wait_ge(pT_dve, m + 1)
            for b in (3, 2, 0, 1):
                if b == 1:
                    pe.wait_ge(pT_act, m * 2 + 2)
                for kb in range(b + 1):
                    c = WHERE[b] + kb * P
                    mm = nc.tensor.matmul(bank[7][:, b * 64:(b + 1) * 64], PT[:, c:c + P],
                                          v_tok[r - 1][:, kb * P + 64 * g:kb * P + 64 * g + 64], start=kb == 0, stop=kb == b)
            mm.then_inc(pv_done, 1)

        def turn_y_tensor(pe, i, j):
            pe.wait_ge(added, i * 8 + (4 * j + 4))
            for b in range(NB):
                mm = nc.tensor.transpose(bank[6][:, b * P:(b + 1) * P], y_tok[:, b * P:(b + 1) * P], ident)
            mm.then_inc(y_turned, 1)
            pe.wait_ge(y_low, i * 2 + (j + 1))

        def attend_tensor(pe):
            with pe.Fori(0, NQ // 2) as i:
                pair_tensor(pe, i, 0)
                for n in range(N_ITEMS + 1):
                    if n < N_ITEMS:
                        scores_tensor(pe, i, n)
                    if n:
                        finish_tensor(pe, i, n - 1)
                    if n == 2:
                        pair_tensor(pe, i, 1)
                    if n == 7:
                        turn_y_tensor(pe, i, 0)
                turn_y_tensor(pe, i, 1)

        def alibi_scalar(act, i, idx):
            j, g, _ = ITEMS[idx]
            slope = param("slopes", i * 2 + (8 * g + j))
            nc.scalar.activation(alibi_c[g][:, :], dist_cmp, ACT.Identity, scale=slope).then_inc(alibi_ready, 1)
            nc.scalar.activation(alibi[g][:, :], dist, ACT.Identity, scale=slope).then_inc(alibi_ready, 1)

        def exp_scalar(act, i, idx):
            j, g, r = ITEMS[idx]
            if r == 0:
                act.wait_ge(c_shifted, c_nth(i, idx) + 1)
                nc.scalar.activation(Pc[:, :], Pc[:, :], ACT.Exp, scale=KEY_SCALE).then_inc(probs_done, 1)
                return
            act.wait_ge(scores_read, nth(i, idx) + 2)
            P_ = Pr[s_parity(idx)]
            for n, pieces in enumerate(PIECES):
                for b, col in pieces:
                    here = P_[:, col:col + (b + 1) * P]
                    ins = nc.scalar.activation(here, here, ACT.Exp, bias=stat(idx, 0)[:, b:b + 1], scale=-1.0,
                                               accum_out=stat(idx, 1)[:, b:b + 1])
            ins.then_inc(probs_done, 1)

        def evict_scalar(act, i, idx):
            j, g, r = ITEMS[idx]
            if r == 0:
                act.wait_ge(c_turned, c_nth(i, idx) + 1)
                nc.scalar.activation(PcT[:, :], bank[5][0:32, :], ACT.Identity).then_inc(cT_ready, 1)
                return
            for n in (0, 2):
                act.wait_ge(turned, s_nth(i, idx) * 3 + n + 1)
                first, end = GROUPS[n]
                nc.scalar.activation(PT[:, first:end], bank[5][:, 0:end - first], ACT.Identity).then_inc(pT_act, 1)

        def y_scalar(act, i, j):
            wait_apart(act, y_turned, i * 2 + (j + 1))
            nc.scalar.activation(cols(MR, i * 2 + (8 + j)), bank[6][:, :], ACT.Identity).then_inc(y_high, 1)

        def attend_scalar(act):
            with act.Fori(0, NQ // 2) as i:
                alibi_scalar(act, i, 0)
                for n in range(N_ITEMS + 1):
                    if n < N_ITEMS:
                        if ITEMS[n][2] == 2 and n + 1 < N_ITEMS:
                            alibi_scalar(act, i, n + 1)
                        exp_scalar(act, i, n)
                    if n:
                        evict_scalar(act, i, n - 1)
                    if n == 7:
                        y_scalar(act, i, 0)
                y_scalar(act, i, 1)

        def q_vector(dve, i, j):
            dve.wait_ge(unit_done, i * 2 + (q_units + j + 1))
            nc.vector.tensor_tensor(qT[j][:, :], bank[(q_tiles + j) % 2][:, :], R[:, :], ALU.mult).then_inc(tile_taken, 1)

        def read_vector(dve, i, idx):
            j, g, r = ITEMS[idx]
            V = nc.vector
            if r == 0:
                c = c_nth(i, idx)
                dve.wait_ge(alibi_ready, c * 2 + 2)
                dve.wait_ge(c_scored, c + 1)
                V.tensor_tensor(Pc[:, :], bank[2][:, 0:P], alibi_c[g][:, :], ALU.add).then_inc(scores_read, 1)
                dve.wait_ge(scores_read, nth(i, idx) + 2)
                by_block = Pc[:, :].rearrange("p (b n) -> p b n", b=NB)
                V.tensor_reduce(c_max[:, 0:4], by_block, AX.X, ALU.max).then_inc(c_maxed, 1)
                dve.wait_ge(c_maxed, c + 1)
                V.tensor_tensor(by_block, by_block, over_columns(c_max[:, 0:4], 32), ALU.subtract).then_inc(c_shifted, 1)
                return
            wait_apart(dve, scored, s_nth(i, idx) + 1)
            P_ = Pr[s_parity(idx)]
            for n, pieces in enumerate(PIECES):
                for b, col in pieces:
                    at0 = col - GROUPS[n][0]
                    ins = V.tensor_tensor_reduce(P_[:, col:col + (b + 1) * P], bank[2 + n][:, at0:at0 + (b + 1) * P],
                                                 alibi[g][:, (3 - b) * P:], -KEY_SCALE, 3.0e38, ALU.add, ALU.min,
                                                 stat(idx, 0)[:, b:b + 1])
            ins.then_inc(scores_read, 1)

        def finish_vector(dve, i, idx):
            j, g, r = ITEMS[idx]
            V = nc.vector
            n = nth(i, idx)
            dve.wait_ge(probs_done, n + 1)
            if r == 0:
                c = c_nth(i, idx)
                V.tensor_reduce(stat(idx, 1), Pc[:, :].rearrange("p (b n) -> p b n", b=NB), AX.X, ALU.add).then_inc(c_summed, 1)
                dve.wait_ge(c_summed, c + 1)
            V.reciprocal(stat(idx, 2), stat(idx, 1)).then_inc(inverse, 1)
            dve.wait_ge(inverse, n + 1)
            gate = gates[:, :].rearrange("p (b c) -> p b c", b=NB)[:, :, bass.ds(i * 2 + (16 * r + 8 * g + j), 1)]
            w, inv = stat(idx, 3), stat(idx, 2)
            V.tensor_tensor(w.unsqueeze(2), inv.unsqueeze(2), gate, ALU.mult).then_inc(weight_ready, 1)
            dve.wait_ge(weight_ready, i * 16 + WEIGHTS[idx] + 1)
            if r == 0:
                V.tensor_tensor(w, w, seen, ALU.mult).then_inc(weight_ready, 1)
                dve.wait_ge(weight_ready, i * 16 + WEIGHTS[idx] + 2)
            else:
                m = s_nth(i, idx)
                dve.wait_ge(turned, m * 3 + 2)
                V.tensor_copy(PT[:, 512:1024], bank[6][:, :]).then_inc(pT_dve, 1)
            dve.wait_ge(pv_done, n + 1)
            o = bank[7][:, 0:2 * P].rearrange("p (b d) -> p b d", b=NB)
            y = y_tok[:, :].rearrange("p (b c) -> p b c", b=NB)[:, :, 64 * g:64 * g + 64]
            tmp = o_tmp[:, :].rearrange("p (b d) -> p b d", b=NB)
            if r == 0:
                if j == 1 and g == 0:
                    dve.wait_ge(y_turned, i * 2 + 1)
                V.tensor_tensor(y, o, over_columns(w, 64), ALU.mult).then_inc(weighed, 1)
            else:
                V.tensor_tensor(tmp, o, over_columns(w, 64), ALU.mult).then_inc(weighed, 1)
                dve.wait_ge(weighed, n + 2)
                V.tensor_tensor(y, y, tmp, ALU.add).then_inc(added, 1)
                dve.wait_ge(added, s_nth(i, idx) + 1)

        WEIGHTS = [idx + c for idx, c in zip(range(N_ITEMS), [sum(1 for it in ITEMS[:n] if not it[2]) for n in range(N_ITEMS)])]

        def y_vector(dve, i, j):
            dve.wait_ge(y_high, i * 2 + (j + 1))
            here = i * 2 + (8 + j)
            nc.vector.tensor_tensor(cols(ML, here), bank[6][:, :], cols(MR, here).bitcast(F32), ALU.subtract).then_inc(y_low, 1)

        def attend_vector(dve):
            nc.vector.sem_inc(scores_read, 1)
            nc.vector.sem_inc(weighed, 1)
            with dve.Fori(0, NQ // 2) as i:
                q_vector(dve, i, 0)
                for n in range(N_ITEMS + 1):
                    if n < N_ITEMS:
                        read_vector(dve, i, n)
                    if n:
                        finish_vector(dve, i, n - 1)
                    if n == 3:
                        q_vector(dve, i, 1)
                    if n == 7:
                        y_vector(dve, i, 0)
                y_vector(dve, i, 1)

        final_ready = sem("final_ready")

        def final_vector(dve):
            dve.wait_ge(norm_ready, NORM["h6"] + 1)
            with dve.Fori(0, DT) as n:
                nc.vector.scalar_tensor_tensor(cols(Y, n), cols(hT, n), param("final", n), R[:, :], ALU.mult, ALU.mult).then_inc(final_ready, 1)

        x_again = sem("x_again")
        block = ctx.enter_context(nc.Block())
        names8 = [n for n, _, _ in SEGMENTS]

        @block.sync
        def _(sp):
            sp.dma_start(memT[:, :], t["memT"]).then_inc(mem_loaded, 16)
            sp.dma_start(table[:, :], t["table"]).then_inc(tables_loaded, 16)
            sp.dma_start(params[:, :], t["params"]).then_inc(tables_loaded, 16)
            sp.dma_start(hT[:, :], t["xT"]).then_inc(x_loaded, 16)
            for name in names8:
                stream(sp, SEG[name], lambda unit, row, turn, slot, name=name:
                       load_unit(sp, SEG[name], unit, row + SEG[name].source0, slot))
            with sp.Fori(0, DT) as n:
                sp.wait_ge(final_ready, n + 1)
                sp.dma_start(out[:, bass.ds(n * SEQ, SEQ)], cols(Y, n)).then_inc(stored, 16)
            sp.wait_ge(stored, 16 * DT)

        @block.gpsimd
        def _(pool):
            for name in names8:
                stream(pool, SEG[name], lambda unit, row, turn, slot, name=name:
                       split_unit(pool, SEG[name], unit, turn, slot))

        @block.tensor
        def _(pe):
            mem_tensor(pe)
            gates_tensor(pe)
            gdn_tensor(pe)
            with pe.Fori(0, MEM_HEADS) as h:
                mem_head_tensor(pe, h)
            pe.wait_ge(m_stored, MEM_HEADS)
            tiles(pe, SEG["out1"], lambda k: M_R[:, k], lambda k: M_L[:, k])
            total(pe, "mix")
            total(pe, "h1")
            ffn_tensor(pe, 1, "h1")
            total(pe, "ffn")
            total(pe, "h2")
            conv_tensor(pe)
            ffn_tensor(pe, 2, "h3")
            total(pe, "h4")
            kv_tensor(pe)
            pe.wait_ge(gate_ready, 1)
            attend_tensor(pe)
            tiles(pe, SEG["out2"], lambda k: M_R[:, 8 + k], lambda k: M_L[:, 8 + k])
            total(pe, "h5")
            ffn_tensor(pe, 3, "h5")
            total(pe, "h6")

        @block.scalar
        def _(act):
            order = Order(act, sca)
            start_scalar(act)
            mem_scalar(act)
            gates_scalar(act)
            gdn_scalar(act, order)
            with act.Fori(0, MEM_HEADS) as h:
                mem_head_scalar(act, h)
            act.wait_ge(m_stored, MEM_HEADS)
            act.dma_start(hT[:, :], t["xT"]).then_inc(x_again, 16)
            keep_scalar(act, SEG["out1"], "mix")
            join_scalar(act, "mix", "h1", "pre_ffn")
            ffn_scalar(act, 1)
            keep_scalar(act, SEG["down1"], "ffn")
            join_scalar(act, "ffn", "h2", "a_norm")
            conv_scalar(act)
            ffn_scalar(act, 2)
            act.wait_ge(mid_low, 2 * FT)
            act.dma_start(phi1[:, :], t["phi1"]).then_inc(phi_loaded, 16)
            act.dma_start(phi2[:, :], t["phi2"]).then_inc(phi2_loaded, 16)
            stream_scalar(act, SEG["down2"], "h4", "kv", "kv_norm")
            kv_scalar(act)
            attend_scalar(act)
            stream_scalar(act, SEG["out2"], "h5", "h5", "ffn2")
            ffn_scalar(act, 3)
            stream_scalar(act, SEG["down3"], "h6", None, None)

        @block.vector
        def _(dve):
            order = Order(dve, vec)
            start_vector(dve, order)
            gates_vector(dve, order)
            gdn_vector(dve, order)
            with dve.Fori(0, MEM_HEADS) as h:
                mem_head_vector(dve, h)
            dve.wait_ge(m_stored, MEM_HEADS)
            keep_vector(dve, order, "mix")
            dve.wait_ge(x_again, 16)
            join_vector(dve, order, "mix", "post_mix", "h1", "pre_ffn")
            ffn_vector(dve, 1, "h1")
            keep_vector(dve, order, "ffn")
            join_vector(dve, order, "ffn", "post_ffn", "h2", "a_norm")
            conv_vector(dve, order)
            ffn_vector(dve, 2, "h3")
            stream_vector(dve, order, SEG["down2"], "h4", "kv", "kv_norm")
            kv_vector(dve, order)
            attend_vector(dve)
            stream_vector(dve, order, SEG["out2"], "h5", "h5", "ffn2")
            ffn_vector(dve, 3, "h5")
            stream_vector(dve, order, SEG["down3"], "h6", None, None)
            final_vector(dve)


def tile_units(weight, kt):
    k, n = weight.shape
    pieces = weight.reshape(k // P, P, n // P, P).transpose(2, 0, 1, 3).reshape(-1, kt, P, P)
    return pieces.transpose(0, 2, 1, 3).reshape(-1, P, kt * P)


def columns(vector):
    return vector.reshape(-1, P).T


def kernel(**inputs):
    import concourse.bacc as bacc
    from concourse.bass_utils import run_bass_kernel_spmd as run

    a = {k: np.asarray(v) for k, v in inputs.items()}
    f32 = np.float32

    gdn = a["gdn_w_in"][0]
    qkv, z, heads = gdn[:, :3072], gdn[:, 3072:4096], gdn[:, 4096:4112]
    q_mem_w = gdn[:, 4112:]
    ab = np.zeros((D, P), f32)
    ab[:, 0:8], ab[:, 32:40] = heads[:, 0:8], heads[:, 8:16]
    kv = a["w_mem_kv"][0]
    values = kv[:, 512:].reshape(4, 2, P, 512).transpose(0, 2, 1, 3).reshape(4, P, 1024)
    groups = np.concatenate([w for h in range(HEADS) for w in (
        qkv[:, 1024 + h * P:1024 + (h + 1) * P], qkv[:, 2048 + h * P:2048 + (h + 1) * P],
        qkv[:, h * P:(h + 1) * P], z[:, h * P:(h + 1) * P])] + [q_mem_w], axis=1)

    def pairs(w, n):
        k = w.shape[0]
        return w.reshape(k, 2, n, P).transpose(0, 2, 1, 3).reshape(k, 2 * n * P)

    ffn = [a["w_ffn_in"][0], a["ffn_w_in_2"][0], a["ffn_w_in_2"][1]]
    down = [a["w_ffn_out"][0], a["ffn_w_out_2"][0], a["ffn_w_out_2"][1]]
    w_in = a["b_w_in_2"][0]
    by_pair = w_in[:, :1024].reshape(D, 2, 8, 64).transpose(0, 2, 1, 3).reshape(D, 1024)
    gate_w = np.zeros((D, P), f32)
    gate_w[:, :48] = w_in[:, 1024:]
    w_kv = a["w_kv_2"].reshape(D, 6, P)[:, [0, 1, 2, 4, 3, 5]].reshape(D, 6 * P)
    w_o = a["b_w_out_2"][0].reshape(2, 8, 64, D).transpose(1, 0, 2, 3).reshape(D, D)
    w8 = np.concatenate([tile_units(kv[:, :512], 8), values, tile_units(ab, 8), tile_units(groups, 8),
                         tile_units(pairs(ffn[0], FT), 8), tile_units(pairs(a["a_pw1_w_2"][0], DT), 8),
                         tile_units(a["a_pw2_w_2"][0], 8), tile_units(pairs(ffn[1], FT), 8),
                         tile_units(w_kv, 8), tile_units(gate_w, 8), tile_units(by_pair, 8), tile_units(w_o, 8),
                         tile_units(pairs(ffn[2], FT), 8)])
    w6 = tile_units(a["w_out"][0], 6)
    w11 = np.concatenate([tile_units(w, 11) for w in down])

    def head_rows(v):
        col = np.zeros((P, 1), f32)
        col[:8, 0] = v
        return col

    slopes = np.broadcast_to(-8.0 * 2.0 ** (-8.0 * (np.arange(16) + 1) / 16), (P, 16)).astype(f32)
    conv4 = a["gdn_conv"][0].reshape(CONV_K, 24, P).transpose(2, 1, 0).reshape(P, 24 * CONV_K)
    conv31 = a["a_dw_w_2"][0].reshape(TAPS, DT, P).transpose(2, 1, 0).reshape(P, DT * TAPS)
    both = lambda pos: np.concatenate([pos.T, pos.T], axis=0)
    parts = {
        "mem_norm": columns(a["mem_norm"]), "pre_mix": columns(a["norm_pre_mix"][0]),
        "post_mix": columns(a["norm_post_mix"][0]), "pre_ffn": columns(a["norm_pre_ffn"][0]),
        "post_ffn": columns(a["norm_post_ffn"][0]), "gdn_out": columns(a["gdn_out_norm"][0]),
        "conv4": conv4, "a_norm": columns(a["a_norm_2"][0]), "pw1_a": columns(a["a_pw1_b_2"][0, :D]),
        "pw1_b": columns(a["a_pw1_b_2"][0, D:]), "dw_b": columns(a["a_dw_b_2"][0]),
        "ln_g": columns(a["a_ln_g_2"][0]), "ln_b": columns(a["a_ln_b_2"][0]), "pw2_b": columns(a["a_pw2_b_2"][0]),
        "kv_norm": columns(a["kv_norm_2"]), "b_norm": columns(a["b_norm_2"][0]),
        "ffn1": columns(a["ffn_norm_2"][0]), "ffn2": columns(a["ffn_norm_2"][1]), "final": columns(a["final_norm_2"]),
        "a_log": head_rows(a["gdn_a_log"][0]), "dt_bias": head_rows(a["gdn_dt_bias"][0]), "slopes": slopes,
        "conv31": conv31, "pos_k": both(a["cmp_pos_k_2"]), "pos_v": both(a["cmp_pos_v_2"]),
    }
    params = np.concatenate([parts[n] for n in PARAMS], axis=1)

    def phi_first(w):
        one = w.reshape(L_CMP, 64, 64).transpose(1, 0, 2).reshape(64, L_CMP * 64)
        return np.concatenate([one, one], axis=0)

    phi1 = np.concatenate([phi_first(a["phi_k_w1_2"]), phi_first(a["phi_v_w1_2"])], axis=1)
    phi2 = np.zeros((P, 2 * P), f32)
    for i, w in enumerate((a["phi_k_w2_2"], a["phi_v_w2_2"])):
        for g in range(2):
            phi2[64 * g:64 * g + 64, i * P + 64 * g:i * P + 64 * g + 64] = w
    feature_rows = lambda x: x.T.reshape(DT, P, -1).transpose(1, 0, 2).reshape(P, -1)
    arrays = {"w8": w8, "w6": w6, "w11": w11, "xT": feature_rows(a["x"][0]), "memT": feature_rows(a["mem"][0]),
              "table": constant_tables(), "params": params, "phi1": phi1, "phi2": phi2}
    arrays = {k: np.ascontiguousarray(v) for k, v in arrays.items()}

    nc = bacc.Bacc("TRN2", target_bir_lowering=False, num_devices=1)
    t = {k: nc.dram_tensor(k, v.shape, F32, kind="ExternalInput").ap() for k, v in arrays.items()}
    out = nc.dram_tensor("out", (P, DT * SEQ), F32, kind="ExternalOutput").ap()
    program(nc, t, out)
    r = run(nc, [arrays], core_ids=[0])
    got = np.asarray(r.results[0]["out"]).reshape(P, DT, SEQ).transpose(2, 1, 0).reshape(1, SEQ, D)
    return got
```

```python
from contextlib import ExitStack

import numpy as np

import concourse.bass as bass
from concourse import mybir

F32 = mybir.dt.float32
F32R = mybir.dt.float32r
ALU = mybir.AluOpType
ACT = mybir.ActivationFunctionType
AX = mybir.AxisListType

P = 128
SEQ = 512
D = 1024
DT = D // P
NB = SEQ // P
EPS = 1e-6
HEADS = 8
CONV_K = 4
MEM = 256
MEM_HEADS = 4
DFF = 2816
FT = DFF // P
TAPS = 31
PAD = TAPS - 1
N_CMP = 31
L_CMP = 32
STRIDE = 16
NQ = 8
LEVELS = 7
FAR = 1.0e34

SEGMENTS = [
    ("mem", 8, 9), ("gdn", 8, 36), ("out1", 6, 16), ("in1", 8, 44), ("down1", 11, 16),
    ("pw1", 8, 16), ("pw2", 8, 8), ("in2", 8, 44), ("down2", 11, 16),
    ("kvq", 8, 15), ("out2", 8, 8), ("in3", 8, 44), ("down3", 11, 16),
]
SHARED = [name for name, _, _ in SEGMENTS if name not in ("mem", "gdn", "kvq")]
UNITS_PER_TILE = {8: 1, 6: 2, 11: 2}
SLOT = 11 * P


class Segment:

    def __init__(self, unit0, tile0, source0, kt, units, own0):
        self.unit0, self.tile0, self.source0, self.kt, self.units = unit0, tile0, source0, kt, units
        self.per_tile = UNITS_PER_TILE[kt]
        self.own0 = own0
        self.ahead0 = unit0 - own0


def plan_segments():
    table, unit, tile, own, source = {}, 0, 0, 0, {8: 0, 6: 0, 11: 0}
    for name, kt, units in SEGMENTS:
        table[name] = Segment(unit, tile, source[kt], kt, units, own)
        own += 2 if name in SHARED else units
        unit += units
        source[kt] += units
        tile += units // UNITS_PER_TILE[kt]
    return table


SEG = plan_segments()

PARAMS = {}
_at = 0
for _name, _n in [("mem_norm", DT), ("pre_mix", DT), ("post_mix", DT), ("pre_ffn", DT), ("post_ffn", DT),
                  ("gdn_out", 1), ("conv4", 24 * CONV_K), ("a_norm", DT), ("pw1_a", DT), ("pw1_b", DT),
                  ("dw_b", DT), ("ln_g", DT), ("ln_b", DT), ("pw2_b", DT), ("kv_norm", DT), ("b_norm", DT),
                  ("ffn1", DT), ("ffn2", DT), ("final", DT), ("a_log", 1), ("dt_bias", 1), ("slopes", 16),
                  ("conv31", DT * TAPS), ("pos_k", L_CMP), ("pos_v", L_CMP)]:
    PARAMS[_name] = (_at, _n)
    _at += _n
N_PARAMS = _at

IDENT, ONES, TRI, LEVEL0 = 0, 1, 2, 3
N_CONST = LEVEL0 + LEVELS


def constant_tables():
    p, f = np.arange(P)[:, None], np.arange(P)[None, :]
    square = np.zeros((P, N_CONST, P), np.float32)
    square[:, IDENT] = p == f
    square[:, ONES] = 1.0
    square[:, TRI] = p <= f
    for s in range(LEVELS):
        square[:, LEVEL0 + s] = (p >> (s + 1) == f >> (s + 1)) & (p >> s & 1 == 1) & (f >> s & 1 == 0)
    dist = SEQ - P + p - np.arange(SEQ)[None, :]
    dist = np.where(dist >= 0, dist, FAR).astype(np.float32)
    n = np.arange(32)[None, None, :]
    t = np.arange(NB)[None, :, None] * P + np.arange(P)[:, None, None]
    cmp = t - (n * STRIDE + L_CMP - 1)
    cmp = np.where((cmp >= 0) & (n < N_CMP), cmp, FAR).astype(np.float32)
    seen = np.broadcast_to(t >= L_CMP - 1, (P, NB, 1)).reshape(P, NB).astype(np.float32)
    return np.concatenate([square.reshape(P, -1), dist, cmp.reshape(P, -1), seen], axis=1)


TABLE_COLS = N_CONST * P + SEQ + NB * 32 + NB
TABLE_ROOM = -(-4 * TABLE_COLS // 32) * 32
PARAM_ROOM = -(-4 * N_PARAMS // 32) * 32


def program(nc, t, out, stop=None):
    with ExitStack() as ctx:
        base = nc.sbuf_base
        base = (base + 31) // 32 * 32
        KB = 1024

        def at(name, offset, cols, dt=F32, parts=P):
            return nc.alloc_sbuf_tensor_at(name, [parts, cols], dt, offset=base + offset)

        hT = at("hT", 0, DT * SEQ)
        XR = at("XR", 16 * KB, DT * SEQ, F32R)
        XL = at("XL", 32 * KB, DT * SEQ, F32R)
        raw = at("raw", 48 * KB, 2 * SLOT)
        WR = at("WR", 59 * KB, 2 * SLOT, F32R)
        WL = at("WL", 70 * KB, 2 * SLOT, F32R)
        MR = at("MR", 81 * KB, FT * SEQ, F32R)
        ML = at("ML", 125 * KB, FT * SEQ, F32R)
        Y = at("Y", 169 * KB, DT * SEQ)
        table = at("table", 185 * KB, TABLE_COLS)
        params = at("params", 185 * KB + TABLE_ROOM, N_PARAMS)
        low = 185 * KB + TABLE_ROOM + PARAM_ROOM
        R = at("R", low, SEQ)
        small = at("small", low + 2 * KB, 8)
        ctx.enter_context(nc.sbuf_tensor("fence", [P, (low + 2 * KB + 32 + 64) // 4], F32))

        X_R = XR[:, :].rearrange("p (k n) -> p k n", k=DT)
        X_L = XL[:, :].rearrange("p (k n) -> p k n", k=DT)
        M_R = MR[:, :].rearrange("p (k n) -> p k n", k=FT)
        M_L = ML[:, :].rearrange("p (k n) -> p k n", k=FT)

        def const(i):
            return table[:, i * P:(i + 1) * P]

        ident, ones, tri = const(IDENT), const(ONES), const(TRI)
        dist = table[:, N_CONST * P:N_CONST * P + SEQ]
        dist_cmp = table[:, N_CONST * P + SEQ:N_CONST * P + SEQ + NB * 32]
        seen = table[:, TABLE_COLS - NB:TABLE_COLS]
        eps_col, one_col = small[:, 0:1], small[:, 1:2]

        def param(name, i=0, n=1):
            first = PARAMS[name][0]
            return params[:, first + i:first + i + n] if isinstance(i, int) else params[:, bass.ds(first + i, n)]

        bank = [ctx.enter_context(nc.psum_tensor(f"bank{i}", [P, 512], F32)) for i in range(8)]

        def sem(name):
            return ctx.enter_context(nc.semaphore(name))

        tables_loaded = sem("tables_loaded")
        x_loaded = sem("x_loaded")
        eps_set = sem("eps_set")
        passed = sem("passed")
        weight_loaded = [sem(f"weight_loaded{i}") for i in range(2)]
        high_split = sem("high_split")
        high_ahead = sem("high_ahead")
        weight_split = sem("weight_split")
        unit_done = sem("unit_done")
        tile_taken = sem("tile_taken")
        input_high = sem("input_high")
        input_ready = sem("input_ready")
        squared = sem("squared")
        summed = sem("summed")
        total_done = sem("total_done")
        log_done = sem("log_done")
        norm_ready = sem("norm_ready")
        vec = sem("vec")
        sca = sem("sca")
        stored = sem("stored")

        def wait_apart(engine, semaphore, value):
            engine.wait_ge(semaphore, value)
            engine.sem_inc(passed, 1)

        source = {8: t["w8"], 6: t["w6"], 11: t["w11"]}

        def load_unit(sp, seg, unit, row, slot):
            if not (isinstance(unit, int) and unit < 2):
                sp.wait_ge(weight_split, unit - 1)
            sp.dma_start(raw[:, slot * SLOT:slot * SLOT + seg.kt * P],
                         source[seg.kt][row]).then_inc(weight_loaded[slot], 16)

        def split_unit(pool, seg, unit, turn, slot):
            here = slice(slot * SLOT, slot * SLOT + seg.kt * P)
            pool.wait_ge(weight_loaded[slot], turn * 16 + 16)
            if not (isinstance(unit, int) and unit < 2):
                wait_apart(pool, unit_done, unit - 1)
            nc.gpsimd.tensor_copy(WR[:, here], raw[:, here]).then_inc(high_split, 1)
            pool.wait_ge(high_split, unit + (seg.own0 - seg.unit0 + 1))
            low_unit(seg, slot)

        def split_ahead(act, seg, i, per_turn, first, n=1):
            for c in range(first, first + n):
                if isinstance(i, int) and i * per_turn + c >= seg.units:
                    return
                slot = (seg.unit0 + c) % 2
                here = slice(slot * SLOT, slot * SLOT + seg.kt * P)
                act.wait_ge(weight_loaded[slot], (i * (per_turn // 2) + (seg.unit0 + c) // 2) * 16 + 16)
                act.wait_ge(unit_done, i * per_turn + (seg.unit0 + c - 1))
                nc.scalar.activation(WR[:, here], raw[:, here], ACT.Identity).then_inc(high_ahead, 1)

        def low_unit(seg, slot):
            here = slice(slot * SLOT, slot * SLOT + seg.kt * P)
            nc.gpsimd.tensor_tensor(WL[:, here], raw[:, here], WR[:, here].bitcast(F32),
                                    ALU.subtract).then_inc(weight_split, 1)

        def stream(engine, seg, step):
            pairs = seg.units // 2
            u0 = seg.unit0
            peel = 1 if u0 == 0 else 0
            for j in range(2 * peel):
                step(j, j, 0, j)
            with engine.Fori(peel, pairs) as i:
                for j in range(2):
                    slot = (u0 + j) % 2
                    step(i * 2 + (u0 + j), i * 2 + j, i + (u0 + j) // 2, slot)
            if seg.units % 2:
                j = seg.units - 1
                step(u0 + j, j, (u0 + j) // 2, (u0 + j) % 2)

        def products(pe, seg, unit, slot, k0, into, xr, xl, first, last, ks=None, ready=None):
            n = seg.kt if ks is None else ks[1] - ks[0]
            k_from = 0 if ks is None else ks[0]
            if k_from == 0:
                pe.wait_ge(weight_split, unit + 1)
            for k in range(k_from, k_from + n):
                if ready and ready[1] + k0 + k + 1 > 0:
                    pe.wait_ge(ready[0], ready[1] + k0 + k + 1)
                wr = WR[:, slot * SLOT + k * P:slot * SLOT + (k + 1) * P]
                wl = WL[:, slot * SLOT + k * P:slot * SLOT + (k + 1) * P]
                start, stop = first and k == 0, last and k == seg.kt - 1
                nc.tensor.matmul(into, wr, xr(k0 + k), start=start, stop=False)
                nc.tensor.matmul(into, wr, xl(k0 + k), start=False, stop=False)
                mm = nc.tensor.matmul(into, wl, xr(k0 + k), start=False, stop=stop)
            if k_from + n == seg.kt:
                mm.then_inc(unit_done, 1)

        def tiles(pe, seg, xr, xl, ready, then=None):
            u0, t0, per = seg.unit0, seg.tile0, seg.per_tile

            def turn(i):
                for j in range(2):
                    opening = isinstance(i, int) and j == 0
                    pe.wait_ge(tile_taken, i * 2 + (t0 + j - 1))
                    for part in range(per):
                        c = per * j + part
                        products(pe, seg, i * 2 * per + (u0 + c), (u0 + c) % 2, part * seg.kt, bank[(t0 + j) % 2][:, :],
                                 xr, xl, part == 0, part == per - 1, ready=ready if opening else None)
                        if opening and part == 0 and then:
                            then()

            turn(0)
            with pe.Fori(1, seg.units // (2 * per)) as i:
                turn(i)

        class Order:

            def __init__(self, engine, s):
                self.engine, self.s, self.base, self.k, self.i, self.per = engine, s, 0, 0, None, 0

            def value(self):
                return self.base + self.k if self.i is None else self.i * self.per + (self.base + self.k)

            def mark(self, ins):
                ins.then_inc(self.s, 1)
                self.k += 1

            def sync(self):
                self.engine.wait_ge(self.s, self.value())

            def link(self, ins):
                self.mark(ins)
                self.sync()

            def enter(self, i, per):
                self.base, self.k, self.i, self.per = self.base + self.k, 0, i, per

            def leave(self, turns):
                assert self.k == self.per, f"{self.k} marks in a loop of {self.per}"
                self.base, self.k, self.i = self.base + self.per * turns, 0, None

        def cols(tile, i, n=SEQ):
            return tile[:, i * n:(i + 1) * n] if isinstance(i, int) else tile[:, bass.ds(i * n, n)]

        def blocks(tile):
            return tile.rearrange("p (b n) -> p b n", b=NB)

        def over_blocks(square):
            return square.unsqueeze(1).broadcast_to([P, NB, P])

        def over_columns(scalars, n=P):
            return scalars.unsqueeze(2).broadcast_to([P, scalars.shape[1], n])

        NORM = {n: i for i, n in enumerate(["mem", "x", "mix", "h1", "ffn", "h2", "var", "h3", "h4", "h5", "h6"])}
        INPUT = {n: DT * i for i, n in enumerate(["mem", "x", "h1", "h2", "conv", "h3", "kv", "q", "h5"])}
        SQ = at("SQ", low + 2 * KB + 32, 2 * SEQ)
        ACC = at("ACC", low + 6 * KB + 32, SEQ)

        def square_tile(act, norm, n, parity, src, width=SEQ):
            if not (isinstance(n, int) and NORM[norm] == 0 and n < 2):
                wait_apart(act, summed, n + (DT * NORM[norm] - 1))
            nc.scalar.activation(SQ[:, parity * SEQ:parity * SEQ + width], src, ACT.Square).then_inc(squared, 1)

        def clear_sum(dve, order, norm, width=SEQ):
            if NORM[norm]:
                dve.wait_ge(total_done, NORM[norm])
            order.link(nc.vector.memset(ACC[:, 0:width], 0.0))

        def add_squares(dve, norm, n, parity, width=SEQ):
            dve.wait_ge(squared, n + (DT * NORM[norm] + 1))
            if not (isinstance(n, int) and NORM[norm] == 0 and n == 0):
                dve.wait_ge(summed, n + DT * NORM[norm])
            nc.vector.tensor_tensor(ACC[:, 0:width], ACC[:, 0:width], SQ[:, parity * SEQ:parity * SEQ + width],
                                    ALU.add).then_inc(summed, 1)

        def total(pe, norm, width=SEQ):
            pe.wait_ge(summed, DT * (NORM[norm] + 1))
            nc.tensor.matmul(bank[2][:, 0:width], ones, ACC[:, 0:width], start=True, stop=True).then_inc(total_done, 1)

        def root(act, norm, width=SEQ):
            e = NORM[norm]
            act.wait_ge(total_done, e + 1)
            nc.scalar.activation(R[:, 0:width], bank[2][:, 0:width], ACT.Ln, bias=eps_col, scale=1.0 / D).then_inc(log_done, 1)
            act.wait_ge(log_done, e + 1)
            nc.scalar.activation(R[:, 0:width], R[:, 0:width], ACT.Exp, scale=-0.5).then_inc(norm_ready, 1)

        def high_part(act, name, n, dst, src, gain):
            nc.scalar.activation(dst, src, ACT.Identity, scale=gain).then_inc(input_high, 1)

        def low_part(dve, name, n, dst, src, high, gain):
            dve.wait_ge(input_high, n + (INPUT[name] + 1))
            nc.vector.scalar_tensor_tensor(dst, src, gain, high.bitcast(F32), ALU.mult, ALU.subtract).then_inc(input_ready, 1)

        mem_loaded = sem("mem_loaded")
        scratch = {}

        def place(regions):
            for start, size, names in regions:
                spot = start
                for name, n in names:
                    scratch[name] = at(name, spot, n)
                    spot += (4 * n + 31) // 32 * 32
                assert spot <= start + size, (names[-1][0], spot - start - size)

        HP = SEQ + 8
        place([
            ((81 + 24) * KB, 20 * KB, [("pre0", HP), ("pre1", HP), ("pre2", HP), ("act0", SEQ), ("act1", SEQ),
                                       ("act2", SEQ), ("gate_z", SEQ), ("keys", SEQ), ("queries", SEQ)]),
            ((125 + 24) * KB, 20 * KB, [("D_E", SEQ), ("q_decayed", SEQ), ("v_beta", SEQ), ("k_gained", SEQ),
                                        ("lower", SEQ), ("pT", SEQ), ("low_a", SEQ), ("low_b", SEQ), ("T", SEQ),
                                        ("U", SEQ)]),
            (169 * KB, 16 * KB, [("As", SEQ), ("sq_k", SEQ), ("sq_q", SEQ), ("r_k", SEQ), ("r_q", SEQ),
                                 ("o_rows", SEQ), ("S", P), ("X", P), ("v_new", P), ("scalars", 6 * 32)]),
        ])
        g_ = scratch
        memT = at("memT", 169 * KB, DT * MEM)
        mem_t = at("mem_t", (81 + 24) * KB, 2 * MEM)
        x_t = at("x_t", (81 + 28) * KB, 2 * SEQ)
        q_mem = at("q_mem", 0, MEM_HEADS * SEQ)
        mem_keys = at("mem_keys", 8 * KB, MEM_HEADS * MEM)
        mem_values = at("mem_values", 12 * KB, 2 * SEQ)
        gates40 = at("gates40", (125 + 24) * KB, SEQ, parts=64)
        gate_t = at("gate_t", (125 + 26) * KB, SEQ, parts=64)
        gate_u = at("gate_u", (125 + 28) * KB, SEQ, parts=64)
        scal = g_["scalars"]
        beta, cum, k_gain, last_gain, neg_beta_decay, gcol = (scal[:, 32 * i:32 * i + 32] for i in range(6))

        mem_in_R = MR[:, 0:DT * MEM].rearrange("p (k n) -> p k n", k=DT)
        mem_in_L = ML[:, 0:DT * MEM].rearrange("p (k n) -> p k n", k=DT)

        scaled = sem("scaled")
        gate_part = sem("gate_part")
        gate_act = sem("gate_act")
        gates_turned = sem("gates_turned")
        gates_copied = sem("gates_copied")
        sums_done = sem("sums_done")
        decay_exp = sem("decay_exp")
        gates_ready = sem("gates_ready")

        def split_normed(act, dve, name, n, dst_r, dst_l, tmp):
            if act is not None:
                act.wait_ge(scaled, INPUT[name] + n + 1)
                nc.scalar.activation(dst_r, tmp, ACT.Identity).then_inc(input_high, 1)
            else:
                dve.wait_ge(input_high, INPUT[name] + n + 1)
                nc.vector.tensor_tensor(dst_l, tmp, dst_r.bitcast(F32), ALU.subtract).then_inc(input_ready, 1)

        START = [("mem", memT, MEM, "mem_norm", mem_t, mem_in_R, mem_in_L),
                 ("x", hT, SEQ, "pre_mix", x_t, X_R, X_L)]

        def start_scalar(act):
            act.wait_ge(tables_loaded, 32)
            for e, (name, src, w, gain, tmp, dr, dl) in enumerate(START):
                if e == 0:
                    act.wait_ge(mem_loaded, 16)
                    act.wait_ge(eps_set, 1)
                else:
                    act.wait_ge(x_loaded, 16)
                for n in range(DT):
                    square_tile(act, name, n, n % 2, cols(src, n, w), w)
                root(act, name, w)
                for n in range(DT):
                    split_normed(act, None, name, n, dr[:, n], dl[:, n], cols(tmp, n % 2, w))

        def start_vector(dve, order):
            nc.vector.memset(eps_col, EPS)
            nc.vector.memset(one_col, 1.0).then_inc(eps_set, 1)
            dve.wait_ge(tables_loaded, 32)
            for e, (name, src, w, gain, tmp, dr, dl) in enumerate(START):
                clear_sum(dve, order, name, w)
                for n in range(DT):
                    add_squares(dve, name, n, n % 2, w)
                dve.wait_ge(norm_ready, e + 1)
                for n in range(DT + 1):
                    if n < DT:
                        if n >= 2:
                            dve.wait_ge(input_ready, INPUT[name] + n - 1)
                        nc.vector.scalar_tensor_tensor(cols(tmp, n % 2, w), cols(src, n, w), param(gain, n), R[:, 0:w],
                                                       ALU.mult, ALU.mult).then_inc(scaled, 1)
                    if n:
                        split_normed(None, dve, name, n - 1, dr[:, n - 1], dl[:, n - 1], cols(tmp, (n - 1) % 2, w))

        def mem_tensor(pe):
            pe.wait_ge(tables_loaded, 32)
            total(pe, "mem", MEM)
            pe.wait_ge(input_ready, DT)
            seg = SEG["mem"]
            for j in range(MEM_HEADS):
                if j == 2:
                    total(pe, "x")
                if j >= 2:
                    pe.wait_ge(tile_taken, j - 1)
                products(pe, seg, j, j % 2, 0, bank[j % 2][:, 0:MEM], lambda k: mem_in_R[:, k], lambda k: mem_in_L[:, k], True, True)
            pe.wait_ge(tile_taken, 4)
            for u in range(4):
                pe.wait_ge(weight_split, 5 + u)
                for kk in range(2):
                    k = 2 * u + kk
                    here = slice((u % 2) * SLOT + kk * SEQ, (u % 2) * SLOT + (kk + 1) * SEQ)
                    for b in range(2):
                        tok = slice(b * P, (b + 1) * P)
                        nc.tensor.matmul(bank[b][:, :], mem_in_R[:, k, tok], WR[:, here], start=k == 0, stop=False)
                        nc.tensor.matmul(bank[b][:, :], mem_in_L[:, k, tok], WR[:, here], start=False, stop=False)
                        mm = nc.tensor.matmul(bank[b][:, :], mem_in_R[:, k, tok], WL[:, here], start=False, stop=k == DT - 1)
                mm.then_inc(unit_done, 1)
            pe.wait_ge(input_ready, 2 * DT)
            pe.wait_ge(tile_taken, 8)
            products(pe, seg, 8, 0, 0, bank[0][:, :], lambda k: X_R[:, k], lambda k: X_L[:, k], True, True)

        def mem_scalar(act):
            for j in range(MEM_HEADS):
                act.wait_ge(unit_done, j + 1)
                if j == 0:
                    act.wait_ge(scaled, 2 * DT)
                nc.scalar.activation(cols(mem_keys, j, MEM), bank[j % 2][:, 0:MEM], ACT.Identity).then_inc(tile_taken, 1)
            act.wait_ge(unit_done, 8)
            for j in range(4):
                b, half = j // 2, j % 2
                nc.scalar.activation(mem_values[:, b * SEQ + half * MEM:b * SEQ + (half + 1) * MEM],
                                     bank[b][:, half * MEM:(half + 1) * MEM], ACT.Identity).then_inc(tile_taken, 1)

        def gates_scalar(act):
            act.wait_ge(gate_part, 1)
            nc.scalar.activation(gate_u[0:8, :], gate_u[0:8, :], ACT.Exp, scale=-1.0).then_inc(gate_act, 1)
            nc.scalar.activation(small[0:8, 2:3], param("a_log")[0:8], ACT.Exp).then_inc(gate_act, 1)
            act.wait_ge(gate_act, 1)
            nc.scalar.activation(gate_u[0:8, :], gate_u[0:8, :], ACT.Ln, bias=one_col[0:8]).then_inc(gate_act, 1)
            act.wait_ge(gate_part, 2)
            nc.scalar.activation(gates40[32:40, :], gates40[32:40, :], ACT.Sigmoid).then_inc(gate_act, 1)
            act.wait_ge(gate_part, 5)
            for i, (dst, src) in enumerate([(k_gain, k_gain), (last_gain, last_gain), (neg_beta_decay, cum)]):
                nc.scalar.activation(dst, src, ACT.Exp).then_inc(decay_exp, 1)

        def gates_vector(dve, order):
            order.link(nc.vector.memset(gates40[:, :], 0.0))
            dve.wait_ge(unit_done, 9)
            order.link(nc.vector.tensor_scalar(gate_t[0:8, :], bank[0][0:8, :], param("dt_bias")[0:8], None, ALU.add))
            nc.vector.scalar_tensor_tensor(gate_u[0:8, :], gate_t[0:8, :], -1.0, gate_t[0:8, :], ALU.mult, ALU.max).then_inc(gate_part, 1)
            nc.vector.tensor_copy(gates40[32:40, :], bank[0][32:40, :]).then_inc(gate_part, 1)
            dve.wait_ge(gate_part, 2)
            nc.vector.tensor_scalar(gate_t[0:8, :], gate_t[0:8, :], 0.0, None, ALU.max).then_inc(tile_taken, 1)
            dve.wait_ge(tile_taken, 9)
            dve.wait_ge(gate_act, 3)
            order.link(nc.vector.tensor_tensor(gate_t[0:8, :], gate_t[0:8, :], gate_u[0:8, :], ALU.add))
            nc.vector.tensor_scalar(gates40[0:8, :], gate_t[0:8, :], small[0:8, 2:3], -1.0, ALU.mult, ALU.mult).then_inc(gate_part, 1)
            dve.wait_ge(gates_turned, 1)
            turned = bank[3][:, 0:NB * 40].rearrange("p (b c) -> p c b", b=NB)
            nc.vector.tensor_copy(gcol.rearrange("p (h b) -> p h b", b=NB), turned[:, 0:8]).then_inc(gates_copied, 1)
            nc.vector.tensor_copy(beta.rearrange("p (h b) -> p h b", b=NB), turned[:, 32:40]).then_inc(gates_copied, 1)
            dve.wait_ge(sums_done, 1)
            order.link(nc.vector.tensor_copy(cum, bank[4][:, 0:32]))
            nc.vector.tensor_tensor(k_gain, bank[4][:, 32:64], cum, ALU.subtract).then_inc(gate_part, 1)
            nc.vector.tensor_copy(last_gain, bank[4][:, 32:64]).then_inc(gate_part, 1)
            dve.wait_ge(decay_exp, 3)
            nc.vector.scalar_tensor_tensor(neg_beta_decay, neg_beta_decay, -1.0, beta, ALU.mult, ALU.mult).then_inc(gates_ready, 1)
            dve.wait_ge(gates_ready, 1)

        def gates_tensor(pe):
            pe.wait_ge(gate_part, 3)
            pe.wait_ge(gate_act, 4)
            for b in range(NB):
                mm = nc.tensor.transpose(bank[3][:, b * 40:b * 40 + 40], gates40[0:40, b * P:(b + 1) * P], ident[0:40, 0:40])
            mm.then_inc(gates_turned, 1)
            pe.wait_ge(gates_copied, 2)
            nc.tensor.matmul(bank[4][:, 0:32], tri, gcol, start=True, stop=True)
            nc.tensor.matmul(bank[4][:, 32:64], ones, gcol, start=True, stop=True).then_inc(sums_done, 1)

        names = ("conv_done silu_done keys_squared norm_summed norms_rooted keys_ready queries_ready "
                 "gate_rows_ready rows_done gap_ready decay_ready row_decay_ready q_decayed_ready v_turned "
                 "k_turned v_beta_ready k_gained_ready kk_done qk_done pT_ready T_ready T_turned U_ready "
                 "low_ready A_done A_ready UT_done UT_ready kS_done X_ready v_done v_ready o_done S_sum_done "
                 "S_ready o_squared o_copied o_summed o_rooted z_ready head_ready head_high head_stored").split()
        s_ = {n: sem(n) for n in names}
        GROUP_TILES = 4
        seg_g = SEG["gdn"]
        pre = [g_["pre0"], g_["pre1"], g_["pre2"]]
        acts = [g_["act0"], g_["act1"], g_["act2"]]
        QS = float(P) ** -0.5

        def row4(tile, h):
            return tile[:, bass.ds(h * NB, NB)] if not isinstance(h, int) else tile[:, h * NB:(h + 1) * NB]

        def col1(tile, h, b):
            return tile[:, bass.ds(h * NB + b, 1)] if not isinstance(h, int) else tile[:, h * NB + b:h * NB + b + 1]

        def group_chunks(pe, g):
            for j in range(GROUP_TILES):
                unit = g * GROUP_TILES + (seg_g.unit0 + j)
                pe.wait_ge(tile_taken, g * GROUP_TILES + (seg_g.tile0 + j - 1))
                for k in range(DT):
                    products(pe, seg_g, unit, (seg_g.unit0 + j) % 2, 0, bank[(seg_g.tile0 + j) % 2][:, :],
                             lambda k: X_R[:, k], lambda k: X_L[:, k], True, True, ks=(k, k + 1))
                    yield

        def head_tensor(pe, h, g):
            chunks = group_chunks(pe, g)

            def gap(n):
                for _ in range(n):
                    next(chunks, None)

            pe.wait_ge(s_["keys_squared"], h * 2 + 1)
            nc.tensor.matmul(bank[2][:, :], ones, g_["sq_k"][:, :], start=True, stop=True).then_inc(s_["norm_summed"], 1)
            pe.wait_ge(s_["keys_squared"], h * 2 + 2)
            nc.tensor.matmul(bank[3][:, :], ones, g_["sq_q"][:, :], start=True, stop=True).then_inc(s_["norm_summed"], 1)
            pe.wait_ge(s_["gate_rows_ready"], h + 1)
            nc.tensor.matmul(bank[4][:, :], ones, g_["D_E"][:, :], start=True, stop=True).then_inc(s_["rows_done"], 1)
            pe.wait_ge(s_["silu_done"], h * 3 + 2)
            for b in range(NB):
                mm = nc.tensor.transpose(bank[5][:, b * P:(b + 1) * P], acts[1][:, b * P:(b + 1) * P], ident)
            mm.then_inc(s_["v_turned"], 1)
            gap(3)
            pe.wait_ge(s_["keys_ready"], h + 1)
            for b in range(NB):
                kb = g_["keys"][:, b * P:(b + 1) * P]
                mm = nc.tensor.matmul(bank[7][:, b * P:(b + 1) * P], kb, kb, start=True, stop=True)
            mm.then_inc(s_["kk_done"], 1)
            for b in range(NB):
                mm = nc.tensor.transpose(bank[6][:, b * P:(b + 1) * P], g_["keys"][:, b * P:(b + 1) * P], ident)
            mm.then_inc(s_["k_turned"], 1)
            pe.wait_ge(s_["queries_ready"], h + 1)
            for b in range(NB):
                here = slice(b * P, (b + 1) * P)
                mm = nc.tensor.matmul(bank[2][:, here], g_["keys"][:, here], g_["queries"][:, here], start=True, stop=True)
            mm.then_inc(s_["qk_done"], 1)
            gap(4)
            pe.wait_ge(s_["T_ready"], h + 1)
            for b in range(NB):
                mm = nc.tensor.transpose(bank[3][:, b * P:(b + 1) * P], g_["T"][:, b * P:(b + 1) * P], ident)
            mm.then_inc(s_["T_turned"], 1)
            gap(1)
            pe.wait_ge(s_["row_decay_ready"], h + 1)
            pe.wait_ge(s_["v_beta_ready"], h + 1)
            pe.wait_ge(s_["k_gained_ready"], h + 1)
            for lv in range(LEVELS - 1):
                joins = g_["low_a"] if lv % 2 == 0 else g_["low_b"]
                pe.wait_ge(s_["low_ready"], h * 6 + (lv + 1))
                if lv == 0:
                    pe.wait_ge(s_["U_ready"], h + 1)
                else:
                    pe.wait_ge(s_["UT_ready"], h * 6 + lv)
                for b in range(NB):
                    here = slice(b * P, (b + 1) * P)
                    mm = nc.tensor.matmul(bank[4][:, here], joins[:, here], g_["U"][:, here], start=True, stop=True)
                mm.then_inc(s_["A_done"], 1)
                gap(1)
                pe.wait_ge(s_["A_ready"], h * 6 + (lv + 1))
                for b in range(NB):
                    here = slice(b * P, (b + 1) * P)
                    mm = nc.tensor.matmul(bank[5][:, here], g_["T"][:, here], g_["As"][:, here], start=True, stop=True)
                if lv < LEVELS - 2:
                    for b in range(NB):
                        here = slice(b * P, (b + 1) * P)
                        mm = nc.tensor.matmul(bank[6][:, here], g_["As"][:, here], g_["T"][:, here], start=True, stop=True)
                mm.then_inc(s_["UT_done"], 1)
                gap(2)
            pe.wait_ge(s_["pT_ready"], h + 1)
            pe.wait_ge(s_["q_decayed_ready"], h + 1)
            pe.wait_ge(s_["UT_ready"], h * 6 + 6)
            for b in range(NB):
                here = slice(b * P, (b + 1) * P)
                if b:
                    pe.wait_ge(s_["S_ready"], h * 3 + b)
                    nc.tensor.matmul(bank[7][:, 0:P], g_["keys"][:, here], g_["S"][:, :], start=True, stop=True).then_inc(s_["kS_done"], 1)
                    gap(1)
                    pe.wait_ge(s_["X_ready"], h * 3 + b)
                rhs = g_["X"][:, :] if b else g_["v_beta"][:, here]
                nc.tensor.matmul(bank[2][:, 0:P], g_["U"][:, here], rhs, start=True, stop=True).then_inc(s_["v_done"], 1)
                if b:
                    nc.tensor.matmul(bank[3][:, here], g_["S"][:, :], g_["q_decayed"][:, here], start=True, stop=False)
                gap(1)
                pe.wait_ge(s_["v_ready"], h * 4 + (b + 1))
                if b < NB - 1:
                    nc.tensor.matmul(bank[4][:, 0:P], g_["k_gained"][:, here], g_["v_new"][:, :], start=True, stop=True).then_inc(s_["S_sum_done"], 1)
                mm = nc.tensor.matmul(bank[3][:, here], g_["v_new"][:, :], g_["pT"][:, here], start=b == 0, stop=True)
                if b == NB - 1:
                    mm.then_inc(s_["o_done"], 1)
            gap(40)
            pe.wait_ge(s_["o_squared"], h + 1)
            nc.tensor.matmul(bank[5][:, :], ones, g_["sq_k"][:, :], start=True, stop=True).then_inc(s_["o_summed"], 1)

        def take_row(act, g, j):
            act.wait_ge(unit_done, g * GROUP_TILES + (seg_g.unit0 + j + 1))
            if not (isinstance(g, int) and g == 0):
                act.wait_ge(s_["conv_done"], g * 3 + (j - 2))
            nc.scalar.activation(pre[j][:, 8:HP], bank[(seg_g.tile0 + j) % 2][:, :], ACT.Identity).then_inc(tile_taken, 1)

        def take_z(act, g):
            act.wait_ge(unit_done, g * GROUP_TILES + (seg_g.unit0 + 4))
            nc.scalar.activation(g_["gate_z"][:, :], bank[(seg_g.tile0 + 3) % 2][:, :], ACT.Identity).then_inc(tile_taken, 1)

        def take_q_mem(act, j):
            act.wait_ge(unit_done, seg_g.unit0 + 8 * GROUP_TILES + j + 1)
            nc.scalar.activation(cols(q_mem, j), bank[(seg_g.tile0 + j) % 2][:, :], ACT.Identity).then_inc(tile_taken, 1)

        def silu_row(act, g, j):
            act.wait_ge(s_["conv_done"], g * 3 + (j + 1))
            nc.scalar.activation(acts[j][:, :], acts[j][:, :], ACT.Silu).then_inc(s_["silu_done"], 1)

        def conv_steps(dve, g, j):
            kind = [8, 16, 0][j]
            dve.wait_ge(tile_taken, g * GROUP_TILES + (seg_g.tile0 + j + 1))
            if j == 1 and not (isinstance(g, int) and g == 0):
                dve.wait_ge(s_["v_turned"], g)

            def tap(k):
                if isinstance(g, int):
                    return param("conv4", (g + kind) * CONV_K + k)
                return param("conv4", g * CONV_K + (kind * CONV_K + k))

            for k in reversed(range(CONV_K)):
                src = pre[j][:, 8 - (CONV_K - 1 - k):HP - (CONV_K - 1 - k)]
                if k == CONV_K - 1:
                    ins = nc.vector.tensor_scalar(acts[j][:, :], src, tap(k), None, ALU.mult)
                else:
                    ins = nc.vector.scalar_tensor_tensor(acts[j][:, :], src, tap(k), acts[j][:, :], ALU.mult, ALU.add)
                if k:
                    ins.then_inc(s_["tap_done"], 1)
                    dve.wait_ge(s_["tap_done"], g * 9 + (3 * j + CONV_K - k))
                else:
                    ins.then_inc(s_["conv_done"], 1)
                yield

        s_["tap_done"] = sem("tap_done")

        def head_scalar(act, order, h, g, last):
            def exp_root(dst, src, scale, done):
                order.link(nc.scalar.activation(dst, src, ACT.Ln, bias=eps_col, scale=scale))
                nc.scalar.activation(dst, dst, ACT.Exp, scale=-0.5).then_inc(done, 1)

            act.wait_ge(s_["silu_done"], h * 3 + 3)
            nc.scalar.activation(g_["sq_k"][:, :], acts[0][:, :], ACT.Square).then_inc(s_["keys_squared"], 1)
            nc.scalar.activation(g_["sq_q"][:, :], acts[2][:, :], ACT.Square).then_inc(s_["keys_squared"], 1)
            act.wait_ge(s_["norm_summed"], h * 2 + 1)
            exp_root(g_["r_k"][:, :], bank[2][:, :], 1.0, s_["norms_rooted"])
            act.wait_ge(s_["norm_summed"], h * 2 + 2)
            exp_root(g_["r_q"][:, :], bank[3][:, :], 1.0, s_["norms_rooted"])
            act.wait_ge(s_["gap_ready"], h + 1)
            nc.scalar.activation(g_["D_E"][:, :], g_["D_E"][:, :], ACT.Exp, scale=-1.0).then_inc(s_["decay_ready"], 1)
            nc.scalar.activation(g_["q_decayed"][:, :], bank[4][:, :], ACT.Exp).then_inc(s_["row_decay_ready"], 1)
            act.wait_ge(s_["T_turned"], h + 1)
            nc.scalar.activation(g_["U"][:, :], bank[3][:, :], ACT.Identity).then_inc(s_["U_ready"], 1)
            for lv in range(LEVELS - 1):
                act.wait_ge(s_["A_done"], h * 6 + (lv + 1))
                nc.scalar.activation(g_["As"][:, :], bank[4][:, :], ACT.Identity).then_inc(s_["A_ready"], 1)
                if lv in (0, 3):
                    take_q_mem(act, lv // 3) if last else take_row(act, g, lv // 3)
            for b in range(NB):
                act.wait_ge(s_["v_done"], h * 4 + (b + 1))
                nc.scalar.activation(g_["v_new"][:, :], bank[2][:, 0:P], ACT.Identity).then_inc(s_["v_ready"], 1)
                if b == 0:
                    take_q_mem(act, 2) if last else take_row(act, g, 2)
            act.wait_ge(s_["o_done"], h + 1)
            nc.scalar.activation(g_["sq_k"][:, :], bank[3][:, :], ACT.Square).then_inc(s_["o_squared"], 1)
            nc.scalar.activation(g_["o_rows"][:, :], bank[3][:, :], ACT.Identity).then_inc(s_["o_copied"], 1)
            act.wait_ge(tile_taken, h * GROUP_TILES + (seg_g.tile0 + 4))
            nc.scalar.activation(g_["gate_z"][:, :], g_["gate_z"][:, :], ACT.Silu).then_inc(s_["z_ready"], 1)
            if not last:
                for j in range(3):
                    silu_row(act, g, j)
            act.wait_ge(s_["o_summed"], h + 1)
            exp_root(g_["r_k"][:, :], bank[5][:, :], 1.0 / P, s_["o_rooted"])
            wait_apart(act, s_["head_ready"], h + 1)
            nc.scalar.activation(M_R[:, h] if isinstance(h, int) else cols(MR, h), g_["o_rows"][:, :], ACT.Identity).then_inc(s_["head_high"], 1)
            if last:
                take_q_mem(act, 3)
            else:
                take_z(act, g)

        def head_vector(dve, order, h, g, last):
            V = nc.vector
            convs = [] if last else [conv_steps(dve, g, j) for j in range(3)]

            def conv(j, n):
                if not last:
                    for _ in range(n):
                        next(convs[j], None)

            D_E, m = g_["D_E"][:, :], g_["lower"][:, :]
            V.tensor_tensor(blocks(D_E), over_blocks(tri), over_columns(row4(gcol, h)), ALU.mult).then_inc(s_["gate_rows_ready"], 1)
            dve.wait_ge(s_["norms_rooted"], h * 2 + 1)
            V.tensor_tensor(g_["keys"][:, :], acts[0][:, :], g_["r_k"][:, :], ALU.mult).then_inc(s_["keys_ready"], 1)
            dve.wait_ge(s_["rows_done"], h + 1)
            order.link(V.tensor_tensor(blocks(D_E), blocks(bank[4][:, :]), over_columns(row4(cum, h)), ALU.subtract))
            V.scalar_tensor_tensor(D_E, D_E, -1.0, D_E, ALU.mult, ALU.max).then_inc(s_["gap_ready"], 1)
            dve.wait_ge(s_["norms_rooted"], h * 2 + 2)
            V.scalar_tensor_tensor(g_["queries"][:, :], acts[2][:, :], QS, g_["r_q"][:, :], ALU.mult, ALU.mult).then_inc(s_["queries_ready"], 1)
            dve.wait_ge(s_["v_turned"], h + 1)
            V.tensor_tensor(blocks(g_["v_beta"][:, :]), blocks(bank[5][:, :]), over_columns(row4(beta, h)), ALU.mult).then_inc(s_["v_beta_ready"], 1)
            dve.wait_ge(s_["kk_done"], h + 1)
            dve.wait_ge(s_["decay_ready"], h + 1)
            order.link(V.tensor_tensor(m, bank[7][:, :], D_E, ALU.mult))
            order.link(V.tensor_tensor(blocks(m), blocks(m), over_columns(row4(beta, h)), ALU.mult))
            order.link(V.tensor_tensor(blocks(g_["low_b"][:, :]), blocks(m), over_blocks(const(LEVEL0)), ALU.mult))
            V.tensor_tensor(blocks(g_["T"][:, :]), over_blocks(ident), blocks(g_["low_b"][:, :]), ALU.subtract).then_inc(s_["T_ready"], 1)
            V.tensor_tensor(blocks(g_["low_a"][:, :]), blocks(m), over_blocks(const(LEVEL0 + 1)), ALU.mult).then_inc(s_["low_ready"], 1)
            dve.wait_ge(s_["k_turned"], h + 1)
            V.tensor_tensor(blocks(g_["k_gained"][:, :]), blocks(bank[6][:, :]), over_columns(row4(k_gain, h)), ALU.mult).then_inc(s_["k_gained_ready"], 1)
            dve.wait_ge(s_["T_ready"], h + 1)
            V.tensor_tensor(blocks(g_["low_b"][:, :]), blocks(m), over_blocks(const(LEVEL0 + 2)), ALU.mult).then_inc(s_["low_ready"], 1)
            dve.wait_ge(s_["qk_done"], h + 1)
            order.link(V.tensor_tensor(g_["pT"][:, :], bank[2][:, :], D_E, ALU.mult))
            V.tensor_tensor(blocks(g_["pT"][:, :]), blocks(g_["pT"][:, :]), over_blocks(tri), ALU.mult).then_inc(s_["pT_ready"], 1)
            dve.wait_ge(s_["row_decay_ready"], h + 1)
            dve.wait_ge(s_["queries_ready"], h + 1)
            V.tensor_tensor(g_["q_decayed"][:, :], g_["q_decayed"][:, :], g_["queries"][:, :], ALU.mult).then_inc(s_["q_decayed_ready"], 1)
            dve.wait_ge(s_["U_ready"], h + 1)
            for lv in range(LEVELS - 1):
                dve.wait_ge(s_["UT_done"], h * 6 + (lv + 1))
                if lv < LEVELS - 2:
                    order.mark(V.tensor_tensor(g_["T"][:, :], g_["T"][:, :], bank[6][:, :], ALU.subtract))
                V.tensor_tensor(g_["U"][:, :], g_["U"][:, :], bank[5][:, :], ALU.subtract).then_inc(s_["UT_ready"], 1)
                if lv < LEVELS - 3:
                    low = g_["low_a"] if lv % 2 == 0 else g_["low_b"]
                    V.tensor_tensor(blocks(low[:, :]), blocks(m), over_blocks(const(LEVEL0 + lv + 3)), ALU.mult).then_inc(s_["low_ready"], 1)
                dve.wait_ge(s_["UT_ready"], h * 6 + (lv + 1))
                if lv < LEVELS - 2:
                    order.sync()
                if lv < 4:
                    conv(0, 1)
                else:
                    conv(1, 2)
            for b in range(NB):
                here = slice(b * P, (b + 1) * P)
                if b:
                    dve.wait_ge(s_["kS_done"], h * 3 + b)
                    V.scalar_tensor_tensor(g_["X"][:, :], bank[7][:, 0:P], col1(neg_beta_decay, h, b), g_["v_beta"][:, here],
                                           ALU.mult, ALU.add).then_inc(s_["X_ready"], 1)
                if b < NB - 1:
                    dve.wait_ge(s_["S_sum_done"], h * 3 + (b + 1))
                    if b == 0:
                        V.tensor_copy(g_["S"][:, :], bank[4][:, 0:P]).then_inc(s_["S_ready"], 1)
                    else:
                        V.scalar_tensor_tensor(g_["S"][:, :], g_["S"][:, :], col1(last_gain, h, b), bank[4][:, 0:P],
                                               ALU.mult, ALU.add).then_inc(s_["S_ready"], 1)
                    dve.wait_ge(s_["S_ready"], h * 3 + (b + 1))
                    if b:
                        conv(2, 2)
            o = g_["o_rows"][:, :]
            dve.wait_ge(s_["o_copied"], h + 1)
            dve.wait_ge(s_["o_rooted"], h + 1)
            order.link(V.scalar_tensor_tensor(o, o, param("gdn_out"), g_["r_k"][:, :], ALU.mult, ALU.mult))
            dve.wait_ge(s_["z_ready"], h + 1)
            V.tensor_tensor(o, o, g_["gate_z"][:, :], ALU.mult).then_inc(s_["head_ready"], 1)
            dve.wait_ge(s_["head_high"], h + 1)
            V.tensor_tensor(M_L[:, h] if isinstance(h, int) else cols(ML, h), o,
                            (M_R[:, h] if isinstance(h, int) else cols(MR, h)).bitcast(F32), ALU.subtract).then_inc(s_["head_stored"], 1)
            if last:
                dve.wait_ge(s_["head_stored"], h + 1)

        def gdn_tensor(pe):
            for _ in group_chunks(pe, 0):
                pass
            with pe.Fori(0, HEADS - 1) as h:
                head_tensor(pe, h, h + 1)
            head_tensor(pe, HEADS - 1, HEADS)

        def gdn_scalar(act, order):
            for j in range(3):
                take_row(act, 0, j)
            take_z(act, 0)
            for j in range(3):
                silu_row(act, 0, j)
            with act.Fori(0, HEADS - 1) as h:
                order.enter(h, 3)
                head_scalar(act, order, h, h + 1, False)
                order.leave(HEADS - 1)
            head_scalar(act, order, HEADS - 1, HEADS, True)

        def gdn_vector(dve, order):
            for j in range(3):
                order.link(nc.vector.memset(pre[j][:, 0:8], 0.0))
            for j in range(3):
                for _ in conv_steps(dve, 0, j):
                    pass
            with dve.Fori(0, HEADS - 1) as h:
                order.enter(h, DVE_PER_HEAD)
                head_vector(dve, order, h, h + 1, False)
                order.leave(HEADS - 1)
            head_vector(dve, order, HEADS - 1, HEADS, True)

        DVE_PER_HEAD = 11

        M_SCALE = float(P) ** -0.5
        mq = at("mq", (125 + 24) * KB, SEQ)
        mv = at("mv", (125 + 26) * KB, 2 * P)
        mp = at("mp", (125 + 27) * KB, NB * MEM)
        mpT = [at(f"mpT{i}", (125 + 31 + 2 * i) * KB, SEQ) for i in range(2)]
        mst = at("mst", (125 + 35) * KB, 16)
        mq_ready, mv_ready, m_scored, m_max, m_neg, m_exp, m_inv, m_normed, m_turned, mT_act, mT_dve, m_out, m_high, m_stored = (
            sem(n) for n in ("mq_ready mv_ready m_scored m_max m_neg m_exp m_inv m_normed m_turned mT_act mT_dve "
                             "m_out m_high m_stored").split())

        def mem_head_tensor(pe, h):
            pe.wait_ge(mq_ready, h + 1)
            keys = mem_keys[:, bass.ds(h * MEM, MEM)]
            for b in range(NB):
                mm = nc.tensor.matmul(bank[3 + b // 2][:, b % 2 * MEM:(b % 2 + 1) * MEM], mq[:, b * P:(b + 1) * P],
                                      keys, start=True, stop=True)
                if b % 2:
                    mm.then_inc(m_scored, 1)
            for b in range(NB):
                pe.wait_ge(m_normed, h * NB + (b + 1))
                for c in range(2):
                    mm = nc.tensor.transpose(bank[5 + c][:, b * P:(b + 1) * P], mp[:, b * MEM + c * P:b * MEM + (c + 1) * P], ident)
            mm.then_inc(m_turned, 1)
            pe.wait_ge(mv_ready, h + 1)
            pe.wait_ge(mT_act, h + 1)
            nc.tensor.matmul(bank[7][:, :], mv[:, 0:P], mpT[0][:, :], start=True, stop=False)
            pe.wait_ge(mT_dve, h + 1)
            nc.tensor.matmul(bank[7][:, :], mv[:, P:2 * P], mpT[1][:, :], start=False, stop=True).then_inc(m_out, 1)

        def mem_head_scalar(act, h):
            nc.scalar.activation(mq[:, :], cols(q_mem, h), ACT.Identity).then_inc(mq_ready, 1)
            for b in range(NB):
                act.wait_ge(m_neg, h * 2 + (b // 2 + 1))
                nc.scalar.activation(mp[:, b * MEM:(b + 1) * MEM], bank[3 + b // 2][:, b % 2 * MEM:(b % 2 + 1) * MEM],
                                     ACT.Exp, bias=mst[:, 4 + b:5 + b], scale=M_SCALE,
                                     accum_out=mst[:, 8 + b:9 + b]).then_inc(m_exp, 1)
            act.wait_ge(m_turned, h + 1)
            nc.scalar.activation(mpT[0][:, :], bank[5][:, :], ACT.Identity).then_inc(mT_act, 1)
            wait_apart(act, m_out, h + 1)
            nc.scalar.activation(cols(MR, h + 8), bank[7][:, :], ACT.Identity).then_inc(m_high, 1)

        def mem_head_vector(dve, h):
            V = nc.vector
            V.tensor_copy(mv[:, :].rearrange("p (c d) -> p c d", c=2),
                          mem_values[:, :].rearrange("p (c n) -> p c n", c=2)[:, :, bass.ds(h * P, P)]).then_inc(mv_ready, 1)
            for j in range(2):
                dve.wait_ge(m_scored, h * 2 + (j + 1))
                V.tensor_reduce(mst[:, 2 * j:2 * j + 2], bank[3 + j][:, :].rearrange("p (b m) -> p b m", b=2), AX.X, ALU.max).then_inc(m_max, 1)
                dve.wait_ge(m_max, h * 2 + (j + 1))
                V.tensor_scalar(mst[:, 4 + 2 * j:6 + 2 * j], mst[:, 2 * j:2 * j + 2], -M_SCALE, None, ALU.mult).then_inc(m_neg, 1)
            dve.wait_ge(m_exp, h * NB + NB)
            V.reciprocal(mst[:, 12:16], mst[:, 8:12]).then_inc(m_inv, 1)
            dve.wait_ge(m_inv, h + 1)
            for b in range(NB):
                V.tensor_scalar(mp[:, b * MEM:(b + 1) * MEM], mp[:, b * MEM:(b + 1) * MEM], mst[:, 12 + b:13 + b], None,
                                ALU.mult).then_inc(m_normed, 1)
            dve.wait_ge(m_turned, h + 1)
            V.tensor_copy(mpT[1][:, :], bank[6][:, :]).then_inc(mT_dve, 1)
            dve.wait_ge(m_high, h + 1)
            V.tensor_tensor(cols(ML, h + 8), bank[7][:, :], cols(MR, h + 8).bitcast(F32), ALU.subtract).then_inc(m_stored, 1)

        residual_ready = sem("residual_ready")
        y_normed = sem("y_normed")
        JOIN = {"mix": 0, "ffn": 1}

        def unit_after(seg, n):
            return n * seg.per_tile + (seg.unit0 + seg.per_tile)

        def keep_scalar(act, seg, norm):
            def turn(i):
                for j in range(2):
                    n = i * 2 + j
                    split_ahead(act, seg, i, 4, 2 * j + 2, 2)
                    act.wait_ge(unit_done, unit_after(seg, n))
                    src = bank[(seg.tile0 + j) % 2][:, :]
                    square_tile(act, norm, n, j, src)
                    nc.scalar.activation(cols(Y, n), src, ACT.Identity).then_inc(tile_taken, 1)

            with act.Fori(0, DT // 2 - 1) as i:
                turn(i)
            turn(DT // 2 - 1)
            root(act, norm)

        def keep_vector(dve, order, norm):
            clear_sum(dve, order, norm)
            with dve.Fori(0, DT // 2) as i:
                for j in range(2):
                    add_squares(dve, norm, i * 2 + j, j)

        def join_scalar(act, norm, nxt, gain):
            base_n = DT * JOIN[norm]
            with act.Fori(0, DT // 2) as i:
                for j in range(2):
                    n = i * 2 + j
                    wait_apart(act, residual_ready, n + (base_n + 1))
                    high_part(act, nxt, n, cols(XR, n), cols(hT, n), param(gain, n))
                    square_tile(act, nxt, n, j, cols(hT, n))
            root(act, nxt)

        def join_vector(dve, order, norm, post_gain, nxt, gain):
            base_n = DT * JOIN[norm]
            dve.wait_ge(norm_ready, NORM[norm] + 1)
            clear_sum(dve, order, nxt)
            with dve.Fori(0, DT // 2) as i:
                for j in range(2):
                    n = i * 2 + j
                    nc.vector.scalar_tensor_tensor(cols(Y, n), cols(Y, n), param(post_gain, n), R[:, :], ALU.mult, ALU.mult).then_inc(y_normed, 1)
                for j in range(2):
                    n = i * 2 + j
                    dve.wait_ge(y_normed, n + (base_n + 1))
                    nc.vector.tensor_tensor(cols(hT, n), cols(hT, n), cols(Y, n), ALU.add).then_inc(residual_ready, 1)
                for j in range(2):
                    n = i * 2 + j
                    low_part(dve, nxt, n, cols(XL, n), cols(hT, n), cols(XR, n), param(gain, n))
                    add_squares(dve, nxt, n, j)

        def stream_scalar(act, seg, nxt, inp, gain):
            def turn(i):
                for j in range(2):
                    n = i * 2 + j
                    split_ahead(act, seg, i, 2 * seg.per_tile, seg.per_tile * j + 2, seg.per_tile)
                    wait_apart(act, tile_taken, n + (seg.tile0 + 1))
                    if inp:
                        high_part(act, inp, n, cols(XR, n), cols(hT, n), param(gain, n))
                    square_tile(act, nxt, n, j, cols(hT, n))

            with act.Fori(0, DT // 2 - 1) as i:
                turn(i)
            turn(DT // 2 - 1)
            root(act, nxt)

        def stream_vector(dve, order, seg, nxt, inp, gain, bias=None):
            clear_sum(dve, order, nxt)
            with dve.Fori(0, DT // 2) as i:
                for j in range(2):
                    n = i * 2 + j
                    dve.wait_ge(unit_done, unit_after(seg, n))
                    src = bank[(seg.tile0 + j) % 2][:, :]
                    if bias:
                        ins = nc.vector.scalar_tensor_tensor(cols(hT, n), src, param(bias, n), cols(hT, n), ALU.add, ALU.add)
                    else:
                        ins = nc.vector.tensor_tensor(cols(hT, n), src, cols(hT, n), ALU.add)
                    ins.then_inc(tile_taken, 1)
                    if inp:
                        dve.wait_ge(tile_taken, n + (seg.tile0 + 1))
                        low_part(dve, inp, n, cols(XL, n), cols(hT, n), cols(XR, n), param(gain, n))
                    add_squares(dve, nxt, n, j)

        gate_silu, mid_ready, mid_high, mid_low = (sem(n) for n in ("gate_silu", "mid_ready", "mid_high", "mid_low"))
        f_gate = at("f_gate", 169 * KB, SEQ)
        f_up = at("f_up", 171 * KB, SEQ)
        f_mid = at("f_mid", 173 * KB, SEQ)

        def ffn_tensor(pe, which, inp):
            seg, down = SEG[f"in{which}"], SEG[f"down{which}"]
            tiles(pe, seg, lambda k: X_R[:, k], lambda k: X_L[:, k], (input_ready, INPUT[inp]), lambda: total(pe, inp))
            tiles(pe, down, lambda k: M_R[:, k], lambda k: M_L[:, k], (mid_low, FT * (which - 1)))

        def ffn_scalar(act, which):
            seg, done = SEG[f"in{which}"], FT * (which - 1)
            def turn(i):
                split_ahead(act, seg, i, 2, 2)
                act.wait_ge(tile_taken, i * 2 + (seg.tile0 + 1))
                nc.scalar.activation(f_gate[:, :], f_gate[:, :], ACT.Silu).then_inc(gate_silu, 1)
                split_ahead(act, seg, i, 2, 3)
                wait_apart(act, mid_ready, i + (done + 1))
                nc.scalar.activation(cols(MR, i), f_mid[:, :], ACT.Identity).then_inc(mid_high, 1)

            with act.Fori(0, FT - 1) as i:
                turn(i)
            turn(FT - 1)

        def ffn_vector(dve, which, norm):
            seg, done = SEG[f"in{which}"], FT * (which - 1)
            dve.wait_ge(norm_ready, NORM[norm] + 1)
            with dve.Fori(0, FT) as i:
                dve.wait_ge(unit_done, i * 2 + (seg.unit0 + 1))
                nc.vector.tensor_tensor(f_gate[:, :], bank[seg.tile0 % 2][:, :], R[:, :], ALU.mult).then_inc(tile_taken, 1)
                dve.wait_ge(unit_done, i * 2 + (seg.unit0 + 2))
                nc.vector.tensor_tensor(f_up[:, :], bank[(seg.tile0 + 1) % 2][:, :], R[:, :], ALU.mult).then_inc(tile_taken, 1)
                dve.wait_ge(tile_taken, i * 2 + (seg.tile0 + 2))
                dve.wait_ge(gate_silu, i + (done + 1))
                nc.vector.tensor_tensor(f_mid[:, :], f_gate[:, :], f_up[:, :], ALU.mult).then_inc(mid_ready, 1)
                dve.wait_ge(mid_high, i + (done + 1))
                nc.vector.tensor_tensor(cols(ML, i), f_mid[:, :], cols(MR, i).bitcast(F32), ALU.subtract).then_inc(mid_low, 1)

        PE_TAPS = 9
        ROW = SEQ + PAD + 2
        c_row = [at(f"c_row{j}", (81 + 3 * j) * KB, ROW) for j in range(2)]
        c_a = at("c_a", (81 + 6) * KB, SEQ)
        c_b = at("c_b", (81 + 8) * KB, SEQ)
        c_odd = at("c_odd", (81 + 10) * KB, SEQ)
        c_t = at("c_t", (125 + 20) * KB, 2 * SEQ)
        diag = [at(f"diag{j}", (125 + 24 + 5 * j) * KB, PE_TAPS * P) for j in range(2)]
        glu_gate, glu_ready, diag_ready, taps_done, tap_added, odd_added, taps_joined, mean_added, mean_done, mean_ready, centred, ln_scaled, ln_silu = (
            sem(n) for n in "glu_gate glu_ready diag_ready taps_done tap_added odd_added taps_joined mean_added mean_done mean_ready centred ln_scaled ln_silu".split())

        def conv_tensor(pe):
            seg = SEG["pw1"]
            u0, t0 = seg.unit0, seg.tile0

            def taps(n, j):
                pe.wait_ge(diag_ready, n + 1)
                pe.wait_ge(glu_ready, n + 1)
                for k in range(PE_TAPS):
                    mm = nc.tensor.matmul(bank[4 + j][:, :], diag[j][:, k * P:(k + 1) * P], c_row[j][:, 2 + k:2 + k + SEQ],
                                          start=k == 0, stop=k == PE_TAPS - 1)
                mm.then_inc(taps_done, 1)

            def turn(i):
                for j in range(2):
                    for half in range(2):
                        c = 2 * j + half
                        opening = isinstance(i, int) and c == 0
                        pe.wait_ge(tile_taken, i * 4 + (t0 + c - 1))
                        products(pe, seg, i * 4 + (u0 + c), (u0 + c) % 2, 0, bank[(t0 + c) % 2][:, :],
                                 lambda k: X_R[:, k], lambda k: X_L[:, k], True, True,
                                 ready=(input_ready, INPUT["h2"]) if opening else None)
                        if opening:
                            total(pe, "h2")
                    if not isinstance(i, int) or j:
                        taps(i * 2 + (j - 1), 1 - j)

            turn(0)
            with pe.Fori(1, DT // 2) as i:
                turn(i)
            taps(DT - 1, 1)
            pe.wait_ge(mean_added, DT)
            nc.tensor.matmul(bank[3][:, :], ones, ACC[:, :], start=True, stop=True).then_inc(mean_done, 1)
            total(pe, "var")
            tiles(pe, SEG["pw2"], lambda k: M_R[:, k], lambda k: M_L[:, k], (input_ready, INPUT["conv"]))

        def conv_scalar(act):
            seg = SEG["pw1"]
            def turn(i):
                for j in range(2):
                    n = i * 2 + j
                    split_ahead(act, seg, i, 4, 2 * j + 2, 2)
                    wait_apart(act, tile_taken, i * 4 + (seg.tile0 + 2 * j + 1))
                    nc.scalar.activation(c_b[:, :], c_b[:, :], ACT.Sigmoid, bias=param("pw1_b", n)).then_inc(glu_gate, 1)
                    if not isinstance(i, int) or i:
                        wait_apart(act, taps_done, n - 1)
                    for k in range(PE_TAPS):
                        ins = nc.scalar.activation(diag[j][:, k * P:(k + 1) * P], ident, ACT.Identity, scale=param("conv31", n * TAPS + k))
                    ins.then_inc(diag_ready, 1)

            turn(0)
            with act.Fori(1, DT // 2 - 1) as i:
                turn(i)
            turn(DT // 2 - 1)
            with act.Fori(0, DT // 2) as i:
                for j in range(2):
                    act.wait_ge(centred, i * 2 + (j + 1))
                    square_tile(act, "var", i * 2 + j, j, cols(Y, i * 2 + j))
            root(act, "var")
            with act.Fori(0, DT // 2) as i:
                for j in range(2):
                    n = i * 2 + j
                    tmp = c_t[:, j * SEQ:(j + 1) * SEQ]
                    wait_apart(act, ln_scaled, n + 1)
                    nc.scalar.activation(tmp, tmp, ACT.Silu, bias=param("ln_b", n), scale=param("ln_g", n)).then_inc(ln_silu, 1)
                    wait_apart(act, ln_silu, n + 1)
                    nc.scalar.activation(cols(MR, n), tmp, ACT.Identity).then_inc(input_high, 1)
            stream_scalar(act, SEG["pw2"], "h3", "h3", "ffn1")

        def conv_vector(dve, order):
            seg = SEG["pw1"]
            V = nc.vector
            for j in range(2):
                order.link(V.memset(c_row[j][:, 0:PAD + 2], 0.0))
            dve.wait_ge(norm_ready, NORM["h2"] + 1)
            clear_sum_now(dve, order, "h2")
            N = TAPS - PE_TAPS

            def turn(i):
                for j in range(2):
                    n = i * 2 + j
                    row, y = c_row[j], cols(Y, n)
                    dve.wait_ge(unit_done, n * 2 + (seg.unit0 + 1))
                    V.tensor_tensor(c_b[:, :], bank[seg.tile0 % 2][:, :], R[:, :], ALU.mult).then_inc(tile_taken, 1)
                    dve.wait_ge(unit_done, n * 2 + (seg.unit0 + 2))
                    V.tensor_tensor(c_a[:, :], bank[(seg.tile0 + 1) % 2][:, :], R[:, :], ALU.mult).then_inc(tile_taken, 1)
                    dve.wait_ge(tile_taken, n * 2 + (seg.tile0 + 2))
                    dve.wait_ge(glu_gate, n + 1)
                    V.scalar_tensor_tensor(row[:, PAD + 2:ROW], c_a[:, :], param("pw1_a", n), c_b[:, :], ALU.add, ALU.mult).then_inc(glu_ready, 1)
                    dve.wait_ge(glu_ready, n + 1)
                    for m in range(N):
                        k = PE_TAPS + m
                        src, w, into = row[:, 2 + k:2 + k + SEQ], param("conv31", n * TAPS + k), (y, c_odd[:, :])[m % 2]
                        if m >= 2:
                            dve.wait_ge(tap_added, n * N + (m - 1))
                        if m == 0:
                            ins = V.tensor_scalar(into, src, w, param("dw_b", n), ALU.mult, ALU.add)
                        elif m == 1:
                            ins = V.tensor_scalar(into, src, w, None, ALU.mult)
                        else:
                            ins = V.scalar_tensor_tensor(into, src, w, into, ALU.mult, ALU.add)
                        ins.then_inc(tap_added, 1)
                    dve.wait_ge(tap_added, n * N + N)
                    V.tensor_tensor(y, y, c_odd[:, :], ALU.add).then_inc(odd_added, 1)
                    dve.wait_ge(taps_done, n + 1)
                    dve.wait_ge(odd_added, n + 1)
                    V.tensor_tensor(y, y, bank[4 + j][:, :], ALU.add).then_inc(taps_joined, 1)
                    dve.wait_ge(taps_joined, n + 1)
                    V.tensor_tensor(ACC[:, :], ACC[:, :], y, ALU.add).then_inc(mean_added, 1)
                    dve.wait_ge(mean_added, n + 1)

            with dve.Fori(0, DT // 2) as i:
                turn(i)
            dve.wait_ge(mean_done, 1)
            V.tensor_scalar(R[:, :], bank[3][:, :], 1.0 / D, None, ALU.mult).then_inc(mean_ready, 1)
            dve.wait_ge(mean_ready, 1)
            order.link(V.memset(ACC[:, :], 0.0))
            with dve.Fori(0, DT // 2) as i:
                for j in range(2):
                    V.tensor_tensor(cols(Y, i * 2 + j), cols(Y, i * 2 + j), R[:, :], ALU.subtract).then_inc(centred, 1)
                for j in range(2):
                    add_squares(dve, "var", i * 2 + j, j)
            dve.wait_ge(norm_ready, NORM["var"] + 1)
            with dve.Fori(0, DT // 2) as i:
                for j in range(2):
                    n = i * 2 + j
                    dve.wait_ge(input_ready, n + (INPUT["conv"] - 1))
                    V.tensor_tensor(c_t[:, j * SEQ:(j + 1) * SEQ], cols(Y, n), R[:, :], ALU.mult).then_inc(ln_scaled, 1)
                for j in range(2):
                    n = i * 2 + j
                    dve.wait_ge(input_high, n + (INPUT["conv"] + 1))
                    V.tensor_tensor(cols(ML, n), c_t[:, j * SEQ:(j + 1) * SEQ], cols(MR, n).bitcast(F32), ALU.subtract).then_inc(input_ready, 1)
            stream_vector(dve, order, SEG["pw2"], "h3", "h3", "ffn1", bias="pw2_b")

        def clear_sum_now(dve, order, norm):
            dve.wait_ge(total_done, NORM[norm] + 1)
            order.link(nc.vector.memset(ACC[:, :], 0.0))

        seg_a = SEG["kvq"]
        q_in_R = [MR[:, k * SEQ:(k + 1) * SEQ] for k in range(DT)]
        q_in_L = [ML[:, k * SEQ:(k + 1) * SEQ] for k in range(DT)]
        phi1 = at("phi1", 169 * KB, 2 * L_CMP * 64)
        behind_r, behind_l = (81 + 32) * KB, (125 + 32) * KB
        k_rows = [at(f"k_rows{i}", behind_r + 2 * i * KB, SEQ) for i in range(2)]
        v_rows = [at(f"v_rows{i}", behind_r + (4 + 2 * i) * KB, SEQ) for i in range(2)]
        v_tok = [at(f"v_tok{i}", behind_r + (8 + 2 * i) * KB, SEQ) for i in range(2)]
        k_cmp = at("k_cmp", behind_l, 32)
        v_cmp = at("v_cmp", behind_l + 128, P, parts=32)
        gates = at("gates", behind_l + 640, NB * 48)
        g_rows = at("g_rows", behind_l + 2 * KB, SEQ)
        c_rows = [at(f"c_rows{i}", behind_l + (4 + 2 * i) * KB, SEQ) for i in range(2)]
        windows = [at(f"windows{i}", (32 + 4 * i) * KB, L_CMP * 32) for i in range(2)]
        hidden = at("hidden", 40 * KB, 64)
        KV_TILES = [c_rows[0], c_rows[1], k_rows[0], k_rows[1], v_rows[0], v_rows[1]]
        phi_loaded, phi2_loaded, windows_ready, hid_done, hid_ready, cmp_done, cmp_ready, vt_turned, vt_ready, gate_sig, gate_turned, gate_ready = (
            sem(n) for n in ("phi_loaded phi2_loaded windows_ready hid_done hid_ready cmp_done cmp_ready "
                             "vt_turned vt_ready gate_sig gate_turned gate_ready").split())
        phi2 = at("phi2", low + 8 * KB + 32, 2 * P)

        def kv_tensor(pe):
            xr, xl = (lambda k: X_R[:, k]), (lambda k: X_L[:, k])
            for j in range(6):
                pe.wait_ge(tile_taken, seg_a.tile0 + j - 1)
                products(pe, seg_a, seg_a.unit0 + j, (seg_a.unit0 + j) % 2, 0, bank[(seg_a.tile0 + j) % 2][:, :], xr, xl, True, True,
                         ready=None if j else (input_ready, INPUT["kv"]))
                if j == 0:
                    total(pe, "h4")
            pe.wait_ge(input_ready, INPUT["q"] + DT)
            pe.wait_ge(tile_taken, seg_a.tile0 + 5)
            products(pe, seg_a, seg_a.unit0 + 6, (seg_a.unit0 + 6) % 2, 0, bank[(seg_a.tile0 + 6) % 2][:, :],
                     lambda k: q_in_R[k], lambda k: q_in_L[k], True, True)
            for i in range(2):
                pe.wait_ge(tile_taken, seg_a.tile0 + 6)
                for b in range(NB):
                    mm = nc.tensor.transpose(bank[3 + i][:, b * P:(b + 1) * P], v_rows[i][:, b * P:(b + 1) * P], ident)
                mm.then_inc(vt_turned, 1)
            pe.wait_ge(phi_loaded, 16)
            pe.wait_ge(phi2_loaded, 16)
            for i in range(2):
                pe.wait_ge(windows_ready, 2 * i + 2)
                for g in range(2):
                    rows = slice(64 * g, 64 * g + 64)
                    for l in range(L_CMP):
                        w = phi1[rows, (i * L_CMP + l) * 64:(i * L_CMP + l + 1) * 64]
                        mm = nc.tensor.matmul(bank[5 + i][rows, 0:32], w, windows[i][rows, l * 32:(l + 1) * 32],
                                              start=l == 0, stop=l == L_CMP - 1)
                mm.then_inc(hid_done, 1)
            pe.wait_ge(hid_ready, 2)
            nc.tensor.matmul(bank[7][:, 0:32], phi2[:, 0:P], hidden[:, 0:32], start=True, stop=True)
            nc.tensor.matmul(bank[7][0:32, 128:256], hidden[:, 32:64], phi2[:, P:2 * P], start=True, stop=True).then_inc(cmp_done, 1)
            pe.wait_ge(gate_sig, 1)
            for b in range(NB):
                mm = nc.tensor.transpose(bank[2][:, b * 48:(b + 1) * 48], g_rows[0:48, b * P:(b + 1) * P], ident[0:48, 0:48])
            mm.then_inc(gate_turned, 1)

        def kv_scalar(act):
            act.wait_ge(unit_done, seg_a.unit0)
            for n in range(DT):
                high_part(act, "q", n, q_in_R[n], cols(hT, n), param("b_norm", n))
            for i in range(2):
                act.wait_ge(hid_done, i + 1)
                nc.scalar.activation(hidden[:, i * 32:(i + 1) * 32], bank[5 + i][:, 0:32], ACT.Silu).then_inc(hid_ready, 1)
            act.wait_ge(tile_taken, seg_a.tile0 + 7)
            nc.scalar.activation(g_rows[0:48, :], g_rows[0:48, :], ACT.Sigmoid).then_inc(gate_sig, 1)

        def kv_vector(dve, order):
            V = nc.vector
            dve.wait_ge(norm_ready, NORM["h4"] + 1)
            low_parts = iter(range(DT))
            for j in range(6):
                dve.wait_ge(unit_done, seg_a.unit0 + j + 1)
                V.tensor_tensor(KV_TILES[j][:, :], bank[(seg_a.tile0 + j) % 2][:, :], R[:, :], ALU.mult).then_inc(tile_taken, 1)
                for n in (next(low_parts, None), next(low_parts, None)):
                    if n is not None:
                        low_part(dve, "q", n, q_in_L[n], cols(hT, n), q_in_R[n], param("b_norm", n))
            dve.wait_ge(tile_taken, seg_a.tile0 + 6)
            dve.wait_ge(unit_done, seg_a.unit0 + 7)
            V.tensor_tensor(g_rows[0:48, :], bank[(seg_a.tile0 + 6) % 2][0:48, :], R[0:48, :], ALU.mult).then_inc(tile_taken, 1)
            for i in range(2):
                order.link(V.memset(windows[i][:, :], 0.0))
                out_w = windows[i][:, :].rearrange("p (l n) -> p l n", l=L_CMP)
                rows = c_rows[i][:, :].rearrange("p (n s) -> p s n", s=STRIDE)
                for half in range(2):
                    pos = params[:, PARAMS["pos_k" if i == 0 else "pos_v"][0] + half * STRIDE:][:, 0:STRIDE]
                    V.tensor_tensor(out_w[:, half * STRIDE:(half + 1) * STRIDE, 0:N_CMP], rows[:, :, half:half + N_CMP],
                                    over_columns(pos, N_CMP), ALU.add).then_inc(windows_ready, 1)
            for i in range(2):
                dve.wait_ge(vt_turned, i + 1)
                V.tensor_copy(v_tok[i][:, :], bank[3 + i][:, :]).then_inc(vt_ready, 1)
            dve.wait_ge(cmp_done, 1)
            V.tensor_copy(k_cmp[:, :], bank[7][:, 0:32]).then_inc(cmp_ready, 1)
            V.tensor_copy(v_cmp[:, :], bank[7][0:32, 128:256]).then_inc(cmp_ready, 1)
            dve.wait_ge(gate_turned, 1)
            V.tensor_copy(gates[:, :], bank[2][:, 0:NB * 48]).then_inc(gate_ready, 1)
            dve.wait_ge(gate_ready, 1)

        PIECES = [[(3, 0)], [(2, 512), (0, 896)], [(1, 1024)]]
        GROUPS = [(0, 512), (512, 1024), (1024, 1280)]
        WHERE = {b: col for piece in PIECES for b, col in piece}
        PCOLS = 1280
        KEY_SCALE = 0.125
        ITEMS = [(j, g, r) for j in range(2) for g in range(2) for r in range(3)]
        N_ITEMS = len(ITEMS)
        xr0 = 16 * KB
        qT = [at(f"qT{j}", xr0 + 2 * j * KB, SEQ) for j in range(2)]
        alibi = [at(f"alibi{g}", xr0 + (4 + 2 * g) * KB, SEQ) for g in range(2)]
        alibi_c = [at(f"alibi_c{g}", xr0 + 8 * KB + 512 * g, P) for g in range(2)]
        Pc = at("Pc", xr0 + 9 * KB, P)
        PcT = at("PcT", xr0 + 29 * KB, SEQ, parts=32)
        y_tok = at("y_tok", xr0 + 10 * KB, SEQ)
        o_tmp = at("o_tmp", xr0 + 12 * KB, 2 * P)
        stats = at("stats", xr0 + 13 * KB, 48)
        c_max = at("c_max", xr0 + 13 * KB + 192, 8)
        Pr = [at(f"Pr{m}", xr0 + (14 + 5 * m) * KB, PCOLS) for m in range(2)]
        PT = at("PT", xr0 + 24 * KB, PCOLS)
        (alibi_ready, c_scored, scores_read, c_maxed, c_shifted, probs_done, c_summed, c_turned, cT_ready, scored,
         turned, pT_act, pT_dve, pv_done, inverse, weight_ready, weighed, added, y_turned, y_high, y_low) = (
            sem(n) for n in ("alibi_ready c_scored scores_read c_maxed c_shifted probs_done c_summed c_turned cT_ready "
                             "scored turned pT_act pT_dve pv_done inverse weight_ready weighed added y_turned y_high y_low").split())
        q_units, q_tiles = seg_a.unit0 + 7, seg_a.tile0 + 7
        TURNS = NQ // 2

        def item(idx):
            return ITEMS[idx % N_ITEMS]

        def nth(i, idx):
            return i * N_ITEMS + idx

        def s_nth(i, idx):
            return i * 8 + (idx // N_ITEMS * 8 + sum(1 for it in ITEMS[:idx % N_ITEMS] if it[2]))

        def c_nth(i, idx):
            return i * 4 + (idx // N_ITEMS * 4 + sum(1 for it in ITEMS[:idx % N_ITEMS] if not it[2]))

        def s_parity(idx):
            return sum(1 for it in ITEMS[:idx % N_ITEMS] if it[2]) % 2

        def stat(idx, what):
            at0 = 16 * (idx % 3) + 4 * what
            return stats[:, at0:at0 + 4]

        def exists(i, idx):
            return idx < N_ITEMS or not (isinstance(i, int) and i == TURNS - 1)

        def pair_tensor(pe, i, j):
            pe.wait_ge(tile_taken, i * 2 + (q_tiles + j))
            products(pe, seg_a, i * 2 + (q_units + j), (q_units + j) % 2, 0, bank[0][:, :],
                     lambda k: q_in_R[k], lambda k: q_in_L[k], True, True)

        def scores_tensor(pe, i, idx):
            j, g, r = item(idx)
            rows = slice(64 * g, 64 * g + 64)
            pe.wait_ge(tile_taken, i * 2 + (q_tiles + idx // N_ITEMS * 2 + j + 1))
            pe.wait_ge(scores_read, nth(i, idx) + 1)
            if r == 0:
                for b in range(NB):
                    mm = nc.tensor.matmul(bank[2][:, b * 32:(b + 1) * 32], qT[j][rows, b * P:(b + 1) * P], k_cmp[rows, :],
                                          start=True, stop=True)
                mm.then_inc(c_scored, 1)
                return
            for n, pieces in enumerate(PIECES):
                for b, col in pieces:
                    at0 = col - GROUPS[n][0]
                    mm = nc.tensor.matmul(bank[2 + n][:, at0:at0 + (b + 1) * P], qT[j][rows, b * P:(b + 1) * P],
                                          k_rows[r - 1][rows, 0:(b + 1) * P], start=True, stop=True)
                mm.then_inc(scored, 1)

        def turn_probs_tensor(pe, i, idx):
            pe.wait_ge(probs_done, nth(i, idx) + 1)
            if item(idx)[2] == 0:
                for b in range(NB):
                    mm = nc.tensor.transpose(bank[5][0:32, b * P:(b + 1) * P], Pc[:, b * 32:(b + 1) * 32], ident)
                mm.then_inc(c_turned, 1)
                return
            P_ = Pr[s_parity(idx)]
            for (first, end), into in zip(GROUPS, (bank[5], bank[6], bank[1])):
                for c in range(first, end, P):
                    mm = nc.tensor.transpose(into[:, c - first:c - first + P], P_[:, c:c + P], ident)
                mm.then_inc(turned, 1)

        def weigh_tensor(pe, i, idx):
            j, g, r = item(idx)
            d = slice(64 * g, 64 * g + 64)
            pe.wait_ge(weighed, nth(i, idx) + 1)
            if r == 0:
                pe.wait_ge(cT_ready, c_nth(i, idx) + 1)
                for b in range(NB):
                    mm = nc.tensor.matmul(bank[7][:, b * 64:(b + 1) * 64], PcT[:, b * P:(b + 1) * P], v_cmp[:, d], start=True, stop=True)
            else:
                m = s_nth(i, idx)
                pe.wait_ge(pT_dve, m + 1)
                pe.wait_ge(pT_act, m * 2 + 2)
                for b in range(NB):
                    for kb in range(b + 1):
                        c = WHERE[b] + kb * P
                        mm = nc.tensor.matmul(bank[7][:, b * 64:(b + 1) * 64], PT[:, c:c + P],
                                              v_tok[r - 1][:, kb * P + 64 * g:kb * P + 64 * g + 64], start=kb == 0, stop=kb == b)
            mm.then_inc(pv_done, 1)

        def turn_y_tensor(pe, i, j):
            pe.wait_ge(added, i * 8 + (4 * j + 4))
            for b in range(NB):
                mm = nc.tensor.transpose(bank[0][:, b * P:(b + 1) * P], y_tok[:, b * P:(b + 1) * P], ident)
            mm.then_inc(y_turned, 1)

        def attend_tensor(pe):
            pair_tensor(pe, 0, 0)
            scores_tensor(pe, 0, 0)
            scores_tensor(pe, 0, 1)

            def turn(i):
                for n in range(N_ITEMS):
                    turn_probs_tensor(pe, i, n)
                    if exists(i, n + 2):
                        scores_tensor(pe, i, n + 2)
                    if n == 6:
                        turn_y_tensor(pe, i, 0)
                    weigh_tensor(pe, i, n)
                    if n == 1:
                        pair_tensor(pe, i, 1)
                    if n == 7 and exists(i, N_ITEMS):
                        pe.wait_ge(y_low, i * 2 + 1)
                        pair_tensor(pe, i + 1, 0)
                turn_y_tensor(pe, i, 1)

            with pe.Fori(0, TURNS - 1) as i:
                turn(i)
            turn(TURNS - 1)
            pe.wait_ge(y_low, NQ)

        def alibi_scalar(act, i, idx):
            j, g, _ = item(idx)
            slope = param("slopes", i * 2 + (8 * g + idx // N_ITEMS * 2 + j))
            nc.scalar.activation(alibi_c[g][:, :], dist_cmp, ACT.Identity, scale=slope).then_inc(alibi_ready, 1)
            nc.scalar.activation(alibi[g][:, :], dist, ACT.Identity, scale=slope).then_inc(alibi_ready, 1)

        def exp_scalar(act, i, idx):
            if item(idx)[2] == 2 and exists(i, idx + 1):
                alibi_scalar(act, i, idx + 1)
            if item(idx)[2] == 0:
                act.wait_ge(c_shifted, c_nth(i, idx) + 1)
                nc.scalar.activation(Pc[:, :], Pc[:, :], ACT.Exp, scale=KEY_SCALE).then_inc(probs_done, 1)
                return
            act.wait_ge(scores_read, nth(i, idx) + 2)
            P_ = Pr[s_parity(idx)]
            for n, pieces in enumerate(PIECES):
                for b, col in pieces:
                    here = P_[:, col:col + (b + 1) * P]
                    ins = nc.scalar.activation(here, here, ACT.Exp, bias=stat(idx, 0)[:, b:b + 1], scale=-1.0,
                                               accum_out=stat(idx, 1)[:, b:b + 1])
            ins.then_inc(probs_done, 1)

        def evict_scalar(act, i, idx):
            if item(idx)[2] == 0:
                act.wait_ge(c_turned, c_nth(i, idx) + 1)
                nc.scalar.activation(PcT[:, :], bank[5][0:32, :], ACT.Identity).then_inc(cT_ready, 1)
                return
            for n, source_bank in ((0, bank[5]), (2, bank[1])):
                act.wait_ge(turned, s_nth(i, idx) * 3 + (n + 1))
                first, end = GROUPS[n]
                nc.scalar.activation(PT[:, first:end], source_bank[:, 0:end - first], ACT.Identity).then_inc(pT_act, 1)

        def y_scalar(act, i, j):
            wait_apart(act, y_turned, i * 2 + (j + 1))
            nc.scalar.activation(cols(MR, i * 2 + (8 + j)), bank[0][:, :], ACT.Identity).then_inc(y_high, 1)

        def attend_scalar(act):
            alibi_scalar(act, 0, 0)
            exp_scalar(act, 0, 0)
            exp_scalar(act, 0, 1)

            def turn(i):
                for n in range(N_ITEMS):
                    evict_scalar(act, i, n)
                    if n == 6:
                        y_scalar(act, i, 0)
                    if exists(i, n + 2):
                        exp_scalar(act, i, n + 2)
                y_scalar(act, i, 1)

            with act.Fori(0, TURNS - 1) as i:
                turn(i)
            turn(TURNS - 1)

        def q_vector(dve, i, j):
            dve.wait_ge(unit_done, i * 2 + (q_units + j + 1))
            nc.vector.tensor_tensor(qT[j][:, :], bank[0][:, :], R[:, :], ALU.mult).then_inc(tile_taken, 1)

        def read_vector(dve, i, idx):
            j, g, r = item(idx)
            V = nc.vector
            if r == 0:
                c = c_nth(i, idx)
                dve.wait_ge(alibi_ready, c * 2 + 2)
                dve.wait_ge(c_scored, c + 1)
                V.tensor_tensor(Pc[:, :], bank[2][:, 0:P], alibi_c[g][:, :], ALU.add).then_inc(scores_read, 1)
                dve.wait_ge(scores_read, nth(i, idx) + 2)
                by_block = Pc[:, :].rearrange("p (b n) -> p b n", b=NB)
                V.tensor_reduce(c_max[:, 0:4], by_block, AX.X, ALU.max).then_inc(c_maxed, 1)
                dve.wait_ge(c_maxed, c + 1)
                V.tensor_tensor(by_block, by_block, over_columns(c_max[:, 0:4], 32), ALU.subtract).then_inc(c_shifted, 1)
                return
            P_ = Pr[s_parity(idx)]
            for n, pieces in enumerate(PIECES):
                wait_apart(dve, scored, s_nth(i, idx) * 3 + (n + 1))
                for b, col in pieces:
                    at0 = col - GROUPS[n][0]
                    ins = V.tensor_tensor_reduce(P_[:, col:col + (b + 1) * P], bank[2 + n][:, at0:at0 + (b + 1) * P],
                                                 alibi[g][:, (3 - b) * P:], -KEY_SCALE, 3.0e38, ALU.add, ALU.min,
                                                 stat(idx, 0)[:, b:b + 1])
            ins.then_inc(scores_read, 1)

        def weights_vector(dve, i, idx):
            j, g, r = item(idx)
            V = nc.vector
            n = nth(i, idx)
            dve.wait_ge(probs_done, n + 1)
            if r == 0:
                V.tensor_reduce(stat(idx, 1), Pc[:, :].rearrange("p (b n) -> p b n", b=NB), AX.X, ALU.add).then_inc(c_summed, 1)
                dve.wait_ge(c_summed, c_nth(i, idx) + 1)
            V.reciprocal(stat(idx, 2), stat(idx, 1)).then_inc(inverse, 1)
            dve.wait_ge(inverse, n + 1)
            gate = gates[:, :].rearrange("p (b c) -> p b c", b=NB)[:, :, bass.ds(i * 2 + (16 * r + 8 * g + j), 1)]
            w, inv = stat(idx, 3), stat(idx, 2)
            V.tensor_tensor(w.unsqueeze(2), inv.unsqueeze(2), gate, ALU.mult).then_inc(weight_ready, 1)
            dve.wait_ge(weight_ready, i * 16 + (WEIGHTS[idx] + 1))
            if r == 0:
                V.tensor_tensor(w, w, seen, ALU.mult).then_inc(weight_ready, 1)
                dve.wait_ge(weight_ready, i * 16 + (WEIGHTS[idx] + 2))
            else:
                m = s_nth(i, idx)
                dve.wait_ge(turned, m * 3 + 2)
                V.tensor_copy(PT[:, 512:1024], bank[6][:, :]).then_inc(pT_dve, 1)

        def output_vector(dve, i, idx):
            j, g, r = item(idx)
            V = nc.vector
            n = nth(i, idx)
            w = stat(idx, 3)
            dve.wait_ge(pv_done, n + 1)
            o = bank[7][:, 0:2 * P].rearrange("p (b d) -> p b d", b=NB)
            y = y_tok[:, :].rearrange("p (b c) -> p b c", b=NB)[:, :, 64 * g:64 * g + 64]
            tmp = o_tmp[:, :].rearrange("p (b d) -> p b d", b=NB)
            if r == 0:
                V.tensor_tensor(y, o, over_columns(w, 64), ALU.mult).then_inc(weighed, 1)
            else:
                V.tensor_tensor(tmp, o, over_columns(w, 64), ALU.mult).then_inc(weighed, 1)
                dve.wait_ge(weighed, n + 2)
                V.tensor_tensor(y, y, tmp, ALU.add).then_inc(added, 1)
                dve.wait_ge(added, s_nth(i, idx) + 1)

        WEIGHTS = [idx + sum(1 for it in ITEMS[:idx] if not it[2]) for idx in range(N_ITEMS)]

        def y_vector(dve, i, j):
            dve.wait_ge(y_high, i * 2 + (j + 1))
            here = i * 2 + (8 + j)
            nc.vector.tensor_tensor(cols(ML, here), bank[0][:, :], cols(MR, here).bitcast(F32), ALU.subtract).then_inc(y_low, 1)

        def attend_vector(dve):
            nc.vector.sem_inc(scores_read, 1)
            nc.vector.sem_inc(weighed, 1)
            q_vector(dve, 0, 0)
            read_vector(dve, 0, 0)
            read_vector(dve, 0, 1)

            def turn(i):
                for n in range(N_ITEMS):
                    weights_vector(dve, i, n)
                    if exists(i, n + 2):
                        read_vector(dve, i, n + 2)
                    if n == 6:
                        y_vector(dve, i, 0)
                    output_vector(dve, i, n)
                    if n == 1:
                        q_vector(dve, i, 1)
                    if n == 7 and exists(i, N_ITEMS):
                        q_vector(dve, i + 1, 0)
                y_vector(dve, i, 1)

            with dve.Fori(0, TURNS - 1) as i:
                turn(i)
            turn(TURNS - 1)

        final_ready = sem("final_ready")

        def final_vector(dve):
            dve.wait_ge(norm_ready, NORM["h6"] + 1)
            with dve.Fori(0, DT) as n:
                nc.vector.scalar_tensor_tensor(cols(Y, n), cols(hT, n), param("final", n), R[:, :], ALU.mult, ALU.mult).then_inc(final_ready, 1)

        x_again = sem("x_again")
        block = ctx.enter_context(nc.Block())
        names8 = [n for n, _, _ in SEGMENTS]

        @block.sync
        def _(sp):
            sp.dma_start(memT[:, :], t["memT"]).then_inc(mem_loaded, 16)
            sp.dma_start(table[:, :], t["table"]).then_inc(tables_loaded, 16)
            sp.dma_start(params[:, :], t["params"]).then_inc(tables_loaded, 16)
            sp.dma_start(hT[:, :], t["xT"]).then_inc(x_loaded, 16)
            for name in names8:
                stream(sp, SEG[name], lambda unit, row, turn, slot, name=name:
                       load_unit(sp, SEG[name], unit, row + SEG[name].source0, slot))
            with sp.Fori(0, DT) as n:
                sp.wait_ge(final_ready, n + 1)
                sp.dma_start(out[:, bass.ds(n * SEQ, SEQ)], cols(Y, n)).then_inc(stored, 16)
            sp.wait_ge(stored, 16 * DT)

        @block.gpsimd
        def _(pool):
            for name in names8:
                seg = SEG[name]
                if name in SHARED:
                    for c in range(2):
                        split_unit(pool, seg, seg.unit0 + c, (seg.unit0 + c) // 2, (seg.unit0 + c) % 2)
                    with pool.Fori(1, seg.units // 2) as i:
                        for c in range(2):
                            pool.wait_ge(high_ahead, i * 2 + (seg.ahead0 + c - 1))
                            low_unit(seg, (seg.unit0 + c) % 2)
                else:
                    stream(pool, seg, lambda unit, row, turn, slot, seg=seg: split_unit(pool, seg, unit, turn, slot))

        @block.tensor
        def _(pe):
            mem_tensor(pe)
            gates_tensor(pe)
            gdn_tensor(pe)
            with pe.Fori(0, MEM_HEADS) as h:
                mem_head_tensor(pe, h)
            tiles(pe, SEG["out1"], lambda k: M_R[:, k], lambda k: M_L[:, k], (m_stored, -8))
            total(pe, "mix")
            ffn_tensor(pe, 1, "h1")
            total(pe, "ffn")
            conv_tensor(pe)
            ffn_tensor(pe, 2, "h3")
            kv_tensor(pe)
            pe.wait_ge(gate_ready, 1)
            attend_tensor(pe)
            tiles(pe, SEG["out2"], lambda k: M_R[:, 8 + k], lambda k: M_L[:, 8 + k], (y_low, 0))
            ffn_tensor(pe, 3, "h5")
            total(pe, "h6")

        @block.scalar
        def _(act):
            order = Order(act, sca)
            start_scalar(act)
            mem_scalar(act)
            gates_scalar(act)
            gdn_scalar(act, order)
            with act.Fori(0, MEM_HEADS) as h:
                mem_head_scalar(act, h)
            act.wait_ge(m_stored, MEM_HEADS)
            act.dma_start(hT[:, :], t["xT"]).then_inc(x_again, 16)
            keep_scalar(act, SEG["out1"], "mix")
            join_scalar(act, "mix", "h1", "pre_ffn")
            ffn_scalar(act, 1)
            keep_scalar(act, SEG["down1"], "ffn")
            join_scalar(act, "ffn", "h2", "a_norm")
            conv_scalar(act)
            ffn_scalar(act, 2)
            act.wait_ge(mid_low, 2 * FT)
            act.dma_start(phi1[:, :], t["phi1"]).then_inc(phi_loaded, 16)
            act.dma_start(phi2[:, :], t["phi2"]).then_inc(phi2_loaded, 16)
            stream_scalar(act, SEG["down2"], "h4", "kv", "kv_norm")
            kv_scalar(act)
            attend_scalar(act)
            stream_scalar(act, SEG["out2"], "h5", "h5", "ffn2")
            ffn_scalar(act, 3)
            stream_scalar(act, SEG["down3"], "h6", None, None)

        @block.vector
        def _(dve):
            order = Order(dve, vec)
            start_vector(dve, order)
            gates_vector(dve, order)
            gdn_vector(dve, order)
            with dve.Fori(0, MEM_HEADS) as h:
                mem_head_vector(dve, h)
            dve.wait_ge(m_stored, MEM_HEADS)
            keep_vector(dve, order, "mix")
            dve.wait_ge(x_again, 16)
            join_vector(dve, order, "mix", "post_mix", "h1", "pre_ffn")
            ffn_vector(dve, 1, "h1")
            keep_vector(dve, order, "ffn")
            join_vector(dve, order, "ffn", "post_ffn", "h2", "a_norm")
            conv_vector(dve, order)
            ffn_vector(dve, 2, "h3")
            stream_vector(dve, order, SEG["down2"], "h4", "kv", "kv_norm")
            kv_vector(dve, order)
            attend_vector(dve)
            stream_vector(dve, order, SEG["out2"], "h5", "h5", "ffn2")
            ffn_vector(dve, 3, "h5")
            stream_vector(dve, order, SEG["down3"], "h6", None, None)
            final_vector(dve)


def tile_units(weight, kt):
    k, n = weight.shape
    pieces = weight.reshape(k // P, P, n // P, P).transpose(2, 0, 1, 3).reshape(-1, kt, P, P)
    return pieces.transpose(0, 2, 1, 3).reshape(-1, P, kt * P)


def columns(vector):
    return vector.reshape(-1, P).T


def kernel(**inputs):
    import concourse.bacc as bacc
    from concourse.bass_utils import run_bass_kernel_spmd as run

    a = {k: np.asarray(v) for k, v in inputs.items()}
    f32 = np.float32

    gdn = a["gdn_w_in"][0]
    qkv, z, heads = gdn[:, :3072], gdn[:, 3072:4096], gdn[:, 4096:4112]
    q_mem_w = gdn[:, 4112:]
    ab = np.zeros((D, P), f32)
    ab[:, 0:8], ab[:, 32:40] = heads[:, 0:8], heads[:, 8:16]
    kv = a["w_mem_kv"][0]
    values = kv[:, 512:].reshape(4, 2, P, 512).transpose(0, 2, 1, 3).reshape(4, P, 1024)
    groups = np.concatenate([w for h in range(HEADS) for w in (
        qkv[:, 1024 + h * P:1024 + (h + 1) * P], qkv[:, 2048 + h * P:2048 + (h + 1) * P],
        qkv[:, h * P:(h + 1) * P], z[:, h * P:(h + 1) * P])] + [q_mem_w], axis=1)

    def pairs(w, n):
        k = w.shape[0]
        return w.reshape(k, 2, n, P).transpose(0, 2, 1, 3).reshape(k, 2 * n * P)

    gate_first = np.r_[D:2 * D, 0:D]
    ffn = [a["w_ffn_in"][0], a["ffn_w_in_2"][0], a["ffn_w_in_2"][1]]
    down = [a["w_ffn_out"][0], a["ffn_w_out_2"][0], a["ffn_w_out_2"][1]]
    w_in = a["b_w_in_2"][0]
    by_pair = w_in[:, :1024].reshape(D, 2, 8, 64).transpose(0, 2, 1, 3).reshape(D, 1024)
    gate_w = np.zeros((D, P), f32)
    gate_w[:, :48] = w_in[:, 1024:]
    w_kv = a["w_kv_2"].reshape(D, 6, P)[:, [0, 1, 2, 4, 3, 5]].reshape(D, 6 * P)
    w_o = a["b_w_out_2"][0].reshape(2, 8, 64, D).transpose(1, 0, 2, 3).reshape(D, D)
    w8 = np.concatenate([tile_units(kv[:, :512], 8), values, tile_units(ab, 8), tile_units(groups, 8),
                         tile_units(pairs(ffn[0], FT), 8), tile_units(pairs(a["a_pw1_w_2"][0][:, gate_first], DT), 8),
                         tile_units(a["a_pw2_w_2"][0], 8), tile_units(pairs(ffn[1], FT), 8),
                         tile_units(w_kv, 8), tile_units(gate_w, 8), tile_units(by_pair, 8), tile_units(w_o, 8),
                         tile_units(pairs(ffn[2], FT), 8)])
    w6 = tile_units(a["w_out"][0], 6)
    w11 = np.concatenate([tile_units(w, 11) for w in down])

    def head_rows(v):
        col = np.zeros((P, 1), f32)
        col[:8, 0] = v
        return col

    slopes = np.broadcast_to(-8.0 * 2.0 ** (-8.0 * (np.arange(16) + 1) / 16), (P, 16)).astype(f32)
    conv4 = a["gdn_conv"][0].reshape(CONV_K, 24, P).transpose(2, 1, 0).reshape(P, 24 * CONV_K)
    conv31 = a["a_dw_w_2"][0].reshape(TAPS, DT, P).transpose(2, 1, 0).reshape(P, DT * TAPS)
    both = lambda pos: np.concatenate([pos.T, pos.T], axis=0)
    parts = {
        "mem_norm": columns(a["mem_norm"]), "pre_mix": columns(a["norm_pre_mix"][0]),
        "post_mix": columns(a["norm_post_mix"][0]), "pre_ffn": columns(a["norm_pre_ffn"][0]),
        "post_ffn": columns(a["norm_post_ffn"][0]), "gdn_out": columns(a["gdn_out_norm"][0]),
        "conv4": conv4, "a_norm": columns(a["a_norm_2"][0]), "pw1_a": columns(a["a_pw1_b_2"][0, :D]),
        "pw1_b": columns(a["a_pw1_b_2"][0, D:]), "dw_b": columns(a["a_dw_b_2"][0]),
        "ln_g": columns(a["a_ln_g_2"][0]), "ln_b": columns(a["a_ln_b_2"][0]), "pw2_b": columns(a["a_pw2_b_2"][0]),
        "kv_norm": columns(a["kv_norm_2"]), "b_norm": columns(a["b_norm_2"][0]),
        "ffn1": columns(a["ffn_norm_2"][0]), "ffn2": columns(a["ffn_norm_2"][1]), "final": columns(a["final_norm_2"]),
        "a_log": head_rows(a["gdn_a_log"][0]), "dt_bias": head_rows(a["gdn_dt_bias"][0]), "slopes": slopes,
        "conv31": conv31, "pos_k": both(a["cmp_pos_k_2"]), "pos_v": both(a["cmp_pos_v_2"]),
    }
    params = np.concatenate([parts[n] for n in PARAMS], axis=1)

    def phi_first(w):
        one = w.reshape(L_CMP, 64, 64).transpose(1, 0, 2).reshape(64, L_CMP * 64)
        return np.concatenate([one, one], axis=0)

    phi1 = np.concatenate([phi_first(a["phi_k_w1_2"]), phi_first(a["phi_v_w1_2"])], axis=1)
    phi2 = np.zeros((P, 2 * P), f32)
    for i, w in enumerate((a["phi_k_w2_2"], a["phi_v_w2_2"])):
        for g in range(2):
            phi2[64 * g:64 * g + 64, i * P + 64 * g:i * P + 64 * g + 64] = w
    feature_rows = lambda x: x.T.reshape(DT, P, -1).transpose(1, 0, 2).reshape(P, -1)
    arrays = {"w8": w8, "w6": w6, "w11": w11, "xT": feature_rows(a["x"][0]), "memT": feature_rows(a["mem"][0]),
              "table": constant_tables(), "params": params, "phi1": phi1, "phi2": phi2}
    arrays = {k: np.ascontiguousarray(v) for k, v in arrays.items()}

    nc = bacc.Bacc("TRN2", target_bir_lowering=False, num_devices=1)
    t = {k: nc.dram_tensor(k, v.shape, F32, kind="ExternalInput").ap() for k, v in arrays.items()}
    out = nc.dram_tensor("out", (P, DT * SEQ), F32, kind="ExternalOutput").ap()
    program(nc, t, out)
    r = run(nc, [arrays], core_ids=[0])
    got = np.asarray(r.results[0]["out"]).reshape(P, DT, SEQ).transpose(2, 1, 0).reshape(1, SEQ, D)
    return got
```

```python
from contextlib import ExitStack

import numpy as np

import concourse.bass as bass
from concourse import mybir

F32 = mybir.dt.float32
F32R = mybir.dt.float32r
ALU = mybir.AluOpType
ACT = mybir.ActivationFunctionType
AX = mybir.AxisListType

P = 128
SEQ = 512
D = 1024
DT = D // P
NB = SEQ // P
EPS = 1e-6
HEADS = 8
CONV_K = 4
MEM = 256
MEM_HEADS = 4
DFF = 2816
FT = DFF // P
TAPS = 31
PAD = TAPS - 1
N_CMP = 31
L_CMP = 32
STRIDE = 16
NQ = 8
LEVELS = 7
FAR = 1.0e34

SEGMENTS = [
    ("heads", 8, 1), ("mem", 8, 8), ("gdn", 8, 36), ("out1", 6, 16), ("in1", 8, 44), ("down1", 11, 16),
    ("pw1", 8, 16), ("pw2", 8, 8), ("in2", 8, 44), ("down2", 11, 16),
    ("kvq", 8, 15), ("out2", 8, 8), ("in3", 8, 44), ("down3", 11, 16),
]
SHARED = [name for name, _, _ in SEGMENTS if name not in ("heads", "gdn", "kvq")]
UNITS_PER_TILE = {8: 1, 6: 2, 11: 2}
SLOT = 11 * P


class Segment:

    def __init__(self, unit0, tile0, source0, kt, units, own0):
        self.unit0, self.tile0, self.source0, self.kt, self.units = unit0, tile0, source0, kt, units
        self.per_tile = UNITS_PER_TILE[kt]
        self.own0 = own0
        self.ahead0 = unit0 - own0
        self.handed, self.follower = False, None


def plan_segments():
    table, unit, tile, own, before, source = {}, 0, 0, 0, None, {8: 0, 6: 0, 11: 0}
    for name, kt, units in SEGMENTS:
        table[name] = Segment(unit, tile, source[kt], kt, units, own)
        if name in SHARED and before in SHARED:
            table[name].handed, table[before].follower = True, table[name]
        else:
            own += 2 if name in SHARED else units
        before = name
        unit += units
        source[kt] += units
        tile += units // UNITS_PER_TILE[kt]
    return table


SEG = plan_segments()

PARAMS = {}
_at = 0
for _name, _n in [("mem_norm", DT), ("pre_mix", DT), ("post_mix", DT), ("pre_ffn", DT), ("post_ffn", DT),
                  ("gdn_out", 1), ("conv4", 24 * CONV_K), ("a_norm", DT), ("pw1_a", DT), ("pw1_b", DT),
                  ("dw_b", DT), ("ln_g", DT), ("ln_b", DT), ("pw2_b", DT), ("kv_norm", DT), ("b_norm", DT),
                  ("ffn1", DT), ("ffn2", DT), ("final", DT), ("a_log", 1), ("dt_bias", 1), ("slopes", 16),
                  ("conv31", DT * TAPS), ("pos_k", L_CMP), ("pos_v", L_CMP)]:
    PARAMS[_name] = (_at, _n)
    _at += _n
N_PARAMS = _at

IDENT, ONES, TRI, LEVEL0 = 0, 1, 2, 3
N_CONST = LEVEL0 + LEVELS


def constant_tables():
    p, f = np.arange(P)[:, None], np.arange(P)[None, :]
    square = np.zeros((P, N_CONST, P), np.float32)
    square[:, IDENT] = p == f
    square[:, ONES] = 1.0
    square[:, TRI] = p <= f
    for s in range(LEVELS):
        square[:, LEVEL0 + s] = (p >> (s + 1) == f >> (s + 1)) & (p >> s & 1 == 1) & (f >> s & 1 == 0)
    dist = SEQ - P + p - np.arange(SEQ)[None, :]
    dist = np.where(dist >= 0, dist, FAR).astype(np.float32)
    n = np.arange(32)[None, None, :]
    t = np.arange(NB)[None, :, None] * P + np.arange(P)[:, None, None]
    cmp = t - (n * STRIDE + L_CMP - 1)
    cmp = np.where((cmp >= 0) & (n < N_CMP), cmp, FAR).astype(np.float32)
    seen = np.broadcast_to(t >= L_CMP - 1, (P, NB, 1)).reshape(P, NB).astype(np.float32)
    return np.concatenate([square.reshape(P, -1), dist, cmp.reshape(P, -1), seen], axis=1)


TABLE_COLS = N_CONST * P + SEQ + NB * 32 + NB
TABLE_ROOM = -(-4 * TABLE_COLS // 32) * 32
PARAM_ROOM = -(-4 * N_PARAMS // 32) * 32


def program(nc, t, out):
    with ExitStack() as ctx:
        base = nc.sbuf_base
        base = (base + 31) // 32 * 32
        KB = 1024

        def at(name, offset, cols, dt=F32, parts=P):
            return nc.alloc_sbuf_tensor_at(name, [parts, cols], dt, offset=base + offset)

        hT = at("hT", 0, DT * SEQ)
        XR = at("XR", 16 * KB, DT * SEQ, F32R)
        XL = at("XL", 32 * KB, DT * SEQ, F32R)
        raw = at("raw", 48 * KB, 2 * SLOT)
        WR = at("WR", 59 * KB, 2 * SLOT, F32R)
        WL = at("WL", 70 * KB, 2 * SLOT, F32R)
        MR = at("MR", 81 * KB, FT * SEQ, F32R)
        ML = at("ML", 125 * KB, FT * SEQ, F32R)
        Y = at("Y", 169 * KB, DT * SEQ)
        table = at("table", 185 * KB, TABLE_COLS)
        params = at("params", 185 * KB + TABLE_ROOM, N_PARAMS)
        low = 185 * KB + TABLE_ROOM + PARAM_ROOM
        R = at("R", low, SEQ)
        small = at("small", low + 2 * KB, 8)
        ctx.enter_context(nc.sbuf_tensor("fence", [P, (low + 2 * KB + 32 + 64) // 4], F32))

        X_R = XR[:, :].rearrange("p (k n) -> p k n", k=DT)
        X_L = XL[:, :].rearrange("p (k n) -> p k n", k=DT)
        M_R = MR[:, :].rearrange("p (k n) -> p k n", k=FT)
        M_L = ML[:, :].rearrange("p (k n) -> p k n", k=FT)

        def const(i):
            return table[:, i * P:(i + 1) * P]

        ident, ones, tri = const(IDENT), const(ONES), const(TRI)
        dist = table[:, N_CONST * P:N_CONST * P + SEQ]
        dist_cmp = table[:, N_CONST * P + SEQ:N_CONST * P + SEQ + NB * 32]
        seen = table[:, TABLE_COLS - NB:TABLE_COLS]
        eps_col, one_col = small[:, 0:1], small[:, 1:2]

        def param(name, i=0, n=1):
            first = PARAMS[name][0]
            return params[:, first + i:first + i + n] if isinstance(i, int) else params[:, bass.ds(first + i, n)]

        bank = [ctx.enter_context(nc.psum_tensor(f"bank{i}", [P, 512], F32)) for i in range(8)]

        def sem(name):
            return ctx.enter_context(nc.semaphore(name))

        tables_loaded = sem("tables_loaded")
        x_loaded = sem("x_loaded")
        eps_set = sem("eps_set")
        passed = sem("passed")
        weight_loaded = [sem(f"weight_loaded{i}") for i in range(2)]
        high_split = sem("high_split")
        high_ahead = sem("high_ahead")
        weight_split = sem("weight_split")
        unit_done = sem("unit_done")
        tile_taken = sem("tile_taken")
        input_high = sem("input_high")
        input_ready = sem("input_ready")
        squared = sem("squared")
        summed = sem("summed")
        total_done = sem("total_done")
        log_done = sem("log_done")
        norm_ready = sem("norm_ready")
        vec = sem("vec")
        sca = sem("sca")
        stored = sem("stored")

        def wait_apart(engine, semaphore, value):
            engine.wait_ge(semaphore, value)
            engine.sem_inc(passed, 1)

        source = {8: t["w8"], 6: t["w6"], 11: t["w11"]}

        def load_unit(sp, seg, unit, row, slot):
            if not (isinstance(unit, int) and unit < 2):
                sp.wait_ge(weight_split, unit - 1)
            sp.dma_start(raw[:, slot * SLOT:slot * SLOT + seg.kt * P],
                         source[seg.kt][row]).then_inc(weight_loaded[slot], 16)

        def split_unit(pool, seg, unit, turn, slot):
            here = slice(slot * SLOT, slot * SLOT + seg.kt * P)
            pool.wait_ge(weight_loaded[slot], turn * 16 + 16)
            if not (isinstance(unit, int) and unit < 2):
                wait_apart(pool, unit_done, unit - 1)
            nc.gpsimd.tensor_copy(WR[:, here], raw[:, here]).then_inc(high_split, 1)
            pool.wait_ge(high_split, unit + (seg.own0 - seg.unit0 + 1))
            low_unit(seg, slot)

        def split_ahead(act, seg, i, per_turn, first, n=1):
            for c in range(first, first + n):
                if isinstance(i, int) and i * per_turn + c >= seg.units:
                    if seg.follower:
                        split_ahead(act, seg.follower, 0, 2, i * per_turn + c - seg.units)
                    continue
                slot = (seg.unit0 + c) % 2
                here = slice(slot * SLOT, slot * SLOT + seg.kt * P)
                act.wait_ge(weight_loaded[slot], (i * (per_turn // 2) + (seg.unit0 + c) // 2) * 16 + 16)
                act.wait_ge(unit_done, i * per_turn + (seg.unit0 + c - 1))
                nc.scalar.activation(WR[:, here], raw[:, here], ACT.Identity).then_inc(high_ahead, 1)

        def low_unit(seg, slot):
            here = slice(slot * SLOT, slot * SLOT + seg.kt * P)
            nc.gpsimd.tensor_tensor(WL[:, here], raw[:, here], WR[:, here].bitcast(F32),
                                    ALU.subtract).then_inc(weight_split, 1)

        def stream(engine, seg, step):
            pairs = seg.units // 2
            u0 = seg.unit0
            peel = min(pairs, 1 if u0 < 2 else 0)
            for j in range(2 * peel):
                step(u0 + j, j, (u0 + j) // 2, (u0 + j) % 2)
            if pairs > peel:
                with engine.Fori(peel, pairs) as i:
                    for j in range(2):
                        slot = (u0 + j) % 2
                        step(i * 2 + (u0 + j), i * 2 + j, i + (u0 + j) // 2, slot)
            if seg.units % 2:
                j = seg.units - 1
                step(u0 + j, j, (u0 + j) // 2, (u0 + j) % 2)

        def products(pe, seg, unit, slot, k0, into, xr, xl, first, last, ks=None, ready=None):
            n = seg.kt if ks is None else ks[1] - ks[0]
            k_from = 0 if ks is None else ks[0]
            if k_from == 0:
                pe.wait_ge(weight_split, unit + 1)
            for k in range(k_from, k_from + n):
                if ready and ready[1] + k0 + k + 1 > 0:
                    pe.wait_ge(ready[0], ready[1] + k0 + k + 1)
                wr = WR[:, slot * SLOT + k * P:slot * SLOT + (k + 1) * P]
                wl = WL[:, slot * SLOT + k * P:slot * SLOT + (k + 1) * P]
                start, stop = first and k == 0, last and k == seg.kt - 1
                nc.tensor.matmul(into, wr, xr(k0 + k), start=start, stop=False)
                nc.tensor.matmul(into, wr, xl(k0 + k), start=False, stop=False)
                mm = nc.tensor.matmul(into, wl, xr(k0 + k), start=False, stop=stop)
            if k_from + n == seg.kt:
                mm.then_inc(unit_done, 1)

        def bank_of(seg, c):
            return bank[(seg.tile0 + c) % 2 if c < 2 else 2 + c]

        def tiles(pe, seg, xr, xl, ready, then=None, wide=False, after_wide=False):
            u0, t0, per, n = seg.unit0, seg.tile0, seg.per_tile, 4 if wide else 2

            def turn(i):
                for j in range(n):
                    opening = isinstance(i, int) and j == 0
                    if not wide:
                        pe.wait_ge(tile_taken, i * 2 + (t0 + j - (3 if after_wide and isinstance(i, int) else 1)))
                    elif not isinstance(i, int):
                        pe.wait_ge(tile_taken, i * 4 + (t0 + j - 3))
                    elif j < 2:
                        pe.wait_ge(tile_taken, t0 + j - 1)
                    for part in range(per):
                        c = per * j + part
                        products(pe, seg, i * n * per + (u0 + c), (u0 + c) % 2, part * seg.kt, bank_of(seg, j)[:, :],
                                 xr, xl, part == 0, part == per - 1, ready=ready if opening else None)
                        if opening and part == 0 and then:
                            then()

            turn(0)
            with pe.Fori(1, seg.units // (n * per)) as i:
                turn(i)

        class Order:

            def __init__(self, engine, s):
                self.engine, self.s, self.base, self.k, self.i, self.per = engine, s, 0, 0, None, 0

            def value(self):
                return self.base + self.k if self.i is None else self.i * self.per + (self.base + self.k)

            def mark(self, ins):
                ins.then_inc(self.s, 1)
                self.k += 1

            def sync(self):
                self.engine.wait_ge(self.s, self.value())

            def link(self, ins):
                self.mark(ins)
                self.sync()

            def enter(self, i, per, i0):
                self.base, self.k, self.i, self.per, self.i0 = self.base + self.k - per * i0, 0, i, per, i0

            def leave(self, turns):
                assert self.k == self.per, f"{self.k} marks in a loop of {self.per}"
                self.base, self.k, self.i = self.base + self.per * (self.i0 + turns), 0, None

        def cols(tile, i, n=SEQ):
            return tile[:, i * n:(i + 1) * n] if isinstance(i, int) else tile[:, bass.ds(i * n, n)]

        def blocks(tile):
            return tile.rearrange("p (b n) -> p b n", b=NB)

        def over_blocks(square):
            return square.unsqueeze(1).broadcast_to([P, NB, P])

        def over_columns(scalars, n=P):
            return scalars.unsqueeze(2).broadcast_to([P, scalars.shape[1], n])

        NORM = {n: i for i, n in enumerate(["x", "mem", "mix", "h1", "ffn", "h2", "var", "h3", "h4", "h5", "h6"])}
        INPUT = {n: DT * i for i, n in enumerate(["x", "mem", "h1", "h2", "conv", "h3", "kv", "q", "h5"])}
        SQ = at("SQ", low + 2 * KB + 32, 2 * SEQ)
        ACC = at("ACC", low + 6 * KB + 32, SEQ)

        def square_tile(act, norm, n, parity, src, width=SEQ):
            if not (isinstance(n, int) and NORM[norm] == 0 and n < 2):
                wait_apart(act, summed, n + (DT * NORM[norm] - 1))
            nc.scalar.activation(SQ[:, parity * SEQ:parity * SEQ + width], src, ACT.Square).then_inc(squared, 1)

        def clear_sum(dve, order, norm, width=SEQ):
            if NORM[norm]:
                dve.wait_ge(total_done, NORM[norm])
            order.link(nc.vector.memset(ACC[:, 0:width], 0.0))

        def add_squares(dve, norm, n, parity, width=SEQ):
            dve.wait_ge(squared, n + (DT * NORM[norm] + 1))
            if not (isinstance(n, int) and NORM[norm] == 0 and n == 0):
                dve.wait_ge(summed, n + DT * NORM[norm])
            nc.vector.tensor_tensor(ACC[:, 0:width], ACC[:, 0:width], SQ[:, parity * SEQ:parity * SEQ + width],
                                    ALU.add).then_inc(summed, 1)

        def total(pe, norm, width=SEQ):
            pe.wait_ge(summed, DT * (NORM[norm] + 1))
            nc.tensor.matmul(bank[2][:, 0:width], ones, ACC[:, 0:width], start=True, stop=True).then_inc(total_done, 1)

        def root(act, norm, width=SEQ):
            e = NORM[norm]
            act.wait_ge(total_done, e + 1)
            nc.scalar.activation(R[:, 0:width], bank[2][:, 0:width], ACT.Ln, bias=eps_col, scale=1.0 / D).then_inc(log_done, 1)
            act.wait_ge(log_done, e + 1)
            nc.scalar.activation(R[:, 0:width], R[:, 0:width], ACT.Exp, scale=-0.5).then_inc(norm_ready, 1)

        def high_part(act, name, n, dst, src, gain):
            nc.scalar.activation(dst, src, ACT.Identity, scale=gain).then_inc(input_high, 1)

        def low_part(dve, name, n, dst, src, high, gain):
            dve.wait_ge(input_high, n + (INPUT[name] + 1))
            nc.vector.scalar_tensor_tensor(dst, src, gain, high.bitcast(F32), ALU.mult, ALU.subtract).then_inc(input_ready, 1)

        mem_loaded = sem("mem_loaded")
        scratch = {}

        def place(regions):
            for start, size, names in regions:
                spot = start
                for name, n in names:
                    scratch[name] = at(name, spot, n)
                    spot += (4 * n + 31) // 32 * 32
                assert spot <= start + size, (names[-1][0], spot - start - size)

        HP = SEQ + 8
        place([
            ((81 + 24) * KB, 20 * KB, [("pre0", HP), ("pre1", HP), ("pre2", HP), ("act0", SEQ), ("act1", SEQ),
                                       ("act2", SEQ), ("gate_z", SEQ), ("keys", SEQ), ("queries", SEQ)]),
            ((125 + 24) * KB, 20 * KB, [("D_E", SEQ), ("q_decayed", SEQ), ("v_beta", SEQ), ("k_gained", SEQ),
                                        ("lower", SEQ), ("pT", SEQ), ("low_a", SEQ), ("low_b", SEQ), ("T", SEQ),
                                        ("U", SEQ)]),
            (169 * KB, 16 * KB, [("As", SEQ), ("sq_k", SEQ), ("sq_q", SEQ), ("r_k", SEQ), ("r_q", SEQ),
                                 ("o_rows", SEQ), ("S", P), ("X", P), ("v_new", P), ("scalars", 6 * 32)]),
        ])
        g_ = scratch
        memT = at("memT", 169 * KB, DT * MEM)
        mem_t = at("mem_t", (81 + 24) * KB, 2 * MEM)
        x_t = at("x_t", (81 + 28) * KB, 2 * SEQ)
        q_mem = at("q_mem", 0, MEM_HEADS * SEQ)
        mem_keys = at("mem_keys", 8 * KB, MEM_HEADS * MEM)
        mem_values = at("mem_values", 12 * KB, 2 * SEQ)
        gates40 = at("gates40", (125 + 24) * KB, SEQ, parts=64)
        gate_t = at("gate_t", (125 + 26) * KB, SEQ, parts=64)
        gate_u = at("gate_u", (125 + 28) * KB, SEQ, parts=64)
        scal = g_["scalars"]
        beta, cum, k_gain, last_gain, neg_beta_decay, gcol = (scal[:, 32 * i:32 * i + 32] for i in range(6))

        mem_in_R = MR[:, 0:DT * MEM].rearrange("p (k n) -> p k n", k=DT)
        mem_in_L = ML[:, 0:DT * MEM].rearrange("p (k n) -> p k n", k=DT)

        scaled = sem("scaled")
        gate_part = sem("gate_part")
        gate_act = sem("gate_act")
        gates_turned = sem("gates_turned")
        gates_copied = sem("gates_copied")
        sums_done = sem("sums_done")
        decay_exp = sem("decay_exp")
        gates_ready = sem("gates_ready")

        def split_normed(act, dve, name, n, dst_r, dst_l, tmp):
            if act is not None:
                act.wait_ge(scaled, INPUT[name] + n + 1)
                nc.scalar.activation(dst_r, tmp, ACT.Identity).then_inc(input_high, 1)
            else:
                dve.wait_ge(input_high, INPUT[name] + n + 1)
                nc.vector.tensor_tensor(dst_l, tmp, dst_r.bitcast(F32), ALU.subtract).then_inc(input_ready, 1)

        START = [("x", hT, SEQ, "pre_mix", x_t, X_R, X_L),
                 ("mem", memT, MEM, "mem_norm", mem_t, mem_in_R, mem_in_L)]

        def start_scalar(act):
            for e, (name, src, w, gain, tmp, dr, dl) in enumerate(START):
                if e == 0:
                    act.wait_ge(x_loaded, 16)
                    act.wait_ge(eps_set, 1)
                else:
                    act.wait_ge(mem_loaded, 16)
                for n in range(DT):
                    square_tile(act, name, n, n % 2, cols(src, n, w), w)
                    if e == 0 and n == 0:
                        act.dma_start(memT[:, :], t["memT"]).then_inc(mem_loaded, 16)
                root(act, name, w)
                for n in range(DT):
                    split_normed(act, None, name, n, dr[:, n], dl[:, n], cols(tmp, n % 2, w))

        def start_vector(dve, order):
            nc.vector.memset(eps_col, EPS)
            nc.vector.memset(one_col, 1.0).then_inc(eps_set, 1)
            for e, (name, src, w, gain, tmp, dr, dl) in enumerate(START):
                clear_sum(dve, order, name, w)
                for n in range(DT):
                    add_squares(dve, name, n, n % 2, w)
                if e == 0:
                    dve.wait_ge(tables_loaded, 32)
                dve.wait_ge(norm_ready, e + 1)
                for n in range(DT + 1):
                    if n < DT:
                        if n >= 2:
                            dve.wait_ge(input_ready, INPUT[name] + n - 1)
                        nc.vector.scalar_tensor_tensor(cols(tmp, n % 2, w), cols(src, n, w), param(gain, n), R[:, 0:w],
                                                       ALU.mult, ALU.mult).then_inc(scaled, 1)
                    if n:
                        split_normed(None, dve, name, n - 1, dr[:, n - 1], dl[:, n - 1], cols(tmp, (n - 1) % 2, w))

        def heads_tensor(pe):
            pe.wait_ge(tables_loaded, 32)
            total(pe, "x")
            products(pe, SEG["heads"], 0, 0, 0, bank[0][:, :], lambda k: X_R[:, k], lambda k: X_L[:, k], True, True,
                     ready=(input_ready, INPUT["x"]))

        def mem_tensor(pe):
            total(pe, "mem", MEM)
            seg = SEG["mem"]
            u0, t0 = seg.unit0, seg.tile0
            for j in range(MEM_HEADS):
                if j:
                    pe.wait_ge(tile_taken, max(t0 + 1, t0 + j - 1))
                products(pe, seg, u0 + j, (u0 + j) % 2, 0, bank[(t0 + j) % 2][:, 0:MEM], lambda k: mem_in_R[:, k],
                         lambda k: mem_in_L[:, k], True, True, ready=None if j else (input_ready, INPUT["mem"]))
            pe.wait_ge(tile_taken, t0 + 4)
            for u in range(4):
                unit = u0 + 4 + u
                pe.wait_ge(weight_split, unit + 1)
                for kk in range(2):
                    k = 2 * u + kk
                    here = slice((unit % 2) * SLOT + kk * SEQ, (unit % 2) * SLOT + (kk + 1) * SEQ)
                    for b in range(2):
                        tok = slice(b * P, (b + 1) * P)
                        nc.tensor.matmul(bank[b][:, :], mem_in_R[:, k, tok], WR[:, here], start=k == 0, stop=False)
                        nc.tensor.matmul(bank[b][:, :], mem_in_L[:, k, tok], WR[:, here], start=False, stop=False)
                        mm = nc.tensor.matmul(bank[b][:, :], mem_in_R[:, k, tok], WL[:, here], start=False, stop=k == DT - 1)
                mm.then_inc(unit_done, 1)
            pe.wait_ge(tile_taken, t0 + 8)

        def mem_scalar(act):
            u0, t0 = SEG["mem"].unit0, SEG["mem"].tile0
            for j in range(MEM_HEADS):
                split_ahead(act, SEG["mem"], 0, 2, j + 2)
                act.wait_ge(unit_done, u0 + j + 1)
                if j == 0:
                    act.wait_ge(scaled, DT)
                nc.scalar.activation(cols(mem_keys, j, MEM), bank[(t0 + j) % 2][:, 0:MEM], ACT.Identity).then_inc(tile_taken, 1)
            split_ahead(act, SEG["mem"], 0, 2, MEM_HEADS + 2, 2)
            act.wait_ge(unit_done, u0 + 8)
            for j in range(4):
                b, half = j // 2, j % 2
                nc.scalar.activation(mem_values[:, b * SEQ + half * MEM:b * SEQ + (half + 1) * MEM],
                                     bank[b][:, half * MEM:(half + 1) * MEM], ACT.Identity).then_inc(tile_taken, 1)

        def gates_scalar(act):
            act.wait_ge(gate_part, 1)
            nc.scalar.activation(gate_u[0:8, :], gate_u[0:8, :], ACT.Exp, scale=-1.0).then_inc(gate_act, 1)
            nc.scalar.activation(small[0:8, 2:3], param("a_log")[0:8], ACT.Exp).then_inc(gate_act, 1)
            act.wait_ge(gate_act, 1)
            nc.scalar.activation(gate_u[0:8, :], gate_u[0:8, :], ACT.Ln, bias=one_col[0:8]).then_inc(gate_act, 1)
            act.wait_ge(gate_part, 2)
            nc.scalar.activation(gates40[32:40, :], gates40[32:40, :], ACT.Sigmoid).then_inc(gate_act, 1)

        def decays_scalar(act):
            act.wait_ge(gate_part, 5)
            for i, (dst, src) in enumerate([(k_gain, k_gain), (last_gain, last_gain), (neg_beta_decay, cum)]):
                nc.scalar.activation(dst, src, ACT.Exp).then_inc(decay_exp, 1)

        def gates_vector(dve, order):
            order.link(nc.vector.memset(gates40[:, :], 0.0))
            dve.wait_ge(unit_done, 1)
            order.link(nc.vector.tensor_scalar(gate_t[0:8, :], bank[0][0:8, :], param("dt_bias")[0:8], None, ALU.add))
            nc.vector.scalar_tensor_tensor(gate_u[0:8, :], gate_t[0:8, :], -1.0, gate_t[0:8, :], ALU.mult, ALU.max).then_inc(gate_part, 1)
            nc.vector.tensor_copy(gates40[32:40, :], bank[0][32:40, :]).then_inc(gate_part, 1)
            dve.wait_ge(gate_part, 2)
            nc.vector.tensor_scalar(gate_t[0:8, :], gate_t[0:8, :], 0.0, None, ALU.max).then_inc(tile_taken, 1)
            dve.wait_ge(tile_taken, 1)
            dve.wait_ge(gate_act, 3)
            order.link(nc.vector.tensor_tensor(gate_t[0:8, :], gate_t[0:8, :], gate_u[0:8, :], ALU.add))
            nc.vector.tensor_scalar(gates40[0:8, :], gate_t[0:8, :], small[0:8, 2:3], -1.0, ALU.mult, ALU.mult).then_inc(gate_part, 1)

        def decays_vector(dve, order):
            dve.wait_ge(gates_turned, 1)
            turned = bank[3][:, 0:NB * 40].rearrange("p (b c) -> p c b", b=NB)
            nc.vector.tensor_copy(gcol.rearrange("p (h b) -> p h b", b=NB), turned[:, 0:8]).then_inc(gates_copied, 1)
            nc.vector.tensor_copy(beta.rearrange("p (h b) -> p h b", b=NB), turned[:, 32:40]).then_inc(gates_copied, 1)
            dve.wait_ge(sums_done, 1)
            order.link(nc.vector.tensor_copy(cum, bank[4][:, 0:32]))
            nc.vector.tensor_tensor(k_gain, bank[4][:, 32:64], cum, ALU.subtract).then_inc(gate_part, 1)
            nc.vector.tensor_copy(last_gain, bank[4][:, 32:64]).then_inc(gate_part, 1)
            dve.wait_ge(decay_exp, 3)
            nc.vector.scalar_tensor_tensor(neg_beta_decay, neg_beta_decay, -1.0, beta, ALU.mult, ALU.mult).then_inc(gates_ready, 1)
            dve.wait_ge(gates_ready, 1)

        def gates_tensor(pe):
            pe.wait_ge(gate_part, 3)
            pe.wait_ge(gate_act, 4)
            for b in range(NB):
                mm = nc.tensor.transpose(bank[3][:, b * 40:b * 40 + 40], gates40[0:40, b * P:(b + 1) * P], ident[0:40, 0:40])
            mm.then_inc(gates_turned, 1)
            pe.wait_ge(gates_copied, 2)
            nc.tensor.matmul(bank[4][:, 0:32], tri, gcol, start=True, stop=True)
            nc.tensor.matmul(bank[4][:, 32:64], ones, gcol, start=True, stop=True).then_inc(sums_done, 1)

        names = ("conv_done silu_done keys_squared norm_summed norms_rooted keys_ready queries_ready "
                 "gate_rows_ready rows_done gap_ready decay_ready row_decay_ready q_decayed_ready v_turned "
                 "k_turned v_beta_ready k_gained_ready kk_done qk_done pT_ready T_ready T_turned U_ready "
                 "low_ready A_done A_ready UT_done UT_ready kS_done X_ready v_done v_ready o_done S_sum_done "
                 "S_ready o_squared o_copied o_summed o_rooted z_ready head_ready head_high head_stored").split()
        s_ = {n: sem(n) for n in names}
        GROUP_TILES = 4
        seg_g = SEG["gdn"]
        pre = [g_["pre0"], g_["pre1"], g_["pre2"]]
        acts = [g_["act0"], g_["act1"], g_["act2"]]
        QS = float(P) ** -0.5

        def row4(tile, h):
            return tile[:, bass.ds(h * NB, NB)] if not isinstance(h, int) else tile[:, h * NB:(h + 1) * NB]

        def col1(tile, h, b):
            return tile[:, bass.ds(h * NB + b, 1)] if not isinstance(h, int) else tile[:, h * NB + b:h * NB + b + 1]

        def group_chunks(pe, g):
            for j in range(GROUP_TILES):
                unit = g * GROUP_TILES + (seg_g.unit0 + j)
                pe.wait_ge(tile_taken, g * GROUP_TILES + (seg_g.tile0 + j - 1))
                for k in range(DT):
                    products(pe, seg_g, unit, (seg_g.unit0 + j) % 2, 0, bank[(seg_g.tile0 + j) % 2][:, :],
                             lambda k: X_R[:, k], lambda k: X_L[:, k], True, True, ks=(k, k + 1))
                    yield

        def key_norm_tensor(pe, g):
            pe.wait_ge(s_["keys_squared"], g * 2 + 1)
            nc.tensor.matmul(bank[5][:, :], ones, g_["sq_k"][:, :], start=True, stop=True).then_inc(s_["norm_summed"], 1)

        def query_norm_tensor(pe, g):
            pe.wait_ge(s_["keys_squared"], g * 2 + 2)
            nc.tensor.matmul(bank[6][:, :], ones, g_["sq_q"][:, :], start=True, stop=True).then_inc(s_["norm_summed"], 1)

        def output_norm_tensor(pe, n):
            pe.wait_ge(s_["o_squared"], n)
            nc.tensor.matmul(bank[2][:, :], ones, o_squares, start=True, stop=True).then_inc(s_["o_summed"], 1)

        def head_tensor(pe, h, g, first, last):
            chunks = group_chunks(pe, g)

            def gap(n):
                for _ in range(n):
                    next(chunks, None)

            pe.wait_ge(s_["gate_rows_ready"], h + 1)
            nc.tensor.matmul(bank[4][:, :], ones, g_["D_E"][:, :], start=True, stop=True).then_inc(s_["rows_done"], 1)
            pe.wait_ge(s_["norms_rooted"], h * 2 + 2)
            pe.wait_ge(s_["silu_done"], h * 3 + 2)
            for b in range(NB):
                mm = nc.tensor.transpose(bank[5][:, b * P:(b + 1) * P], acts[1][:, b * P:(b + 1) * P], ident)
            mm.then_inc(s_["v_turned"], 1)
            gap(1)
            pe.wait_ge(s_["keys_ready"], h + 1)
            for b in range(NB):
                kb = g_["keys"][:, b * P:(b + 1) * P]
                mm = nc.tensor.matmul(bank[7][:, b * P:(b + 1) * P], kb, kb, start=True, stop=True)
            mm.then_inc(s_["kk_done"], 1)
            for b in range(NB):
                mm = nc.tensor.transpose(bank[6][:, b * P:(b + 1) * P], g_["keys"][:, b * P:(b + 1) * P], ident)
            mm.then_inc(s_["k_turned"], 1)
            gap(4)
            if not first:
                output_norm_tensor(pe, h)
            gap(2)
            pe.wait_ge(s_["T_ready"], h + 1)
            for b in range(NB):
                mm = nc.tensor.transpose(bank[3][:, b * P:(b + 1) * P], g_["T"][:, b * P:(b + 1) * P], ident)
            mm.then_inc(s_["T_turned"], 1)
            gap(2)
            pe.wait_ge(s_["row_decay_ready"], h + 1)
            pe.wait_ge(s_["v_beta_ready"], h + 1)
            pe.wait_ge(s_["k_gained_ready"], h + 1)
            pe.wait_ge(s_["queries_ready"], h + 1)
            if not first:
                pe.wait_ge(s_["o_rooted"], h)
            for b in range(NB):
                here = slice(b * P, (b + 1) * P)
                mm = nc.tensor.matmul(bank[2][:, here], g_["keys"][:, here], g_["queries"][:, here], start=True, stop=True)
            mm.then_inc(s_["qk_done"], 1)
            for lv in range(LEVELS - 1):
                joins = g_["low_a"] if lv % 2 == 0 else g_["low_b"]
                pe.wait_ge(s_["low_ready"], h * 6 + (lv + 1))
                if lv == 0:
                    pe.wait_ge(s_["U_ready"], h + 1)
                else:
                    pe.wait_ge(s_["UT_ready"], h * 6 + lv)
                for b in range(NB):
                    here = slice(b * P, (b + 1) * P)
                    mm = nc.tensor.matmul(bank[4][:, here], joins[:, here], g_["U"][:, here], start=True, stop=True)
                mm.then_inc(s_["A_done"], 1)
                gap(1)
                pe.wait_ge(s_["A_ready"], h * 6 + (lv + 1))
                for b in range(NB):
                    here = slice(b * P, (b + 1) * P)
                    mm = nc.tensor.matmul(bank[5][:, here], g_["T"][:, here], g_["As"][:, here], start=True, stop=True)
                if lv < LEVELS - 2:
                    for b in range(NB):
                        here = slice(b * P, (b + 1) * P)
                        mm = nc.tensor.matmul(bank[6][:, here], g_["As"][:, here], g_["T"][:, here], start=True, stop=True)
                mm.then_inc(s_["UT_done"], 1)
                gap(2)
            pe.wait_ge(s_["pT_ready"], h + 1)
            pe.wait_ge(s_["q_decayed_ready"], h + 1)
            pe.wait_ge(s_["UT_ready"], h * 6 + 6)
            for b in range(NB):
                here = slice(b * P, (b + 1) * P)
                if b:
                    pe.wait_ge(s_["S_ready"], h * 3 + b)
                    nc.tensor.matmul(bank[7][:, 0:P], g_["keys"][:, here], g_["S"][:, :], start=True, stop=True).then_inc(s_["kS_done"], 1)
                    gap(1)
                    pe.wait_ge(s_["X_ready"], h * 3 + b)
                rhs = g_["X"][:, :] if b else g_["v_beta"][:, here]
                nc.tensor.matmul(bank[2][:, 0:P], g_["U"][:, here], rhs, start=True, stop=True).then_inc(s_["v_done"], 1)
                if b:
                    nc.tensor.matmul(bank[3][:, here], g_["S"][:, :], g_["q_decayed"][:, here], start=True, stop=False)
                if not last and b == 1:
                    key_norm_tensor(pe, g)
                elif not last and b == 2:
                    query_norm_tensor(pe, g)
                gap(1)
                pe.wait_ge(s_["v_ready"], h * 4 + (b + 1))
                if b < NB - 1:
                    nc.tensor.matmul(bank[4][:, 0:P], g_["k_gained"][:, here], g_["v_new"][:, :], start=True, stop=True).then_inc(s_["S_sum_done"], 1)
                mm = nc.tensor.matmul(bank[3][:, here], g_["v_new"][:, :], g_["pT"][:, here], start=b == 0, stop=True)
                if b == NB - 1:
                    mm.then_inc(s_["o_done"], 1)
            gap(40)

        def take_row(act, g, j):
            act.wait_ge(unit_done, g * GROUP_TILES + (seg_g.unit0 + j + 1))
            if not (isinstance(g, int) and g == 0):
                act.wait_ge(s_["conv_done"], g * 3 + (j - 2))
            nc.scalar.activation(pre[j][:, 8:HP], bank[(seg_g.tile0 + j) % 2][:, :], ACT.Identity).then_inc(tile_taken, 1)

        def take_z(act, g):
            act.wait_ge(unit_done, g * GROUP_TILES + (seg_g.unit0 + 4))
            nc.scalar.activation(g_["gate_z"][:, :], bank[(seg_g.tile0 + 3) % 2][:, :], ACT.Identity).then_inc(tile_taken, 1)

        def take_q_mem(act, j):
            act.wait_ge(unit_done, seg_g.unit0 + 8 * GROUP_TILES + j + 1)
            nc.scalar.activation(cols(q_mem, j), bank[(seg_g.tile0 + j) % 2][:, :], ACT.Identity).then_inc(tile_taken, 1)

        def silu_row(act, g, j):
            act.wait_ge(s_["conv_done"], g * 3 + (j + 1))
            nc.scalar.activation(acts[j][:, :], acts[j][:, :], ACT.Silu).then_inc(s_["silu_done"], 1)

        def conv_steps(dve, g, j):
            kind = [8, 16, 0][j]
            dve.wait_ge(tile_taken, g * GROUP_TILES + (seg_g.tile0 + j + 1))
            if j == 1 and not (isinstance(g, int) and g == 0):
                dve.wait_ge(s_["v_turned"], g)

            def tap(k):
                if isinstance(g, int):
                    return param("conv4", (g + kind) * CONV_K + k)
                return param("conv4", g * CONV_K + (kind * CONV_K + k))

            for k in reversed(range(CONV_K)):
                src = pre[j][:, 8 - (CONV_K - 1 - k):HP - (CONV_K - 1 - k)]
                if k == CONV_K - 1:
                    ins = nc.vector.tensor_scalar(acts[j][:, :], src, tap(k), None, ALU.mult)
                else:
                    ins = nc.vector.scalar_tensor_tensor(acts[j][:, :], src, tap(k), acts[j][:, :], ALU.mult, ALU.add)
                if k:
                    ins.then_inc(s_["tap_done"], 1)
                    dve.wait_ge(s_["tap_done"], g * 9 + (3 * j + CONV_K - k))
                else:
                    ins.then_inc(s_["conv_done"], 1)
                yield

        s_["tap_done"] = sem("tap_done")
        o_squares, r_o, z_act = SQ[:, 0:SEQ], SQ[:, SEQ:2 * SEQ], ACC[:, :]

        def key_squares_scalar(act, g):
            act.wait_ge(s_["silu_done"], g * 3 + 1)
            nc.scalar.activation(g_["sq_k"][:, :], acts[0][:, :], ACT.Square).then_inc(s_["keys_squared"], 1)

        def query_squares_scalar(act, g):
            act.wait_ge(s_["silu_done"], g * 3 + 3)
            nc.scalar.activation(g_["sq_q"][:, :], acts[2][:, :], ACT.Square).then_inc(s_["keys_squared"], 1)

        def norm_roots_scalar(act, order, g):
            for i, (dst, src) in enumerate([(g_["r_k"], bank[5]), (g_["r_q"], bank[6])]):
                act.wait_ge(s_["norm_summed"], g * 2 + (i + 1))
                order.link(nc.scalar.activation(dst[:, :], src[:, :], ACT.Ln, bias=eps_col))
            for dst in (g_["r_k"], g_["r_q"]):
                nc.scalar.activation(dst[:, :], dst[:, :], ACT.Exp, scale=-0.5).then_inc(s_["norms_rooted"], 1)

        def output_root_scalar(act, order, n):
            act.wait_ge(s_["o_summed"], n)
            order.link(nc.scalar.activation(r_o, bank[2][:, :], ACT.Ln, bias=eps_col, scale=1.0 / P))
            nc.scalar.activation(r_o, r_o, ACT.Exp, scale=-0.5).then_inc(s_["o_rooted"], 1)

        def output_high_scalar(act, n):
            wait_apart(act, s_["head_ready"], n)
            nc.scalar.activation(cols(MR, n - 1), g_["o_rows"][:, :], ACT.Identity).then_inc(s_["head_high"], 1)

        def head_scalar(act, order, h, g, first, last):
            def take(j):
                take_q_mem(act, j) if last else take_row(act, g, j)

            act.wait_ge(s_["gap_ready"], h + 1)
            nc.scalar.activation(g_["D_E"][:, :], g_["D_E"][:, :], ACT.Exp, scale=-1.0).then_inc(s_["decay_ready"], 1)
            nc.scalar.activation(g_["q_decayed"][:, :], bank[4][:, :], ACT.Exp).then_inc(s_["row_decay_ready"], 1)
            if not first:
                output_root_scalar(act, order, h)
            act.wait_ge(s_["T_turned"], h + 1)
            nc.scalar.activation(g_["U"][:, :], bank[3][:, :], ACT.Identity).then_inc(s_["U_ready"], 1)
            take(0)
            for lv in range(LEVELS - 1):
                act.wait_ge(s_["A_done"], h * 6 + (lv + 1))
                nc.scalar.activation(g_["As"][:, :], bank[4][:, :], ACT.Identity).then_inc(s_["A_ready"], 1)
                if lv == 1 and not first:
                    output_high_scalar(act, h)
                if lv in (2, 4):
                    take(lv // 2)
                if lv == 2 and not last:
                    silu_row(act, g, 0)
                    key_squares_scalar(act, g)
                elif lv == 4 and not last:
                    silu_row(act, g, 1)
            act.wait_ge(tile_taken, h * GROUP_TILES + (seg_g.tile0 + 4))
            nc.scalar.activation(z_act, g_["gate_z"][:, :], ACT.Silu).then_inc(s_["z_ready"], 1)
            if not last:
                silu_row(act, g, 2)
                query_squares_scalar(act, g)
                norm_roots_scalar(act, order, g)
                act.wait_ge(s_["z_ready"], h + 1)
                take_z(act, g)
            else:
                take_q_mem(act, 3)
            act.wait_ge(s_["o_done"], h + 1)
            nc.scalar.activation(o_squares, bank[3][:, :], ACT.Square).then_inc(s_["o_squared"], 1)
            nc.scalar.activation(g_["o_rows"][:, :], bank[3][:, :], ACT.Identity).then_inc(s_["o_copied"], 1)

        def gate_rows_vector(h):
            nc.vector.tensor_tensor(blocks(g_["D_E"][:, :]), over_blocks(tri), over_columns(row4(gcol, h)), ALU.mult).then_inc(s_["gate_rows_ready"], 1)

        def output_vector(dve, order, n):
            o = g_["o_rows"][:, :]
            dve.wait_ge(s_["o_copied"], n)
            dve.wait_ge(s_["o_rooted"], n)
            order.link(nc.vector.scalar_tensor_tensor(o, o, param("gdn_out"), r_o, ALU.mult, ALU.mult))
            dve.wait_ge(s_["z_ready"], n)
            nc.vector.tensor_tensor(o, o, z_act, ALU.mult).then_inc(s_["head_ready"], 1)

        def output_low_vector(dve, n):
            dve.wait_ge(s_["head_high"], n)
            nc.vector.tensor_tensor(cols(ML, n - 1), g_["o_rows"][:, :], cols(MR, n - 1).bitcast(F32), ALU.subtract).then_inc(s_["head_stored"], 1)

        def head_vector(dve, order, h, g, first, last):
            V = nc.vector
            convs = [] if last else [conv_steps(dve, g, j) for j in range(3)]

            def conv(j, n):
                if not last:
                    for _ in range(n):
                        next(convs[j], None)

            D_E, m = g_["D_E"][:, :], g_["lower"][:, :]
            dve.wait_ge(s_["norms_rooted"], h * 2 + 1)
            V.tensor_tensor(g_["keys"][:, :], acts[0][:, :], g_["r_k"][:, :], ALU.mult).then_inc(s_["keys_ready"], 1)
            dve.wait_ge(s_["rows_done"], h + 1)
            order.link(V.tensor_tensor(blocks(D_E), blocks(bank[4][:, :]), over_columns(row4(cum, h)), ALU.subtract))
            V.scalar_tensor_tensor(D_E, D_E, -1.0, D_E, ALU.mult, ALU.max).then_inc(s_["gap_ready"], 1)
            dve.wait_ge(s_["norms_rooted"], h * 2 + 2)
            V.scalar_tensor_tensor(g_["queries"][:, :], acts[2][:, :], QS, g_["r_q"][:, :], ALU.mult, ALU.mult).then_inc(s_["queries_ready"], 1)
            dve.wait_ge(s_["v_turned"], h + 1)
            V.tensor_tensor(blocks(g_["v_beta"][:, :]), blocks(bank[5][:, :]), over_columns(row4(beta, h)), ALU.mult).then_inc(s_["v_beta_ready"], 1)
            dve.wait_ge(s_["kk_done"], h + 1)
            dve.wait_ge(s_["decay_ready"], h + 1)
            order.link(V.tensor_tensor(m, bank[7][:, :], D_E, ALU.mult))
            order.link(V.tensor_tensor(blocks(m), blocks(m), over_columns(row4(beta, h)), ALU.mult))
            order.link(V.tensor_tensor(blocks(g_["low_b"][:, :]), blocks(m), over_blocks(const(LEVEL0)), ALU.mult))
            V.tensor_tensor(blocks(g_["T"][:, :]), over_blocks(ident), blocks(g_["low_b"][:, :]), ALU.subtract).then_inc(s_["T_ready"], 1)
            V.tensor_tensor(blocks(g_["low_a"][:, :]), blocks(m), over_blocks(const(LEVEL0 + 1)), ALU.mult).then_inc(s_["low_ready"], 1)
            dve.wait_ge(s_["k_turned"], h + 1)
            V.tensor_tensor(blocks(g_["k_gained"][:, :]), blocks(bank[6][:, :]), over_columns(row4(k_gain, h)), ALU.mult).then_inc(s_["k_gained_ready"], 1)
            dve.wait_ge(s_["T_ready"], h + 1)
            V.tensor_tensor(blocks(g_["low_b"][:, :]), blocks(m), over_blocks(const(LEVEL0 + 2)), ALU.mult).then_inc(s_["low_ready"], 1)
            dve.wait_ge(s_["row_decay_ready"], h + 1)
            dve.wait_ge(s_["queries_ready"], h + 1)
            V.tensor_tensor(g_["q_decayed"][:, :], g_["q_decayed"][:, :], g_["queries"][:, :], ALU.mult).then_inc(s_["q_decayed_ready"], 1)
            dve.wait_ge(s_["qk_done"], h + 1)
            order.link(V.tensor_tensor(g_["pT"][:, :], bank[2][:, :], D_E, ALU.mult))
            V.tensor_tensor(blocks(g_["pT"][:, :]), blocks(g_["pT"][:, :]), over_blocks(tri), ALU.mult).then_inc(s_["pT_ready"], 1)
            dve.wait_ge(s_["U_ready"], h + 1)
            for lv in range(LEVELS - 1):
                dve.wait_ge(s_["UT_done"], h * 6 + (lv + 1))
                if lv < LEVELS - 2:
                    order.mark(V.tensor_tensor(g_["T"][:, :], g_["T"][:, :], bank[6][:, :], ALU.subtract))
                V.tensor_tensor(g_["U"][:, :], g_["U"][:, :], bank[5][:, :], ALU.subtract).then_inc(s_["UT_ready"], 1)
                if lv < LEVELS - 3:
                    low = g_["low_a"] if lv % 2 == 0 else g_["low_b"]
                    V.tensor_tensor(blocks(low[:, :]), blocks(m), over_blocks(const(LEVEL0 + lv + 3)), ALU.mult).then_inc(s_["low_ready"], 1)
                dve.wait_ge(s_["UT_ready"], h * 6 + (lv + 1))
                if lv < LEVELS - 2:
                    order.sync()
                if lv == 0 and not first:
                    output_vector(dve, order, h)
                if lv == 2 and not first:
                    output_low_vector(dve, h)
                conv(lv // 2, 2)
            if not last:
                gate_rows_vector(g)
            for b in range(NB):
                here = slice(b * P, (b + 1) * P)
                if b:
                    dve.wait_ge(s_["kS_done"], h * 3 + b)
                    V.scalar_tensor_tensor(g_["X"][:, :], bank[7][:, 0:P], col1(neg_beta_decay, h, b), g_["v_beta"][:, here],
                                           ALU.mult, ALU.add).then_inc(s_["X_ready"], 1)
                dve.wait_ge(s_["v_done"], h * 4 + (b + 1))
                V.tensor_copy(g_["v_new"][:, :], bank[2][:, 0:P]).then_inc(s_["v_ready"], 1)
                if b < NB - 1:
                    dve.wait_ge(s_["S_sum_done"], h * 3 + (b + 1))
                    if b == 0:
                        V.tensor_copy(g_["S"][:, :], bank[4][:, 0:P]).then_inc(s_["S_ready"], 1)
                    else:
                        V.scalar_tensor_tensor(g_["S"][:, :], g_["S"][:, :], col1(last_gain, h, b), bank[4][:, 0:P],
                                               ALU.mult, ALU.add).then_inc(s_["S_ready"], 1)
                    dve.wait_ge(s_["S_ready"], h * 3 + (b + 1))

        def gdn_tensor(pe):
            for _ in group_chunks(pe, 0):
                pass
            gates_tensor(pe)
            key_norm_tensor(pe, 0)
            query_norm_tensor(pe, 0)
            head_tensor(pe, 0, 1, True, False)
            with pe.Fori(1, HEADS - 1) as h:
                head_tensor(pe, h, h + 1, False, False)
            head_tensor(pe, HEADS - 1, HEADS, False, True)
            output_norm_tensor(pe, HEADS)

        def gdn_scalar(act, order):
            for j in range(3):
                take_row(act, 0, j)
            take_z(act, 0)
            decays_scalar(act)
            for j in range(3):
                silu_row(act, 0, j)
            key_squares_scalar(act, 0)
            query_squares_scalar(act, 0)
            norm_roots_scalar(act, order, 0)
            head_scalar(act, order, 0, 1, True, False)
            with act.Fori(1, HEADS - 1) as h:
                order.enter(h, 3, 1)
                head_scalar(act, order, h, h + 1, False, False)
                order.leave(HEADS - 2)
            head_scalar(act, order, HEADS - 1, HEADS, False, True)
            output_root_scalar(act, order, HEADS)
            output_high_scalar(act, HEADS)

        def gdn_vector(dve, order):
            for j in range(3):
                order.link(nc.vector.memset(pre[j][:, 0:8], 0.0))
            for j in range(3):
                for _ in conv_steps(dve, 0, j):
                    pass
            decays_vector(dve, order)
            gate_rows_vector(0)
            head_vector(dve, order, 0, 1, True, False)
            with dve.Fori(1, HEADS - 1) as h:
                order.enter(h, DVE_PER_HEAD, 1)
                head_vector(dve, order, h, h + 1, False, False)
                order.leave(HEADS - 2)
            head_vector(dve, order, HEADS - 1, HEADS, False, True)
            output_vector(dve, order, HEADS)
            output_low_vector(dve, HEADS)
            dve.wait_ge(s_["head_stored"], HEADS)

        DVE_PER_HEAD = 11

        M_SCALE = float(P) ** -0.5
        mp = [at(f"mp{i}", (125 + 24 + 4 * i) * KB, NB * MEM) for i in range(2)]
        mpT = [at(f"mpT{i}", (125 + 32 + 2 * i) * KB, SEQ) for i in range(2)]
        mst = [at(f"mst{i}", (125 + 36) * KB + 64 * i, 16) for i in range(2)]
        m_scored, m_max, m_neg, m_exp, m_inv, m_normed, m_turned, mT_act, mT_dve, m_out, m_high, m_stored = (
            sem(n) for n in ("m_scored m_max m_neg m_exp m_inv m_normed m_turned mT_act mT_dve "
                             "m_out m_high m_stored").split())
        M_BANKS = [(3, 4), (1, 2)]

        def mem_scores_tensor(pe, h):
            pe.wait_ge(tile_taken, seg_g.tile0 + HEADS * GROUP_TILES + MEM_HEADS)
            for b in range(NB):
                mm = nc.tensor.matmul(bank[M_BANKS[h % 2][b // 2]][:, b % 2 * MEM:(b % 2 + 1) * MEM],
                                      q_mem[:, h * SEQ + b * P:h * SEQ + (b + 1) * P],
                                      mem_keys[:, h * MEM:(h + 1) * MEM], start=True, stop=True)
                if b % 2:
                    mm.then_inc(m_scored, 1)

        def mem_attend_tensor(pe):
            pe.wait_ge(s_["o_copied"], HEADS)
            mem_scores_tensor(pe, 0)
            pe.wait_ge(s_["o_rooted"], HEADS)
            mem_scores_tensor(pe, 1)
            for h in range(MEM_HEADS):
                for b in range(NB):
                    pe.wait_ge(m_normed, h * NB + b + 1)
                    for c in range(2):
                        mm = nc.tensor.transpose(bank[5 + c][:, b * P:(b + 1) * P], mp[h % 2][:, b * MEM + c * P:b * MEM + (c + 1) * P], ident)
                mm.then_inc(m_turned, 1)
                if h + 2 < MEM_HEADS:
                    mem_scores_tensor(pe, h + 2)
                if h:
                    pe.wait_ge(m_stored, h)
                for c, ready in ((0, mT_act), (1, mT_dve)):
                    pe.wait_ge(ready, h + 1)
                    mm = nc.tensor.matmul(bank[7][:, :], mem_values[:, c * SEQ + h * P:c * SEQ + (h + 1) * P], mpT[c][:, :],
                                          start=c == 0, stop=c == 1)
                mm.then_inc(m_out, 1)

        def mem_exp_scalar(act, h):
            for b in range(NB):
                act.wait_ge(m_neg, h * 2 + b // 2 + 1)
                nc.scalar.activation(mp[h % 2][:, b * MEM:(b + 1) * MEM], bank[M_BANKS[h % 2][b // 2]][:, b % 2 * MEM:(b % 2 + 1) * MEM],
                                     ACT.Exp, bias=mst[h % 2][:, 4 + b:5 + b], scale=M_SCALE,
                                     accum_out=mst[h % 2][:, 8 + b:9 + b]).then_inc(m_exp, 1)

        def mem_attend_scalar(act):
            mem_exp_scalar(act, 0)
            mem_exp_scalar(act, 1)
            for h in range(MEM_HEADS):
                act.wait_ge(m_turned, h + 1)
                nc.scalar.activation(mpT[0][:, :], bank[5][:, :], ACT.Identity).then_inc(mT_act, 1)
                if h + 2 < MEM_HEADS:
                    mem_exp_scalar(act, h + 2)
                act.wait_ge(m_out, h + 1)
                nc.scalar.activation(cols(MR, h + 8), bank[7][:, :], ACT.Identity).then_inc(m_high, 1)

        def mem_maxima_vector(dve, h):
            st = mst[h % 2]
            for j in range(2):
                dve.wait_ge(m_scored, h * 2 + j + 1)
                nc.vector.tensor_reduce(st[:, 2 * j:2 * j + 2], bank[M_BANKS[h % 2][j]][:, :].rearrange("p (b m) -> p b m", b=2),
                                        AX.X, ALU.max).then_inc(m_max, 1)
                dve.wait_ge(m_max, h * 2 + j + 1)
                nc.vector.tensor_scalar(st[:, 4 + 2 * j:6 + 2 * j], st[:, 2 * j:2 * j + 2], -M_SCALE, None, ALU.mult).then_inc(m_neg, 1)

        def mem_normalise_vector(dve, h):
            st = mst[h % 2]
            dve.wait_ge(m_exp, h * NB + NB)
            nc.vector.reciprocal(st[:, 12:16], st[:, 8:12]).then_inc(m_inv, 1)
            dve.wait_ge(m_inv, h + 1)
            for b in range(NB):
                here = mp[h % 2][:, b * MEM:(b + 1) * MEM]
                nc.vector.tensor_scalar(here, here, st[:, 12 + b:13 + b], None, ALU.mult).then_inc(m_normed, 1)

        def mem_attend_vector(dve):
            mem_maxima_vector(dve, 0)
            mem_maxima_vector(dve, 1)
            mem_normalise_vector(dve, 0)
            for h in range(MEM_HEADS):
                dve.wait_ge(m_turned, h + 1)
                nc.vector.tensor_copy(mpT[1][:, :], bank[6][:, :]).then_inc(mT_dve, 1)
                if h + 1 < MEM_HEADS:
                    mem_normalise_vector(dve, h + 1)
                if h + 2 < MEM_HEADS:
                    mem_maxima_vector(dve, h + 2)
                dve.wait_ge(m_high, h + 1)
                nc.vector.tensor_tensor(cols(ML, h + 8), bank[7][:, :], cols(MR, h + 8).bitcast(F32), ALU.subtract).then_inc(m_stored, 1)

        x_again = sem("x_again")
        residual_ready = sem("residual_ready")
        y_normed = sem("y_normed")
        JOIN = {"mix": 0, "ffn": 1}
        JOINED = {"in1": "mix", "pw1": "ffn"}

        def unit_after(seg, n):
            return n * seg.per_tile + (seg.unit0 + seg.per_tile)

        def keep_scalar(act, seg, norm):
            def turn(i):
                for j in range(2):
                    n = i * 2 + j
                    split_ahead(act, seg, i, 4, 2 * j + 2, 2)
                    act.wait_ge(unit_done, unit_after(seg, n))
                    src = bank[(seg.tile0 + j) % 2][:, :]
                    square_tile(act, norm, n, j, src)
                    nc.scalar.activation(cols(Y, n), src, ACT.Identity).then_inc(tile_taken, 1)

            with act.Fori(0, DT // 2 - 1) as i:
                turn(i)
            turn(DT // 2 - 1)
            root(act, norm)

        def keep_vector(dve, order, norm):
            clear_sum(dve, order, norm)
            with dve.Fori(0, DT // 2) as i:
                for j in range(2):
                    add_squares(dve, norm, i * 2 + j, j)

        def join_scalar(act, norm, nxt, gain):
            base_n = DT * JOIN[norm]
            with act.Fori(0, DT // 2) as i:
                for j in range(2):
                    n = i * 2 + j
                    wait_apart(act, residual_ready, n + (base_n + 1))
                    high_part(act, nxt, n, cols(XR, n), cols(hT, n), param(gain, n))
                    square_tile(act, nxt, n, j, cols(hT, n))
            root(act, nxt)

        def join_vector(dve, order, norm, post_gain, nxt, gain):
            base_n = DT * JOIN[norm]
            dve.wait_ge(norm_ready, NORM[norm] + 1)
            clear_sum(dve, order, nxt)

            def norm_pair(i):
                for j in range(2):
                    n = i * 2 + j
                    nc.vector.scalar_tensor_tensor(cols(Y, n), cols(Y, n), param(post_gain, n), R[:, :], ALU.mult, ALU.mult).then_inc(y_normed, 1)

            def low_pair(i):
                for j in range(2):
                    n = i * 2 + j
                    low_part(dve, nxt, n, cols(XL, n), cols(hT, n), cols(XR, n), param(gain, n))
                    add_squares(dve, nxt, n, j)

            norm_pair(0)
            with dve.Fori(0, DT // 2 - 1) as i:
                norm_pair(i + 1)
                low_pair(i)
            low_pair(DT // 2 - 1)

        def join_gpsimd(pool, norm):
            base_n = DT * JOIN[norm]
            if norm == "mix":
                pool.wait_ge(x_again, 16)
            with pool.Fori(0, DT) as n:
                pool.wait_ge(y_normed, n + (base_n + 1))
                nc.gpsimd.tensor_tensor(cols(hT, n), cols(hT, n), cols(Y, n), ALU.add).then_inc(residual_ready, 1)

        def stream_scalar(act, seg, nxt, inp, gain):
            def turn(i):
                for j in range(2):
                    n = i * 2 + j
                    split_ahead(act, seg, i, 2 * seg.per_tile, seg.per_tile * j + 2, seg.per_tile)
                    wait_apart(act, tile_taken, n + (seg.tile0 + 1))
                    if inp:
                        high_part(act, inp, n, cols(XR, n), cols(hT, n), param(gain, n))
                    square_tile(act, nxt, n, j, cols(hT, n))

            with act.Fori(0, DT // 2 - 1) as i:
                turn(i)
            turn(DT // 2 - 1)
            root(act, nxt)

        def stream_vector(dve, order, seg, nxt, inp, gain, bias=None):
            clear_sum(dve, order, nxt)
            with dve.Fori(0, DT // 2) as i:
                for j in range(2):
                    n = i * 2 + j
                    dve.wait_ge(unit_done, unit_after(seg, n))
                    src = bank[(seg.tile0 + j) % 2][:, :]
                    if bias:
                        ins = nc.vector.scalar_tensor_tensor(cols(hT, n), src, param(bias, n), cols(hT, n), ALU.add, ALU.add)
                    else:
                        ins = nc.vector.tensor_tensor(cols(hT, n), src, cols(hT, n), ALU.add)
                    ins.then_inc(tile_taken, 1)
                    if inp:
                        dve.wait_ge(tile_taken, n + (seg.tile0 + 1))
                        low_part(dve, inp, n, cols(XL, n), cols(hT, n), cols(XR, n), param(gain, n))
                    add_squares(dve, nxt, n, j)

        gate_silu, mid_ready, mid_high, mid_low = (sem(n) for n in ("gate_silu", "mid_ready", "mid_high", "mid_low"))
        f_gate = at("f_gate", 169 * KB, SEQ)
        f_up = at("f_up", 171 * KB, SEQ)
        f_mid = at("f_mid", 173 * KB, SEQ)

        def ffn_tensor(pe, which, inp):
            seg, down = SEG[f"in{which}"], SEG[f"down{which}"]
            tiles(pe, seg, lambda k: X_R[:, k], lambda k: X_L[:, k], (input_ready, INPUT[inp]), lambda: total(pe, inp), wide=True)
            tiles(pe, down, lambda k: M_R[:, k], lambda k: M_L[:, k], (mid_low, FT * (which - 1)), after_wide=True)

        def ffn_scalar(act, which):
            seg, done = SEG[f"in{which}"], FT * (which - 1)
            def turn(i):
                for p in range(2):
                    n = i * 2 + p
                    split_ahead(act, seg, i, 4, 2 * p + 2)
                    act.wait_ge(tile_taken, n * 2 + (seg.tile0 + 1))
                    nc.scalar.activation(f_gate[:, :], f_gate[:, :], ACT.Silu).then_inc(gate_silu, 1)
                    split_ahead(act, seg, i, 4, 2 * p + 3)
                    wait_apart(act, mid_ready, n + (done + 1))
                    nc.scalar.activation(cols(MR, n), f_mid[:, :], ACT.Identity).then_inc(mid_high, 1)

            with act.Fori(0, FT // 2 - 1) as i:
                turn(i)
            turn(FT // 2 - 1)

        def ffn_vector(dve, which, norm):
            seg, done = SEG[f"in{which}"], FT * (which - 1)
            dve.wait_ge(norm_ready, NORM[norm] + 1)
            with dve.Fori(0, FT // 2) as i:
                for p in range(2):
                    n = i * 2 + p
                    dve.wait_ge(unit_done, n * 2 + (seg.unit0 + 1))
                    nc.vector.tensor_tensor(f_gate[:, :], bank_of(seg, 2 * p)[:, :], R[:, :], ALU.mult).then_inc(tile_taken, 1)
                    dve.wait_ge(unit_done, n * 2 + (seg.unit0 + 2))
                    nc.vector.tensor_tensor(f_up[:, :], bank_of(seg, 2 * p + 1)[:, :], R[:, :], ALU.mult).then_inc(tile_taken, 1)
                    dve.wait_ge(tile_taken, n * 2 + (seg.tile0 + 2))
                    dve.wait_ge(gate_silu, n + (done + 1))
                    nc.vector.tensor_tensor(f_mid[:, :], f_gate[:, :], f_up[:, :], ALU.mult).then_inc(mid_ready, 1)
                    dve.wait_ge(mid_high, n + (done + 1))
                    nc.vector.tensor_tensor(cols(ML, n), f_mid[:, :], cols(MR, n).bitcast(F32), ALU.subtract).then_inc(mid_low, 1)

        PE_TAPS = 10
        ROW = SEQ + PAD + 2
        c_row = [at(f"c_row{j}", (81 + 3 * j) * KB, ROW) for j in range(2)]
        c_a = at("c_a", (81 + 6) * KB, SEQ)
        c_b = at("c_b", (81 + 8) * KB, SEQ)
        c_odd = at("c_odd", (81 + 10) * KB, SEQ)
        c_t = [at(f"c_t{j}", (125 + 20 + 4 * j) * KB, 2 * SEQ) for j in range(2)]
        diag = [at(f"diag{j}", (125 + 24 + 5 * j) * KB, PE_TAPS * P) for j in range(2)]
        glu_gate, glu_ready, diag_ready, taps_done, tap_added, odd_added, taps_joined, mean_added, mean_done, mean_ready, centred, ln_scaled, ln_silu = (
            sem(n) for n in "glu_gate glu_ready diag_ready taps_done tap_added odd_added taps_joined mean_added mean_done mean_ready centred ln_scaled ln_silu".split())

        def conv_bank(seg, c):
            return bank[(seg.tile0 + c) % 2 if c < 2 else 4 + c]

        def conv_tensor(pe):
            seg = SEG["pw1"]
            u0, t0 = seg.unit0, seg.tile0

            def taps(n, j):
                pe.wait_ge(diag_ready, n + 1)
                pe.wait_ge(glu_ready, n + 1)
                for k in range(PE_TAPS):
                    mm = nc.tensor.matmul(bank[4 + j][:, :], diag[j][:, k * P:(k + 1) * P], c_row[j][:, 2 + k:2 + k + SEQ],
                                          start=k == 0, stop=k == PE_TAPS - 1)
                mm.then_inc(taps_done, 1)

            def turn(i):
                for j in range(2):
                    for half in range(2):
                        c = 2 * j + half
                        opening = isinstance(i, int) and c == 0
                        if not isinstance(i, int):
                            pe.wait_ge(tile_taken, i * 4 + (t0 + c - 3))
                        elif c < 2:
                            pe.wait_ge(tile_taken, t0 + c - 1)
                        products(pe, seg, i * 4 + (u0 + c), (u0 + c) % 2, 0, conv_bank(seg, c)[:, :],
                                 lambda k: X_R[:, k], lambda k: X_L[:, k], True, True,
                                 ready=(input_ready, INPUT["h2"]) if opening else None)
                        if opening:
                            total(pe, "h2")
                    if not isinstance(i, int) or j:
                        taps(i * 2 + (j - 1), 1 - j)

            turn(0)
            with pe.Fori(1, DT // 2) as i:
                turn(i)
            taps(DT - 1, 1)
            pe.wait_ge(mean_added, DT)
            nc.tensor.matmul(bank[3][:, :], ones, ACC[:, :], start=True, stop=True).then_inc(mean_done, 1)
            first = DT * NORM["var"]
            for n in range(DT):
                pe.wait_ge(squared, first + n + 1)
                nc.tensor.matmul(bank[2][:, :], ones, SQ[:, n % 2 * SEQ:(n % 2 + 1) * SEQ], start=n == 0, stop=n == DT - 1).then_inc(summed, 1)
            pe.wait_ge(summed, first + DT)
            nc.tensor.sem_inc(total_done, 1)
            tiles(pe, SEG["pw2"], lambda k: M_R[:, k], lambda k: M_L[:, k], (input_ready, INPUT["conv"]))

        def conv_scalar(act):
            seg = SEG["pw1"]
            def turn(i):
                for j in range(2):
                    n = i * 2 + j
                    split_ahead(act, seg, i, 4, 2 * j + 2, 2)
                    wait_apart(act, tile_taken, i * 4 + (seg.tile0 + 2 * j + 1))
                    nc.scalar.activation(c_b[:, :], c_b[:, :], ACT.Sigmoid, bias=param("pw1_b", n)).then_inc(glu_gate, 1)
                    if not isinstance(i, int) or i:
                        wait_apart(act, taps_done, n - 1)
                    for k in range(PE_TAPS):
                        ins = nc.scalar.activation(diag[j][:, k * P:(k + 1) * P], ident, ACT.Identity, scale=param("conv31", n * TAPS + k))
                    ins.then_inc(diag_ready, 1)

            turn(0)
            with act.Fori(1, DT // 2 - 1) as i:
                turn(i)
            turn(DT // 2 - 1)
            with act.Fori(0, DT // 2) as i:
                for j in range(2):
                    act.wait_ge(centred, i * 2 + (j + 1))
                    square_tile(act, "var", i * 2 + j, j, cols(Y, i * 2 + j))
            root(act, "var")
            for n in range(DT):
                tmp = c_t[n % 4 // 2][:, n % 2 * SEQ:(n % 2 + 1) * SEQ]
                act.wait_ge(ln_scaled, n + 1)
                nc.scalar.activation(tmp, tmp, ACT.Silu, bias=param("ln_b", n), scale=param("ln_g", n)).then_inc(ln_silu, 1)
                act.wait_ge(ln_silu, n + 1)
                nc.scalar.activation(cols(MR, n), tmp, ACT.Identity).then_inc(input_high, 1)
            stream_scalar(act, SEG["pw2"], "h3", "h3", "ffn1")

        def conv_vector(dve, order):
            seg = SEG["pw1"]
            V = nc.vector
            for j in range(2):
                order.link(V.memset(c_row[j][:, 0:PAD + 2], 0.0))
            dve.wait_ge(norm_ready, NORM["h2"] + 1)
            clear_sum_now(dve, order, "h2")
            N = TAPS - PE_TAPS

            def turn(i):
                for j in range(2):
                    n = i * 2 + j
                    row, y = c_row[j], cols(Y, n)
                    dve.wait_ge(unit_done, n * 2 + (seg.unit0 + 1))
                    V.tensor_tensor(c_b[:, :], conv_bank(seg, 2 * j)[:, :], R[:, :], ALU.mult).then_inc(tile_taken, 1)
                    dve.wait_ge(unit_done, n * 2 + (seg.unit0 + 2))
                    V.tensor_tensor(c_a[:, :], conv_bank(seg, 2 * j + 1)[:, :], R[:, :], ALU.mult).then_inc(tile_taken, 1)
                    dve.wait_ge(tile_taken, n * 2 + (seg.tile0 + 2))
                    dve.wait_ge(glu_gate, n + 1)
                    V.scalar_tensor_tensor(row[:, PAD + 2:ROW], c_a[:, :], param("pw1_a", n), c_b[:, :], ALU.add, ALU.mult).then_inc(glu_ready, 1)
                    dve.wait_ge(glu_ready, n + 1)
                    for m in range(N):
                        k = PE_TAPS + m
                        src, w, into = row[:, 2 + k:2 + k + SEQ], param("conv31", n * TAPS + k), (y, c_odd[:, :])[m % 2]
                        if m >= 2:
                            dve.wait_ge(tap_added, n * N + (m - 1))
                        if m == 0:
                            ins = V.tensor_scalar(into, src, w, param("dw_b", n), ALU.mult, ALU.add)
                        elif m == 1:
                            ins = V.tensor_scalar(into, src, w, None, ALU.mult)
                        else:
                            ins = V.scalar_tensor_tensor(into, src, w, into, ALU.mult, ALU.add)
                        ins.then_inc(tap_added, 1)
                    dve.wait_ge(tap_added, n * N + N)
                    V.tensor_tensor(y, y, c_odd[:, :], ALU.add).then_inc(odd_added, 1)
                    dve.wait_ge(taps_done, n + 1)
                    dve.wait_ge(odd_added, n + 1)
                    V.tensor_tensor(y, y, bank[4 + j][:, :], ALU.add).then_inc(taps_joined, 1)
                    dve.wait_ge(taps_joined, n + 1)
                    V.tensor_tensor(ACC[:, :], ACC[:, :], y, ALU.add).then_inc(mean_added, 1)
                    dve.wait_ge(mean_added, n + 1)

            with dve.Fori(0, DT // 2) as i:
                turn(i)
            dve.wait_ge(mean_done, 1)
            V.tensor_scalar(R[:, :], bank[3][:, :], 1.0 / D, None, ALU.mult).then_inc(mean_ready, 1)
            dve.wait_ge(mean_ready, 1)
            with dve.Fori(0, DT) as n:
                V.tensor_tensor(cols(Y, n), cols(Y, n), R[:, :], ALU.subtract).then_inc(centred, 1)
            dve.wait_ge(norm_ready, NORM["var"] + 1)

            def scale(n, j):
                V.tensor_tensor(c_t[j // 2][:, j % 2 * SEQ:(j % 2 + 1) * SEQ], cols(Y, n), R[:, :], ALU.mult).then_inc(ln_scaled, 1)

            def low(n, j):
                dve.wait_ge(input_high, n + (INPUT["conv"] + 1))
                V.tensor_tensor(cols(ML, n), c_t[j // 2][:, j % 2 * SEQ:(j % 2 + 1) * SEQ], cols(MR, n).bitcast(F32), ALU.subtract).then_inc(input_ready, 1)

            for n in range(4):
                scale(n, n)
            for n in range(DT):
                low(n, n % 4)
                if n + 4 < DT:
                    dve.wait_ge(input_ready, INPUT["conv"] + n + 1)
                    scale(n + 4, n % 4)
            stream_vector(dve, order, SEG["pw2"], "h3", "h3", "ffn1", bias="pw2_b")

        def clear_sum_now(dve, order, norm):
            dve.wait_ge(total_done, NORM[norm] + 1)
            order.link(nc.vector.memset(ACC[:, :], 0.0))

        seg_a = SEG["kvq"]
        q_in_R = [MR[:, k * SEQ:(k + 1) * SEQ] for k in range(DT)]
        q_in_L = [ML[:, k * SEQ:(k + 1) * SEQ] for k in range(DT)]
        phi1 = at("phi1", 169 * KB, 2 * L_CMP * 64)
        behind_r, behind_l = (81 + 32) * KB, (125 + 32) * KB
        k_rows = [at(f"k_rows{i}", behind_r + 2 * i * KB, SEQ) for i in range(2)]
        v_rows = [at(f"v_rows{i}", behind_r + (4 + 2 * i) * KB, SEQ) for i in range(2)]
        v_tok = [at(f"v_tok{i}", behind_r + (8 + 2 * i) * KB, SEQ) for i in range(2)]
        k_cmp = at("k_cmp", behind_l, 32)
        v_cmp = at("v_cmp", behind_l + 128, P, parts=32)
        gates = at("gates", behind_l + 640, NB * 48)
        g_rows = at("g_rows", behind_l + 2 * KB, SEQ)
        c_rows = [at(f"c_rows{i}", behind_l + (4 + 2 * i) * KB, SEQ) for i in range(2)]
        windows = [at(f"windows{i}", (32 + 4 * i) * KB, L_CMP * 32) for i in range(2)]
        hidden = at("hidden", 40 * KB, 64)
        KV_TILES = [c_rows[0], c_rows[1], k_rows[0], k_rows[1], v_rows[0], v_rows[1]]
        phi_loaded, phi2_loaded, windows_ready, hid_done, hid_ready, cmp_done, cmp_ready, vt_turned, vt_ready, gate_sig, gate_turned, gate_ready = (
            sem(n) for n in ("phi_loaded phi2_loaded windows_ready hid_done hid_ready cmp_done cmp_ready "
                             "vt_turned vt_ready gate_sig gate_turned gate_ready").split())
        phi2 = at("phi2", low + 8 * KB + 32, 2 * P)

        def kv_bank(j):
            return bank[(seg_a.tile0 + j) % 2 if j % 4 < 2 else 3 + j % 4]

        def kv_tensor(pe):
            xr, xl = (lambda k: X_R[:, k]), (lambda k: X_L[:, k])
            for j in range(6):
                if j not in (2, 3):
                    pe.wait_ge(tile_taken, seg_a.tile0 + (j - 1 if j < 2 else j - 3))
                products(pe, seg_a, seg_a.unit0 + j, (seg_a.unit0 + j) % 2, 0, kv_bank(j)[:, :], xr, xl, True, True,
                         ready=None if j else (input_ready, INPUT["kv"]))
                if j == 0:
                    total(pe, "h4")
            pe.wait_ge(input_ready, INPUT["q"] + DT)
            pe.wait_ge(tile_taken, seg_a.tile0 + 3)
            products(pe, seg_a, seg_a.unit0 + 6, (seg_a.unit0 + 6) % 2, 0, kv_bank(6)[:, :],
                     lambda k: q_in_R[k], lambda k: q_in_L[k], True, True)
            for i in range(2):
                pe.wait_ge(tile_taken, seg_a.tile0 + 6)
                for b in range(NB):
                    mm = nc.tensor.transpose(bank[3 + i][:, b * P:(b + 1) * P], v_rows[i][:, b * P:(b + 1) * P], ident)
                mm.then_inc(vt_turned, 1)
            pe.wait_ge(phi_loaded, 16)
            pe.wait_ge(phi2_loaded, 16)
            for i in range(2):
                pe.wait_ge(windows_ready, 2 * i + 2)
                for g in range(2):
                    rows = slice(64 * g, 64 * g + 64)
                    for l in range(L_CMP):
                        w = phi1[rows, (i * L_CMP + l) * 64:(i * L_CMP + l + 1) * 64]
                        mm = nc.tensor.matmul(bank[5 + i][rows, 0:32], w, windows[i][rows, l * 32:(l + 1) * 32],
                                              start=l == 0, stop=l == L_CMP - 1)
                mm.then_inc(hid_done, 1)
            pe.wait_ge(hid_ready, 2)
            nc.tensor.matmul(bank[7][:, 0:32], phi2[:, 0:P], hidden[:, 0:32], start=True, stop=True)
            nc.tensor.matmul(bank[7][0:32, 128:256], hidden[:, 32:64], phi2[:, P:2 * P], start=True, stop=True).then_inc(cmp_done, 1)
            pe.wait_ge(gate_sig, 1)
            for b in range(NB):
                mm = nc.tensor.transpose(bank[2][:, b * 48:(b + 1) * 48], g_rows[0:48, b * P:(b + 1) * P], ident[0:48, 0:48])
            mm.then_inc(gate_turned, 1)

        def kv_scalar(act):
            act.wait_ge(unit_done, seg_a.unit0)
            for n in range(DT):
                high_part(act, "q", n, q_in_R[n], cols(hT, n), param("b_norm", n))
            for i in range(2):
                act.wait_ge(hid_done, i + 1)
                nc.scalar.activation(hidden[:, i * 32:(i + 1) * 32], bank[5 + i][:, 0:32], ACT.Silu).then_inc(hid_ready, 1)
            act.wait_ge(tile_taken, seg_a.tile0 + 7)
            nc.scalar.activation(g_rows[0:48, :], g_rows[0:48, :], ACT.Sigmoid).then_inc(gate_sig, 1)

        def kv_vector(dve, order):
            V = nc.vector
            dve.wait_ge(norm_ready, NORM["h4"] + 1)
            low_parts = iter(range(DT))
            for j in range(6):
                dve.wait_ge(unit_done, seg_a.unit0 + j + 1)
                V.tensor_tensor(KV_TILES[j][:, :], kv_bank(j)[:, :], R[:, :], ALU.mult).then_inc(tile_taken, 1)
                for n in (next(low_parts, None), next(low_parts, None)):
                    if n is not None:
                        low_part(dve, "q", n, q_in_L[n], cols(hT, n), q_in_R[n], param("b_norm", n))
            dve.wait_ge(tile_taken, seg_a.tile0 + 6)
            dve.wait_ge(unit_done, seg_a.unit0 + 7)
            V.tensor_tensor(g_rows[0:48, :], kv_bank(6)[0:48, :], R[0:48, :], ALU.mult).then_inc(tile_taken, 1)
            for i in range(2):
                order.link(V.memset(windows[i][:, :], 0.0))
                out_w = windows[i][:, :].rearrange("p (l n) -> p l n", l=L_CMP)
                rows = c_rows[i][:, :].rearrange("p (n s) -> p s n", s=STRIDE)
                for half in range(2):
                    pos = params[:, PARAMS["pos_k" if i == 0 else "pos_v"][0] + half * STRIDE:][:, 0:STRIDE]
                    V.tensor_tensor(out_w[:, half * STRIDE:(half + 1) * STRIDE, 0:N_CMP], rows[:, :, half:half + N_CMP],
                                    over_columns(pos, N_CMP), ALU.add).then_inc(windows_ready, 1)
            for i in range(2):
                dve.wait_ge(vt_turned, i + 1)
                V.tensor_copy(v_tok[i][:, :], bank[3 + i][:, :]).then_inc(vt_ready, 1)
            dve.wait_ge(cmp_done, 1)
            V.tensor_copy(k_cmp[:, :], bank[7][:, 0:32]).then_inc(cmp_ready, 1)
            V.tensor_copy(v_cmp[:, :], bank[7][0:32, 128:256]).then_inc(cmp_ready, 1)
            dve.wait_ge(gate_turned, 1)
            V.tensor_copy(gates[:, :], bank[2][:, 0:NB * 48]).then_inc(gate_ready, 1)
            dve.wait_ge(gate_ready, 1)

        PIECES = [[(3, 0)], [(2, 512), (0, 896)], [(1, 1024)]]
        GROUPS = [(0, 512), (512, 1024), (1024, 1280)]
        WHERE = {b: col for piece in PIECES for b, col in piece}
        PCOLS = 1280
        TURNED = [[(0, 0)], [(1, 512), (3, 896)], [(2, 1024)]]
        KEYS_AT = {kb: col for piece in TURNED for kb, col in piece}
        KEY_SCALE = 0.125
        ITEMS = [(j, g, r) for j in range(2) for g in range(2) for r in range(3)]
        N_ITEMS = len(ITEMS)
        xr0 = 16 * KB
        qT = [at(f"qT{j}", xr0 + 2 * j * KB, SEQ) for j in range(2)]
        alibi = [at(f"alibi{g}", xr0 + (4 + 2 * g) * KB, SEQ) for g in range(2)]
        alibi_c = [at(f"alibi_c{g}", xr0 + 8 * KB + 512 * g, P) for g in range(2)]
        Pc = at("Pc", xr0 + 9 * KB, P)
        PcT = at("PcT", xr0 + 29 * KB, SEQ, parts=32)
        stats = at("stats", xr0 + 13 * KB, 48)
        c_max = at("c_max", xr0 + 13 * KB + 192, 8)
        Pr = [at(f"Pr{m}", xr0 + (14 + 5 * m) * KB, PCOLS) for m in range(2)]
        PT = at("PT", xr0 + 24 * KB, PCOLS)
        (alibi_ready, c_scored, scores_read, piece_read, c_maxed, c_shifted, probs_done, c_summed, c_turned, cT_ready, scored,
         turned, pT_act, pT_dve, inverse, weight_ready, probs_scaled, pair_done, y_high, y_low) = (
            sem(n) for n in ("alibi_ready c_scored scores_read piece_read c_maxed c_shifted probs_done c_summed c_turned cT_ready "
                             "scored turned pT_act pT_dve inverse weight_ready probs_scaled pair_done y_high y_low").split())
        q_units, q_tiles = seg_a.unit0 + 7, seg_a.tile0 + 7
        TURNS = NQ // 2

        def item(idx):
            return ITEMS[idx % N_ITEMS]

        def nth(i, idx):
            return i * N_ITEMS + idx

        def s_nth(i, idx):
            return i * 8 + (idx // N_ITEMS * 8 + sum(1 for it in ITEMS[:idx % N_ITEMS] if it[2]))

        def c_nth(i, idx):
            return i * 4 + (idx // N_ITEMS * 4 + sum(1 for it in ITEMS[:idx % N_ITEMS] if not it[2]))

        def s_parity(idx):
            return sum(1 for it in ITEMS[:idx % N_ITEMS] if it[2]) % 2

        def stat(idx, what):
            at0 = 16 * (idx % 3) + 4 * what
            return stats[:, at0:at0 + 4]

        def exists(i, idx):
            return idx < N_ITEMS or not (isinstance(i, int) and i == TURNS - 1)

        def pair_tensor(pe, i, j):
            pe.wait_ge(tile_taken, i * 2 + (q_tiles + j))
            products(pe, seg_a, i * 2 + (q_units + j), (q_units + j) % 2, 0, bank[0][:, :],
                     lambda k: q_in_R[k], lambda k: q_in_L[k], True, True)

        def scores_tensor(pe, i, idx):
            j, g, r = item(idx)
            rows = slice(64 * g, 64 * g + 64)
            pe.wait_ge(tile_taken, i * 2 + (q_tiles + idx // N_ITEMS * 2 + j + 1))
            pe.wait_ge(scores_read, nth(i, idx) + 1)
            if r == 0:
                for b in range(NB):
                    mm = nc.tensor.matmul(bank[2][:, b * 32:(b + 1) * 32], qT[j][rows, b * P:(b + 1) * P], k_cmp[rows, :],
                                          start=True, stop=True)
                mm.then_inc(c_scored, 1)
                return
            for n, pieces in enumerate(PIECES):
                for b, col in pieces:
                    at0 = col - GROUPS[n][0]
                    mm = nc.tensor.matmul(bank[2 + n][:, at0:at0 + (b + 1) * P], qT[j][rows, b * P:(b + 1) * P],
                                          k_rows[r - 1][rows, 0:(b + 1) * P], start=True, stop=True)
                mm.then_inc(scored, 1)

        def turn_probs_tensor(pe, i, idx):
            pe.wait_ge(probs_scaled, nth(i, idx) + 1)
            if item(idx)[2] == 0:
                for b in range(NB):
                    mm = nc.tensor.transpose(bank[5][0:32, b * P:(b + 1) * P], Pc[:, b * 32:(b + 1) * 32], ident)
                mm.then_inc(c_turned, 1)
                return
            P_ = Pr[s_parity(idx)]
            for pieces, (first, _), into in zip(TURNED, GROUPS, (bank[5], bank[6], bank[1])):
                for kb, col in pieces:
                    for b in range(kb, NB):
                        at0 = col - first + (b - kb) * P
                        c = WHERE[b] + kb * P
                        mm = nc.tensor.transpose(into[:, at0:at0 + P], P_[:, c:c + P], ident)
                mm.then_inc(turned, 1)

        def weigh_tensor(pe, i, idx):
            j, g, r = item(idx)
            rows = slice(64 * g, 64 * g + 64)
            if r == 0:
                if g == 0:
                    pe.wait_ge(y_low, i * 2 + (j + 1))
                pe.wait_ge(cT_ready, c_nth(i, idx) + 1)
                nc.tensor.matmul(bank[7][rows, :], v_cmp[:, rows], PcT[:, :], start=True, stop=False)
                return
            m = s_nth(i, idx)
            pe.wait_ge(pT_dve, m + 1)
            pe.wait_ge(pT_act, m * 2 + 2)
            for kb in range(NB):
                col = KEYS_AT[kb]
                mm = nc.tensor.matmul(bank[7][rows, kb * P:], v_tok[r - 1][:, kb * P + 64 * g:kb * P + 64 * g + 64],
                                      PT[:, col:col + (NB - kb) * P], start=False, stop=r == 2 and kb == NB - 1)
            if r == 2 and g == 1:
                mm.then_inc(pair_done, 1)

        def attend_tensor(pe):
            pair_tensor(pe, 0, 0)
            scores_tensor(pe, 0, 0)
            scores_tensor(pe, 0, 1)

            def turn(i):
                for n in range(N_ITEMS):
                    turn_probs_tensor(pe, i, n)
                    if exists(i, n + 2):
                        scores_tensor(pe, i, n + 2)
                    weigh_tensor(pe, i, n)
                    if n == 1:
                        pair_tensor(pe, i, 1)
                    if n == 7 and exists(i, N_ITEMS):
                        pair_tensor(pe, i + 1, 0)

            with pe.Fori(0, TURNS - 1) as i:
                turn(i)
            turn(TURNS - 1)

        def alibi_scalar(act, i, idx):
            j, g, _ = item(idx)
            slope = param("slopes", i * 2 + (8 * g + idx // N_ITEMS * 2 + j))
            nc.scalar.activation(alibi_c[g][:, :], dist_cmp, ACT.Identity, scale=slope).then_inc(alibi_ready, 1)
            nc.scalar.activation(alibi[g][:, :], dist, ACT.Identity, scale=slope).then_inc(alibi_ready, 1)

        def exp_scalar(act, i, idx):
            if item(idx)[2] == 2 and exists(i, idx + 1):
                alibi_scalar(act, i, idx + 1)
            if item(idx)[2] == 0:
                act.wait_ge(c_shifted, c_nth(i, idx) + 1)
                nc.scalar.activation(Pc[:, :], Pc[:, :], ACT.Exp, scale=KEY_SCALE).then_inc(probs_done, 1)
                return
            P_ = Pr[s_parity(idx)]
            for n, pieces in enumerate(PIECES):
                if n < 2:
                    act.wait_ge(piece_read, s_nth(i, idx) * 2 + (n + 1))
                else:
                    act.wait_ge(scores_read, nth(i, idx) + 2)
                for b, col in pieces:
                    here = P_[:, col:col + (b + 1) * P]
                    ins = nc.scalar.activation(here, here, ACT.Exp, bias=stat(idx, 0)[:, b:b + 1], scale=-1.0,
                                               accum_out=stat(idx, 1)[:, b:b + 1])
            ins.then_inc(probs_done, 1)

        def evict_scalar(act, i, idx):
            if item(idx)[2] == 0:
                act.wait_ge(c_turned, c_nth(i, idx) + 1)
                nc.scalar.activation(PcT[:, :], bank[5][0:32, :], ACT.Identity).then_inc(cT_ready, 1)
                return
            for n, source_bank in ((0, bank[5]), (2, bank[1])):
                act.wait_ge(turned, s_nth(i, idx) * 3 + (n + 1))
                first, end = GROUPS[n]
                nc.scalar.activation(PT[:, first:end], source_bank[:, 0:end - first], ACT.Identity).then_inc(pT_act, 1)

        def y_scalar(act, i, j):
            wait_apart(act, pair_done, i * 2 + (j + 1))
            nc.scalar.activation(cols(MR, i * 2 + (8 + j)), bank[7][:, :], ACT.Identity).then_inc(y_high, 1)

        def attend_scalar(act):
            alibi_scalar(act, 0, 0)
            exp_scalar(act, 0, 0)
            exp_scalar(act, 0, 1)

            def turn(i):
                for n in range(N_ITEMS):
                    if n == 6:
                        y_scalar(act, i, 0)
                    evict_scalar(act, i, n)
                    if exists(i, n + 2):
                        exp_scalar(act, i, n + 2)
                y_scalar(act, i, 1)

            with act.Fori(0, TURNS - 1) as i:
                turn(i)
            turn(TURNS - 1)

        def q_vector(dve, i, j):
            dve.wait_ge(unit_done, i * 2 + (q_units + j + 1))
            nc.vector.tensor_tensor(qT[j][:, :], bank[0][:, :], R[:, :], ALU.mult).then_inc(tile_taken, 1)

        def read_vector(dve, i, idx):
            j, g, r = item(idx)
            V = nc.vector
            if r == 0:
                c = c_nth(i, idx)
                dve.wait_ge(alibi_ready, c * 2 + 2)
                dve.wait_ge(c_scored, c + 1)
                V.tensor_tensor(Pc[:, :], bank[2][:, 0:P], alibi_c[g][:, :], ALU.add).then_inc(scores_read, 1)
                dve.wait_ge(scores_read, nth(i, idx) + 2)
                by_block = Pc[:, :].rearrange("p (b n) -> p b n", b=NB)
                V.tensor_reduce(c_max[:, 0:4], by_block, AX.X, ALU.max).then_inc(c_maxed, 1)
                dve.wait_ge(c_maxed, c + 1)
                V.tensor_tensor(by_block, by_block, over_columns(c_max[:, 0:4], 32), ALU.subtract).then_inc(c_shifted, 1)
                return
            P_ = Pr[s_parity(idx)]
            for n, pieces in enumerate(PIECES):
                wait_apart(dve, scored, s_nth(i, idx) * 3 + (n + 1))
                for b, col in pieces:
                    at0 = col - GROUPS[n][0]
                    ins = V.tensor_tensor_reduce(P_[:, col:col + (b + 1) * P], bank[2 + n][:, at0:at0 + (b + 1) * P],
                                                 alibi[g][:, (3 - b) * P:], -KEY_SCALE, 3.0e38, ALU.add, ALU.min,
                                                 stat(idx, 0)[:, b:b + 1])
                ins.then_inc(piece_read if n < 2 else scores_read, 1)

        def evict_vector(dve, i, idx):
            if item(idx)[2]:
                m = s_nth(i, idx)
                dve.wait_ge(turned, m * 3 + 2)
                nc.vector.tensor_copy(PT[:, 512:1024], bank[6][:, :]).then_inc(pT_dve, 1)

        def scale_vector(dve, i, idx):
            j, g, r = item(idx)
            V = nc.vector
            n, turn_on = nth(i, idx), idx // N_ITEMS
            dve.wait_ge(probs_done, n + 1)
            by_block = Pc[:, :].rearrange("p (b n) -> p b n", b=NB)
            if r == 0:
                V.tensor_reduce(stat(idx, 1), by_block, AX.X, ALU.add).then_inc(c_summed, 1)
                dve.wait_ge(c_summed, c_nth(i, idx) + 1)
            V.reciprocal(stat(idx, 2), stat(idx, 1)).then_inc(inverse, 1)
            dve.wait_ge(inverse, n + 1)
            gate = gates[:, :].rearrange("p (b c) -> p b c", b=NB)[:, :, bass.ds(i * 2 + (2 * turn_on + 16 * r + 8 * g + j), 1)]
            w, inv = stat(idx, 3), stat(idx, 2)
            marks = 16 * turn_on + WEIGHTS[idx % N_ITEMS]
            V.tensor_tensor(w.unsqueeze(2), inv.unsqueeze(2), gate, ALU.mult).then_inc(weight_ready, 1)
            dve.wait_ge(weight_ready, i * 16 + (marks + 1))
            if r == 0:
                V.tensor_tensor(w, w, seen, ALU.mult).then_inc(weight_ready, 1)
                dve.wait_ge(weight_ready, i * 16 + (marks + 2))
                V.tensor_tensor(by_block, by_block, over_columns(w, 32), ALU.mult).then_inc(probs_scaled, 1)
                return
            P_ = Pr[s_parity(idx)]
            for b in (3, 2, 0, 1):
                here = P_[:, WHERE[b]:WHERE[b] + (b + 1) * P]
                ins = V.tensor_scalar(here, here, w[:, b:b + 1], None, ALU.mult)
            ins.then_inc(probs_scaled, 1)

        WEIGHTS = [idx + sum(1 for it in ITEMS[:idx] if not it[2]) for idx in range(N_ITEMS)]

        def y_vector(dve, i, j):
            dve.wait_ge(y_high, i * 2 + (j + 1))
            here = i * 2 + (8 + j)
            nc.vector.tensor_tensor(cols(ML, here), bank[7][:, :], cols(MR, here).bitcast(F32), ALU.subtract).then_inc(y_low, 1)

        def attend_vector(dve):
            nc.vector.sem_inc(scores_read, 1)
            nc.vector.sem_inc(y_low, 1)
            q_vector(dve, 0, 0)
            read_vector(dve, 0, 0)
            read_vector(dve, 0, 1)
            scale_vector(dve, 0, 0)

            def turn(i):
                for n in range(N_ITEMS):
                    if n == 6:
                        y_vector(dve, i, 0)
                    evict_vector(dve, i, n)
                    if exists(i, n + 1):
                        scale_vector(dve, i, n + 1)
                    if exists(i, n + 2):
                        read_vector(dve, i, n + 2)
                    if n == 1:
                        q_vector(dve, i, 1)
                    if n == 7 and exists(i, N_ITEMS):
                        q_vector(dve, i + 1, 0)
                y_vector(dve, i, 1)

            with dve.Fori(0, TURNS - 1) as i:
                turn(i)
            turn(TURNS - 1)

        final_ready = sem("final_ready")

        def final_vector(dve):
            dve.wait_ge(norm_ready, NORM["h6"] + 1)
            with dve.Fori(0, DT) as n:
                nc.vector.scalar_tensor_tensor(cols(Y, n), cols(hT, n), param("final", n), R[:, :], ALU.mult, ALU.mult).then_inc(final_ready, 1)

        block = ctx.enter_context(nc.Block())
        layers = [n for n, _, _ in SEGMENTS]

        @block.sync
        def _(sp):
            sp.dma_start(hT[:, :], t["xT"]).then_inc(x_loaded, 16)
            sp.dma_start(table[:, :], t["table"]).then_inc(tables_loaded, 16)
            sp.dma_start(params[:, :], t["params"]).then_inc(tables_loaded, 16)
            for name in layers:
                stream(sp, SEG[name], lambda unit, row, turn, slot, name=name:
                       load_unit(sp, SEG[name], unit, row + SEG[name].source0, slot))
            with sp.Fori(0, DT) as n:
                sp.wait_ge(final_ready, n + 1)
                sp.dma_start(out[:, bass.ds(n * SEQ, SEQ)], cols(Y, n)).then_inc(stored, 16)
            sp.wait_ge(stored, 16 * DT)

        @block.gpsimd
        def _(pool):
            for name in layers:
                seg = SEG[name]
                if name in SHARED:
                    for c in range(2):
                        if seg.handed:
                            pool.wait_ge(high_ahead, seg.ahead0 + c + 1)
                            low_unit(seg, (seg.unit0 + c) % 2)
                        else:
                            split_unit(pool, seg, seg.unit0 + c, (seg.unit0 + c) // 2, (seg.unit0 + c) % 2)
                    if name in JOINED:
                        join_gpsimd(pool, JOINED[name])
                    with pool.Fori(1, seg.units // 2) as i:
                        for c in range(2):
                            pool.wait_ge(high_ahead, i * 2 + (seg.ahead0 + c + (1 if seg.handed else -1)))
                            low_unit(seg, (seg.unit0 + c) % 2)
                else:
                    stream(pool, seg, lambda unit, row, turn, slot, seg=seg: split_unit(pool, seg, unit, turn, slot))

        @block.tensor
        def _(pe):
            heads_tensor(pe)
            mem_tensor(pe)
            gdn_tensor(pe)
            mem_attend_tensor(pe)
            tiles(pe, SEG["out1"], lambda k: M_R[:, k], lambda k: M_L[:, k], (m_stored, -8))
            total(pe, "mix")
            ffn_tensor(pe, 1, "h1")
            total(pe, "ffn")
            conv_tensor(pe)
            ffn_tensor(pe, 2, "h3")
            kv_tensor(pe)
            pe.wait_ge(gate_ready, 1)
            attend_tensor(pe)
            tiles(pe, SEG["out2"], lambda k: M_R[:, 8 + k], lambda k: M_L[:, 8 + k], (y_low, 1))
            ffn_tensor(pe, 3, "h5")
            total(pe, "h6")

        @block.scalar
        def _(act):
            order = Order(act, sca)
            start_scalar(act)
            mem_scalar(act)
            gates_scalar(act)
            gdn_scalar(act, order)
            mem_attend_scalar(act)
            act.wait_ge(m_stored, MEM_HEADS)
            act.dma_start(hT[:, :], t["xT"]).then_inc(x_again, 16)
            keep_scalar(act, SEG["out1"], "mix")
            join_scalar(act, "mix", "h1", "pre_ffn")
            ffn_scalar(act, 1)
            keep_scalar(act, SEG["down1"], "ffn")
            join_scalar(act, "ffn", "h2", "a_norm")
            conv_scalar(act)
            ffn_scalar(act, 2)
            act.wait_ge(mid_low, 2 * FT)
            act.dma_start(phi1[:, :], t["phi1"]).then_inc(phi_loaded, 16)
            act.dma_start(phi2[:, :], t["phi2"]).then_inc(phi2_loaded, 16)
            stream_scalar(act, SEG["down2"], "h4", "kv", "kv_norm")
            kv_scalar(act)
            attend_scalar(act)
            stream_scalar(act, SEG["out2"], "h5", "h5", "ffn2")
            ffn_scalar(act, 3)
            stream_scalar(act, SEG["down3"], "h6", None, None)

        @block.vector
        def _(dve):
            order = Order(dve, vec)
            start_vector(dve, order)
            gates_vector(dve, order)
            gdn_vector(dve, order)
            mem_attend_vector(dve)
            dve.wait_ge(m_stored, MEM_HEADS)
            keep_vector(dve, order, "mix")
            join_vector(dve, order, "mix", "post_mix", "h1", "pre_ffn")
            ffn_vector(dve, 1, "h1")
            keep_vector(dve, order, "ffn")
            join_vector(dve, order, "ffn", "post_ffn", "h2", "a_norm")
            conv_vector(dve, order)
            ffn_vector(dve, 2, "h3")
            stream_vector(dve, order, SEG["down2"], "h4", "kv", "kv_norm")
            kv_vector(dve, order)
            attend_vector(dve)
            stream_vector(dve, order, SEG["out2"], "h5", "h5", "ffn2")
            ffn_vector(dve, 3, "h5")
            stream_vector(dve, order, SEG["down3"], "h6", None, None)
            final_vector(dve)


def tile_units(weight, kt):
    k, n = weight.shape
    pieces = weight.reshape(k // P, P, n // P, P).transpose(2, 0, 1, 3).reshape(-1, kt, P, P)
    return pieces.transpose(0, 2, 1, 3).reshape(-1, P, kt * P)


def columns(vector):
    return vector.reshape(-1, P).T


def kernel(**inputs):
    import concourse.bacc as bacc
    from concourse.bass_utils import run_bass_kernel_spmd as run

    a = {k: np.asarray(v) for k, v in inputs.items()}
    f32 = np.float32

    gdn = a["gdn_w_in"][0]
    qkv, z, heads = gdn[:, :3072], gdn[:, 3072:4096], gdn[:, 4096:4112]
    q_mem_w = gdn[:, 4112:]
    ab = np.zeros((D, P), f32)
    ab[:, 0:8], ab[:, 32:40] = heads[:, 0:8], heads[:, 8:16]
    kv = a["w_mem_kv"][0]
    values = kv[:, 512:].reshape(4, 2, P, 512).transpose(0, 2, 1, 3).reshape(4, P, 1024)
    groups = np.concatenate([w for h in range(HEADS) for w in (
        qkv[:, 1024 + h * P:1024 + (h + 1) * P], qkv[:, 2048 + h * P:2048 + (h + 1) * P],
        qkv[:, h * P:(h + 1) * P], z[:, h * P:(h + 1) * P])] + [q_mem_w], axis=1)

    def pairs(w, n):
        k = w.shape[0]
        return w.reshape(k, 2, n, P).transpose(0, 2, 1, 3).reshape(k, 2 * n * P)

    gate_first = np.r_[D:2 * D, 0:D]
    ffn = [a["w_ffn_in"][0], a["ffn_w_in_2"][0], a["ffn_w_in_2"][1]]
    down = [a["w_ffn_out"][0], a["ffn_w_out_2"][0], a["ffn_w_out_2"][1]]
    w_in = a["b_w_in_2"][0]
    by_pair = w_in[:, :1024].reshape(D, 2, 8, 64).transpose(0, 2, 1, 3).reshape(D, 1024)
    gate_w = np.zeros((D, P), f32)
    gate_w[:, :48] = w_in[:, 1024:]
    w_kv = a["w_kv_2"].reshape(D, 6, P)[:, [0, 1, 2, 4, 3, 5]].reshape(D, 6 * P)
    w_o = a["b_w_out_2"][0].reshape(2, 8, 64, D).transpose(1, 0, 2, 3).reshape(D, D)
    w8 = np.concatenate([tile_units(ab, 8), tile_units(kv[:, :512], 8), values, tile_units(groups, 8),
                         tile_units(pairs(ffn[0], FT), 8), tile_units(pairs(a["a_pw1_w_2"][0][:, gate_first], DT), 8),
                         tile_units(a["a_pw2_w_2"][0], 8), tile_units(pairs(ffn[1], FT), 8),
                         tile_units(w_kv, 8), tile_units(gate_w, 8), tile_units(by_pair, 8), tile_units(w_o, 8),
                         tile_units(pairs(ffn[2], FT), 8)])
    w6 = tile_units(a["w_out"][0], 6)
    w11 = np.concatenate([tile_units(w, 11) for w in down])

    def head_rows(v):
        col = np.zeros((P, 1), f32)
        col[:8, 0] = v
        return col

    slopes = np.broadcast_to(-8.0 * 2.0 ** (-8.0 * (np.arange(16) + 1) / 16), (P, 16)).astype(f32)
    conv4 = a["gdn_conv"][0].reshape(CONV_K, 24, P).transpose(2, 1, 0).reshape(P, 24 * CONV_K)
    conv31 = a["a_dw_w_2"][0].reshape(TAPS, DT, P).transpose(2, 1, 0).reshape(P, DT * TAPS)
    both = lambda pos: np.concatenate([pos.T, pos.T], axis=0)
    parts = {
        "mem_norm": columns(a["mem_norm"]), "pre_mix": columns(a["norm_pre_mix"][0]),
        "post_mix": columns(a["norm_post_mix"][0]), "pre_ffn": columns(a["norm_pre_ffn"][0]),
        "post_ffn": columns(a["norm_post_ffn"][0]), "gdn_out": columns(a["gdn_out_norm"][0]),
        "conv4": conv4, "a_norm": columns(a["a_norm_2"][0]), "pw1_a": columns(a["a_pw1_b_2"][0, :D]),
        "pw1_b": columns(a["a_pw1_b_2"][0, D:]), "dw_b": columns(a["a_dw_b_2"][0]),
        "ln_g": columns(a["a_ln_g_2"][0]), "ln_b": columns(a["a_ln_b_2"][0]), "pw2_b": columns(a["a_pw2_b_2"][0]),
        "kv_norm": columns(a["kv_norm_2"]), "b_norm": columns(a["b_norm_2"][0]),
        "ffn1": columns(a["ffn_norm_2"][0]), "ffn2": columns(a["ffn_norm_2"][1]), "final": columns(a["final_norm_2"]),
        "a_log": head_rows(a["gdn_a_log"][0]), "dt_bias": head_rows(a["gdn_dt_bias"][0]), "slopes": slopes,
        "conv31": conv31, "pos_k": both(a["cmp_pos_k_2"]), "pos_v": both(a["cmp_pos_v_2"]),
    }
    params = np.concatenate([parts[n] for n in PARAMS], axis=1)

    def phi_first(w):
        one = w.reshape(L_CMP, 64, 64).transpose(1, 0, 2).reshape(64, L_CMP * 64)
        return np.concatenate([one, one], axis=0)

    phi1 = np.concatenate([phi_first(a["phi_k_w1_2"]), phi_first(a["phi_v_w1_2"])], axis=1)
    phi2 = np.zeros((P, 2 * P), f32)
    for i, w in enumerate((a["phi_k_w2_2"], a["phi_v_w2_2"])):
        for g in range(2):
            phi2[64 * g:64 * g + 64, i * P + 64 * g:i * P + 64 * g + 64] = w
    feature_rows = lambda x: x.T.reshape(DT, P, -1).transpose(1, 0, 2).reshape(P, -1)
    arrays = {"w8": w8, "w6": w6, "w11": w11, "xT": feature_rows(a["x"][0]), "memT": feature_rows(a["mem"][0]),
              "table": constant_tables(), "params": params, "phi1": phi1, "phi2": phi2}
    arrays = {k: np.ascontiguousarray(v) for k, v in arrays.items()}

    nc = bacc.Bacc("TRN2", target_bir_lowering=False, num_devices=1)
    t = {k: nc.dram_tensor(k, v.shape, F32, kind="ExternalInput").ap() for k, v in arrays.items()}
    out = nc.dram_tensor("out", (P, DT * SEQ), F32, kind="ExternalOutput").ap()
    program(nc, t, out)
    r = run(nc, [arrays], core_ids=[0])
    got = np.asarray(r.results[0]["out"]).reshape(P, DT, SEQ).transpose(2, 1, 0).reshape(1, SEQ, D)
    return got
```
